# Optimizing a Trainium2 kernel written in Bass

```python
import math
import jax
import jax.numpy as jnp
from jax import lax
import numpy as np
import jax, jax.numpy as jnp

D_MODEL = 1024
BATCH = 1
SEQ = 256
DEPTH = 2

CHUNK = 64
Q_BLOCK = 128
NORM_EPS = 1e-6
NEG_INF = -1e30

N_EVEN = (DEPTH + 1) // 2
N_ODD = DEPTH // 2

RWKV_HEAD_DIM = 64
RWKV_WIDTH = D_MODEL // 2
RWKV_HEADS = RWKV_WIDTH // RWKV_HEAD_DIM
DECAY_LORA = 64
ICLR_LORA = 64
GATE_LORA = 160
RWKV_GN_EPS = 1e-5 * RWKV_HEAD_DIM
RWKV_SPLITS = (RWKV_WIDTH, 2 * RWKV_WIDTH, 3 * RWKV_WIDTH,
               3 * RWKV_WIDTH + DECAY_LORA, 3 * RWKV_WIDTH + DECAY_LORA + ICLR_LORA)
RWKV_COLS = 3 * RWKV_WIDTH + DECAY_LORA + ICLR_LORA + GATE_LORA

S5_WIDTH = D_MODEL - RWKV_WIDTH
S5_GROUP = 16
S5_GROUPS = S5_WIDTH // S5_GROUP
S5_STATE = 64
S5_DT_MIN = 1e-3
S5_DT_MAX = 1e-1

IN_COLS = RWKV_COLS + S5_WIDTH
MIX_WIDTH = RWKV_WIDTH + S5_WIDTH

DIFF_HEAD_DIM = 64
DIFF_V_DIM = 2 * DIFF_HEAD_DIM
DIFF_HEADS = D_MODEL // DIFF_V_DIM
DIFF_WIDTH = DIFF_HEADS * DIFF_V_DIM

MEM_LEN = 256
MEM_HEADS = 4
MEM_HEAD_DIM = D_MODEL // MEM_HEADS

D_FF = 2816
N_EXPERTS = 8
TOP_K = 2
D_FF_EXPERT = 3584


F32 = jnp.float32

def rms_norm(x, gain):
    xf = x.astype(F32)
    y = xf * lax.rsqrt(jnp.mean(xf * xf, axis=-1, keepdims=True) + NORM_EPS)
    return (y * gain.astype(F32)).astype(x.dtype)

def token_shift(z):
    return jnp.pad(z, ((0, 0), (1, 0), (0, 0)))[:, :-1]

def alibi_slopes(n_heads):
    return 2.0 ** (-8.0 * jnp.arange(1, n_heads + 1, dtype=F32) / n_heads)

def rwkv7_recurrence(r, decay, k, v, kk, a):
    b, _, h, n = r.shape

    def step(state, inp):
        r_t, w_t, k_t, v_t, kk_t, a_t = inp
        s_kk = jnp.einsum('bhvk,bhk->bhv', state, kk_t)
        state = (state * w_t[:, :, None, :]
                 - s_kk[..., None] * (kk_t * a_t)[:, :, None, :]
                 + v_t[..., None] * k_t[:, :, None, :])
        return state, jnp.einsum('bhvk,bhk->bhv', state, r_t)

    xs = tuple(jnp.moveaxis(t, 1, 0) for t in (r, decay, k, v, kk, a))
    _, out = lax.scan(step, jnp.zeros((b, h, n, n), F32), xs)
    return jnp.moveaxis(out, 0, 1)

def rwkv7_time_mix(zr, mu, w0, w_up, a0, a_up, g_up, k_k, k_a, r_k, ln_w, ln_b):
    b, t, _ = zr.shape
    zr = zr.astype(F32)
    zr = zr + (token_shift(zr) - zr) * mu.astype(F32)
    r, k, v, wd, ad, gd = jnp.split(zr, RWKV_SPLITS, axis=-1)
    heads = lambda u: u.reshape(b, t, RWKV_HEADS, RWKV_HEAD_DIM)
    w_log = -jax.nn.softplus(-(w0.astype(F32) + jnp.tanh(wd) @ w_up.astype(F32))) - 0.5
    decay = jnp.exp(-jnp.exp(w_log))
    a = jax.nn.sigmoid(a0.astype(F32) + ad @ a_up.astype(F32))
    g = jax.nn.sigmoid(gd) @ g_up.astype(F32)
    kk = heads(k * k_k.astype(F32))
    kk = kk * lax.rsqrt(jnp.maximum(jnp.sum(kk * kk, axis=-1, keepdims=True), 1e-24))
    k = k * (1.0 + (a - 1.0) * k_a.astype(F32))
    r_h, k_h, v_h = heads(r), heads(k), heads(v)
    o = rwkv7_recurrence(r_h, heads(decay), k_h, v_h, kk, heads(a))
    mean = jnp.mean(o, axis=-1, keepdims=True)
    var = jnp.mean(jnp.square(o - mean), axis=-1, keepdims=True)
    o = ((o - mean) * lax.rsqrt(var + RWKV_GN_EPS)).reshape(b, t, RWKV_WIDTH)
    o = o * ln_w.astype(F32) + ln_b.astype(F32)
    bonus = jnp.sum(r_h * k_h * r_k.astype(F32), axis=-1, keepdims=True) * v_h
    return (o + bonus.reshape(b, t, RWKV_WIDTH)) * g

def s5_ssm(u, lam_re, lam_im, log_dt, b_re, b_im, c_re, c_im, d_skip, w_glu, b_glu):
    b, t, _ = u.shape
    ug = u.astype(F32).reshape(b, t, S5_GROUPS, S5_GROUP)
    lam = lax.complex(lam_re.astype(F32), lam_im.astype(F32))
    dt = jnp.exp(log_dt.astype(F32))[:, None]
    lam_bar = jnp.exp(lam * dt)
    b_bar = ((lam_bar - 1.0) / lam)[..., None] * lax.complex(b_re.astype(F32), b_im.astype(F32))
    bu = jnp.einsum('gpi,btgi->btgp', b_bar, ug.astype(jnp.complex64))

    def combine(left, right):
        a_l, x_l = left
        a_r, x_r = right
        return a_r * a_l, a_r * x_l + x_r

    _, states = lax.associative_scan(combine, (jnp.broadcast_to(lam_bar, bu.shape), bu), axis=1)
    c_mat = lax.complex(c_re.astype(F32), c_im.astype(F32))
    y = jnp.real(jnp.einsum('gip,btgp->btgi', c_mat, states))
    y = y + d_skip.astype(F32).reshape(S5_GROUPS, S5_GROUP) * ug
    y = jax.nn.gelu(y.reshape(b, t, S5_WIDTH))
    return y * jax.nn.sigmoid(y @ w_glu.astype(F32) + b_glu.astype(F32))

def diff_attention(h, w_qkv, q_gain, k_gain, lam_q1, lam_k1, lam_q2, lam_k2, sub_gain, w_o, lambda_init):
    b, t, _ = h.shape
    q, k, v = jnp.split(h @ w_qkv, 3, axis=-1)
    q = rms_norm(q.reshape(b, t, DIFF_HEADS, 2, DIFF_HEAD_DIM), q_gain).astype(F32)
    k = rms_norm(k.reshape(b, t, DIFF_HEADS, 2, DIFF_HEAD_DIM), k_gain).astype(F32)
    v = v.reshape(b, t, DIFF_HEADS, DIFF_V_DIM).astype(F32)
    lam = (jnp.exp(jnp.sum(lam_q1.astype(F32) * lam_k1.astype(F32)))
           - jnp.exp(jnp.sum(lam_q2.astype(F32) * lam_k2.astype(F32))) + lambda_init)
    slopes = alibi_slopes(DIFF_HEADS)
    key_pos = jnp.arange(t)
    n_blocks = t // Q_BLOCK
    q_blocks = jnp.moveaxis(q.reshape(b, n_blocks, Q_BLOCK, DIFF_HEADS, 2, DIFF_HEAD_DIM), 1, 0)
    starts = jnp.arange(n_blocks) * Q_BLOCK
    scale = DIFF_HEAD_DIM ** -0.5

    def attend_block(args):
        qb, start = args
        q_pos = start + jnp.arange(Q_BLOCK)
        s = jnp.einsum('bqhcd,bshcd->bhcqs', qb, k) * scale
        dist = jnp.abs(q_pos[:, None] - key_pos[None, :]).astype(F32)
        bias = -slopes[:, None, None, None] * dist
        visible = (key_pos[None, :] // CHUNK) <= (q_pos[:, None] // CHUNK)
        p = jax.nn.softmax(jnp.where(visible, s + bias, NEG_INF), axis=-1)
        attn = p[:, :, 0] - lam * p[:, :, 1]
        return jnp.einsum('bhqs,bshe->bqhe', attn, v)

    o = lax.map(attend_block, (q_blocks, starts))
    o = jnp.moveaxis(o, 0, 1).reshape(b, t, DIFF_HEADS, DIFF_V_DIM)
    o = rms_norm(o, sub_gain) * (1.0 - lambda_init)
    return o.reshape(b, t, DIFF_WIDTH).astype(h.dtype) @ w_o

def memory_cross_attention(h, mem_n, w_q, w_kv, q_gain, k_gain, w_o):
    b, t, _ = h.shape
    m = mem_n.shape[1]
    q = rms_norm((h @ w_q).reshape(b, t, MEM_HEADS, MEM_HEAD_DIM), q_gain).astype(F32)
    k, v = jnp.split(mem_n @ w_kv, 2, axis=-1)
    k = rms_norm(k.reshape(b, m, MEM_HEADS, MEM_HEAD_DIM), k_gain).astype(F32)
    v = v.reshape(b, m, MEM_HEADS, MEM_HEAD_DIM).astype(F32)
    p = jax.nn.softmax(jnp.einsum('bthd,bmhd->bhtm', q, k) * MEM_HEAD_DIM ** -0.5, axis=-1)
    o = jnp.einsum('bhtm,bmhd->bthd', p, v).reshape(b, t, D_MODEL)
    return o.astype(h.dtype) @ w_o

def swiglu(h, w_gate, w_up, w_down):
    return (jax.nn.silu(h @ w_gate) * (h @ w_up)) @ w_down

def moe_swiglu(h, w_router, b_router, w_gate, w_up, w_down):
    logits = (h @ w_router).astype(F32) + b_router.astype(F32)
    top_logits, top_idx = lax.top_k(logits, TOP_K)
    top_w = jax.nn.softmax(top_logits, axis=-1)
    gates = jnp.sum(jax.nn.one_hot(top_idx, N_EXPERTS, dtype=F32) * top_w[..., None], axis=-2)
    out = jnp.zeros(h.shape, F32)
    for e in range(N_EXPERTS):
        y_e = swiglu(h, w_gate[e], w_up[e], w_down[e]).astype(F32)
        out = out + gates[..., e:e + 1] * y_e
    return out.astype(h.dtype)

def first_inputs(seed: int = 0) -> dict:
    key = jax.random.key(seed)
    keys = iter(jax.random.split(key, 80))

    def nrm(shape, scale):
        return jax.random.normal(next(keys), shape, F32) * scale

    def gain(shape):
        return 1.0 + nrm(shape, 0.02)

    D, L, NE, NO = D_MODEL, DEPTH, N_EVEN, N_ODD
    G, P, I = S5_GROUPS, S5_STATE, S5_GROUP
    decay_ramp = -6.5 + 5.0 * jnp.linspace(0.0, 1.0, RWKV_WIDTH, dtype=F32) ** 0.85
    return {
        'x': nrm((BATCH, SEQ, D), 1.0),
        'mem': nrm((BATCH, MEM_LEN, D), 1.0),
        'norm_mix': gain((L, D)),
        'norm_xattn': gain((L, D)),
        'norm_mem': gain((L, D)),
        'norm_ffn': gain((L, D)),
        'xa_w_q': nrm((L, D, D), D ** -0.5),
        'xa_w_kv': nrm((L, D, 2 * D), D ** -0.5),
        'xa_q_gain': gain((L, MEM_HEAD_DIM)),
        'xa_k_gain': gain((L, MEM_HEAD_DIM)),
        'xa_w_o': nrm((L, D, D), D ** -0.5),
        'hy_w_in': nrm((NE, D, IN_COLS), D ** -0.5),
        'rw_mu': jax.random.uniform(next(keys), (NE, RWKV_COLS), F32),
        'rw_w0': decay_ramp + nrm((NE, RWKV_WIDTH), 0.01),
        'rw_w_up': nrm((NE, DECAY_LORA, RWKV_WIDTH), 0.1),
        'rw_a0': nrm((NE, RWKV_WIDTH), 0.1),
        'rw_a_up': nrm((NE, ICLR_LORA, RWKV_WIDTH), ICLR_LORA ** -0.5),
        'rw_g_up': nrm((NE, GATE_LORA, RWKV_WIDTH), GATE_LORA ** -0.5),
        'rw_k_k': 0.85 + nrm((NE, RWKV_WIDTH), 0.02),
        'rw_k_a': gain((NE, RWKV_WIDTH)),
        'rw_r_k': nrm((NE, RWKV_HEADS, RWKV_HEAD_DIM), 0.1),
        'rw_ln_w': gain((NE, RWKV_WIDTH)),
        'rw_ln_b': nrm((NE, RWKV_WIDTH), 0.02),
        's5_lam_re': -0.5 + nrm((NE, G, P), 0.01),
        's5_lam_im': jnp.pi * jnp.arange(P, dtype=F32) + nrm((NE, G, P), 0.01),
        's5_log_dt': jax.random.uniform(next(keys), (NE, G), F32, math.log(S5_DT_MIN), math.log(S5_DT_MAX)),
        's5_b_re': nrm((NE, G, P, I), (2 * I) ** -0.5),
        's5_b_im': nrm((NE, G, P, I), (2 * I) ** -0.5),
        's5_c_re': nrm((NE, G, I, P), P ** -0.5),
        's5_c_im': nrm((NE, G, I, P), P ** -0.5),
        's5_d': nrm((NE, S5_WIDTH), 1.0),
        's5_w_glu': nrm((NE, S5_WIDTH, S5_WIDTH), S5_WIDTH ** -0.5),
        's5_b_glu': nrm((NE, S5_WIDTH), 0.02),
        'hy_w_out': nrm((NE, MIX_WIDTH, D), MIX_WIDTH ** -0.5),
        'ff_w_gate': nrm((NE, D, D_FF), D ** -0.5),
        'ff_w_up': nrm((NE, D, D_FF), D ** -0.5),
        'ff_w_down': nrm((NE, D_FF, D), D_FF ** -0.5),
        'da_w_qkv': nrm((NO, D, 3 * DIFF_WIDTH), D ** -0.5),
        'da_q_gain': gain((NO, DIFF_HEAD_DIM)),
        'da_k_gain': gain((NO, DIFF_HEAD_DIM)),
        'da_lam_q1': nrm((NO, DIFF_HEAD_DIM), 0.1),
        'da_lam_k1': nrm((NO, DIFF_HEAD_DIM), 0.1),
        'da_lam_q2': nrm((NO, DIFF_HEAD_DIM), 0.1),
        'da_lam_k2': nrm((NO, DIFF_HEAD_DIM), 0.1),
        'da_sub_gain': gain((NO, DIFF_V_DIM)),
        'da_w_o': nrm((NO, DIFF_WIDTH, D), DIFF_WIDTH ** -0.5),
        'moe_w_router': nrm((NO, D, N_EXPERTS), D ** -0.5),
        'moe_b_router': nrm((NO, N_EXPERTS), 0.01),
        'moe_w_gate': nrm((NO, N_EXPERTS, D, D_FF_EXPERT), D ** -0.5),
        'moe_w_up': nrm((NO, N_EXPERTS, D, D_FF_EXPERT), D ** -0.5),
        'moe_w_down': nrm((NO, N_EXPERTS, D_FF_EXPERT, D), D_FF_EXPERT ** -0.5),
    }

def first_block(x, mem, norm_mix, norm_xattn, norm_mem, norm_ffn,
              xa_w_q, xa_w_kv, xa_q_gain, xa_k_gain, xa_w_o,
              hy_w_in, rw_mu, rw_w0, rw_w_up, rw_a0, rw_a_up, rw_g_up, rw_k_k, rw_k_a, rw_r_k,
              rw_ln_w, rw_ln_b,
              s5_lam_re, s5_lam_im, s5_log_dt, s5_b_re, s5_b_im, s5_c_re, s5_c_im, s5_d,
              s5_w_glu, s5_b_glu, hy_w_out,
              ff_w_gate, ff_w_up, ff_w_down,
              da_w_qkv, da_q_gain, da_k_gain, da_lam_q1, da_lam_k1, da_lam_q2, da_lam_k2,
              da_sub_gain, da_w_o,
              moe_w_router, moe_b_router, moe_w_gate, moe_w_up, moe_w_down):
    h = x
    for l in range(DEPTH):
        i = l // 2
        hn = rms_norm(h, norm_mix[l])
        if l % 2 == 0:
            z = hn @ hy_w_in[i]
            y_a = rwkv7_time_mix(z[..., :RWKV_COLS], rw_mu[i], rw_w0[i], rw_w_up[i], rw_a0[i],
                                 rw_a_up[i], rw_g_up[i], rw_k_k[i], rw_k_a[i], rw_r_k[i],
                                 rw_ln_w[i], rw_ln_b[i])
            y_b = s5_ssm(z[..., RWKV_COLS:], s5_lam_re[i], s5_lam_im[i], s5_log_dt[i], s5_b_re[i],
                         s5_b_im[i], s5_c_re[i], s5_c_im[i], s5_d[i], s5_w_glu[i], s5_b_glu[i])
            y_mix = jnp.concatenate([y_a, y_b], axis=-1).astype(h.dtype) @ hy_w_out[i]
        else:
            lambda_init = 0.8 - 0.6 * math.exp(-0.3 * l)
            y_mix = diff_attention(hn, da_w_qkv[i], da_q_gain[i], da_k_gain[i], da_lam_q1[i],
                                   da_lam_k1[i], da_lam_q2[i], da_lam_k2[i], da_sub_gain[i],
                                   da_w_o[i], lambda_init)
        h = h + y_mix.astype(h.dtype)
        y_mem = memory_cross_attention(rms_norm(h, norm_xattn[l]), rms_norm(mem, norm_mem[l]),
                                       xa_w_q[l], xa_w_kv[l], xa_q_gain[l], xa_k_gain[l], xa_w_o[l])
        h = h + y_mem.astype(h.dtype)
        hn = rms_norm(h, norm_ffn[l])
        if l % 2 == 0:
            y_ff = swiglu(hn, ff_w_gate[i], ff_w_up[i], ff_w_down[i])
        else:
            y_ff = moe_swiglu(hn, moe_w_router[i], moe_b_router[i], moe_w_gate[i],
                              moe_w_up[i], moe_w_down[i])
        h = h + y_ff.astype(h.dtype)
    return h


HEAD_DIM = 64
D_MIX = D_MODEL
N_Q_HEADS = 8
N_KV_HEADS = 2
GQA_GROUP = N_Q_HEADS // N_KV_HEADS
ATTN_W = N_Q_HEADS * HEAD_DIM
KV_W = N_KV_HEADS * HEAD_DIM
N_SG_HEADS = 4
SG_W = N_SG_HEADS * HEAD_DIM
SG_CHUNK = 128
N_CONV_GROUPS = 4
CONV_W = N_CONV_GROUPS * HEAD_DIM
CONV_K = 3
GRID_W = 64
ROPE_THETA = 10000.0
AXIS_DIM = HEAD_DIM // 2
EPS = 1e-6
PROJ_SPLITS = (ATTN_W, KV_W, KV_W, SG_W, SG_W, CONV_W, CONV_W, CONV_W)
PROJ_W = sum(PROJ_SPLITS)


def _rmsnorm(x, g):
    x32 = x.astype(jnp.float32)
    y = x32 * lax.rsqrt(jnp.mean(x32 * x32, axis=-1, keepdims=True) + EPS)
    return y.astype(x.dtype) * g

def _dwconv3(x, w):
    xp = jnp.pad(x, ((0, 0), (1, 1), (0, 0)))
    return xp[:, :-2] * w[0] + xp[:, 1:-1] * w[1] + xp[:, 2:] * w[2]

def _axial_angles(seq):
    rows = seq // GRID_W
    row = jnp.broadcast_to(jnp.arange(rows)[:, None], (rows, GRID_W)).reshape(-1)
    col = jnp.broadcast_to(jnp.arange(GRID_W)[None, :], (rows, GRID_W)).reshape(-1)
    inv = 1.0 / (ROPE_THETA ** (jnp.arange(AXIS_DIM // 2, dtype=jnp.float32) * 2.0 / AXIS_DIM))
    ang_r = row.astype(jnp.float32)[:, None] * inv[None, :]
    ang_c = col.astype(jnp.float32)[:, None] * inv[None, :]
    return ang_r, ang_c

def _rotate(x, cos, sin):
    x1, x2 = jnp.split(x, 2, axis=-1)
    return jnp.concatenate([x1 * cos - x2 * sin, x1 * sin + x2 * cos], axis=-1)

def _axial_rope(x, tabs):
    cr, sr, cc, sc = tabs
    return jnp.concatenate([_rotate(x[..., :AXIS_DIM], cr, sr),
                            _rotate(x[..., AXIS_DIM:], cc, sc)], axis=-1)

def _block_attention(q, k, v):
    b, s = q.shape[0], q.shape[1]
    nblk = s // Q_BLOCK
    scale = HEAD_DIM ** -0.5
    qb = q.reshape(b, nblk, Q_BLOCK, N_KV_HEADS, GQA_GROUP, HEAD_DIM).transpose(1, 0, 2, 3, 4, 5)

    def one_block(qblk):
        sc = jnp.einsum('bqgrd,bkgd->bgrqk', qblk, k).astype(jnp.float32) * scale
        p = jax.nn.softmax(sc, axis=-1).astype(v.dtype)
        return jnp.einsum('bgrqk,bkgd->bqgrd', p, v)

    out = lax.map(one_block, qb)
    return out.transpose(1, 0, 2, 3, 4, 5).reshape(b, s, ATTN_W)

def _spatial_gating(u, v, g_v, w_s, b_s):
    b, s = u.shape[0], u.shape[1]
    nchunk = s // SG_CHUNK
    vn = _rmsnorm(v, g_v).reshape(b, nchunk, SG_CHUNK, N_SG_HEADS, HEAD_DIM)
    mixed = jnp.einsum('hpq,bnqhc->bnphc', w_s, vn) + b_s.T[:, :, None]
    return u * mixed.reshape(b, s, SG_W)

def second_inputs(seed: int = 0) -> dict:
    key = jax.random.key(seed)
    ks = jax.random.split(key, 16)
    f32 = jnp.float32
    nrm = lambda k, shape, s: jax.random.normal(k, shape, f32) * s
    res_scale = (2.0 * DEPTH) ** -0.5
    return {
        "x": jax.random.normal(ks[0], (BATCH, SEQ, D_MODEL), f32),
        "norm1_g": 1.0 + nrm(ks[1], (DEPTH, D_MODEL), 0.02),
        "w_in": nrm(ks[2], (DEPTH, D_MODEL, PROJ_W), D_MODEL ** -0.5),
        "q_norm_g": 1.0 + nrm(ks[3], (DEPTH, HEAD_DIM), 0.02),
        "k_norm_g": 1.0 + nrm(ks[4], (DEPTH, HEAD_DIM), 0.02),
        "sg_norm_g": 1.0 + nrm(ks[5], (DEPTH, SG_W), 0.02),
        "sg_w": nrm(ks[6], (DEPTH, N_SG_HEADS, SG_CHUNK, SG_CHUNK), 0.5 * SG_CHUNK ** -0.5),
        "sg_b": 1.0 + nrm(ks[7], (DEPTH, N_SG_HEADS, SG_CHUNK), 0.1),
        "conv_w": nrm(ks[8], (DEPTH, CONV_K, CONV_W), CONV_K ** -0.5),
        "w_out": nrm(ks[9], (DEPTH, D_MIX, D_MODEL), D_MIX ** -0.5 * res_scale),
        "norm2_g": 1.0 + nrm(ks[10], (DEPTH, D_MODEL), 0.02),
        "ffn_w_up": nrm(ks[11], (DEPTH, D_MODEL, 2 * D_FF), D_MODEL ** -0.5),
        "ffn_conv_w": nrm(ks[12], (DEPTH, CONV_K, 2 * D_FF), CONV_K ** -0.5),
        "ffn_w_down": nrm(ks[13], (DEPTH, D_FF, D_MODEL), D_FF ** -0.5 * res_scale),
    }

def second_block(x, norm1_g, w_in, q_norm_g, k_norm_g, sg_norm_g, sg_w, sg_b, conv_w,
              w_out, norm2_g, ffn_w_up, ffn_conv_w, ffn_w_down):
    b, s, _ = x.shape
    ang_r, ang_c = _axial_angles(s)
    dt = x.dtype
    tabs = (jnp.cos(ang_r)[:, None, :].astype(dt), jnp.sin(ang_r)[:, None, :].astype(dt),
            jnp.cos(ang_c)[:, None, :].astype(dt), jnp.sin(ang_c)[:, None, :].astype(dt))
    split_at = np.cumsum(PROJ_SPLITS)[:-1].tolist()

    for l in range(DEPTH):
        h = _rmsnorm(x, norm1_g[l])
        p = h @ w_in[l]
        q, k, v, su, sv, cb, cc, cx = jnp.split(p, split_at, axis=-1)

        q = _rmsnorm(q.reshape(b, s, N_Q_HEADS, HEAD_DIM), q_norm_g[l])
        k = _rmsnorm(k.reshape(b, s, N_KV_HEADS, HEAD_DIM), k_norm_g[l])
        q = _axial_rope(q, tabs)
        k = _axial_rope(k, tabs)
        a_out = _block_attention(q, k, v.reshape(b, s, N_KV_HEADS, HEAD_DIM))

        g_out = _spatial_gating(su, sv, sg_norm_g[l], sg_w[l], sg_b[l])

        c_out = cb * _dwconv3(cc * cx, conv_w[l])

        mix = jnp.concatenate([a_out, g_out, c_out], axis=-1)
        x = x + mix @ w_out[l]

        h2 = _rmsnorm(x, norm2_g[l])
        up = _dwconv3(h2 @ ffn_w_up[l], ffn_conv_w[l])
        gate, val = jnp.split(up, 2, axis=-1)
        x = x + (jax.nn.silu(gate) * val) @ ffn_w_down[l]
    return x


def setup_inputs(seed=0):
    out = dict(first_inputs(seed))
    for name, value in second_inputs(seed + 1).items():
        if name != "x":
            out[name + "_2"] = value
    return out


def reference(
    x, mem, norm_mix, norm_xattn, norm_mem, norm_ffn, xa_w_q, xa_w_kv, xa_q_gain, xa_k_gain,
    xa_w_o, hy_w_in, rw_mu, rw_w0, rw_w_up, rw_a0, rw_a_up, rw_g_up, rw_k_k, rw_k_a, rw_r_k,
    rw_ln_w, rw_ln_b, s5_lam_re, s5_lam_im, s5_log_dt, s5_b_re, s5_b_im, s5_c_re, s5_c_im, s5_d,
    s5_w_glu, s5_b_glu, hy_w_out, ff_w_gate, ff_w_up, ff_w_down, da_w_qkv, da_q_gain, da_k_gain,
    da_lam_q1, da_lam_k1, da_lam_q2, da_lam_k2, da_sub_gain, da_w_o, moe_w_router, moe_b_router,
    moe_w_gate, moe_w_up, moe_w_down, norm1_g_2, w_in_2, q_norm_g_2, k_norm_g_2, sg_norm_g_2,
    sg_w_2, sg_b_2, conv_w_2, w_out_2, norm2_g_2, ffn_w_up_2, ffn_conv_w_2, ffn_w_down_2,
):
    x = first_block(
        x, mem, norm_mix, norm_xattn, norm_mem, norm_ffn, xa_w_q, xa_w_kv, xa_q_gain, xa_k_gain,
        xa_w_o, hy_w_in, rw_mu, rw_w0, rw_w_up, rw_a0, rw_a_up, rw_g_up, rw_k_k, rw_k_a, rw_r_k,
        rw_ln_w, rw_ln_b, s5_lam_re, s5_lam_im, s5_log_dt, s5_b_re, s5_b_im, s5_c_re, s5_c_im,
        s5_d, s5_w_glu, s5_b_glu, hy_w_out, ff_w_gate, ff_w_up, ff_w_down, da_w_qkv, da_q_gain,
        da_k_gain, da_lam_q1, da_lam_k1, da_lam_q2, da_lam_k2, da_sub_gain, da_w_o,
        moe_w_router, moe_b_router, moe_w_gate, moe_w_up, moe_w_down,
    )
    return second_block(
        x, norm1_g_2, w_in_2, q_norm_g_2, k_norm_g_2, sg_norm_g_2, sg_w_2, sg_b_2, conv_w_2,
        w_out_2, norm2_g_2, ffn_w_up_2, ffn_conv_w_2, ffn_w_down_2,
    )


_drawn_inputs = setup_inputs


def setup_inputs(seed=0):
    import zlib

    import numpy as np

    out = dict(_drawn_inputs(seed))
    spreads = {}
    factors = {'norm_xattn': 4.273,
     'norm_mem': 4.042,
     'xa_q_gain': 4.222,
     'xa_k_gain': 3.902,
     'rw_k_k': 8.0,
     's5_lam_re': 64.0,
     's5_b_glu': 2.932,
     'da_lam_q1': 4.105,
     'norm1_g_2': 5.443,
     'q_norm_g_2': 48.912,
     'k_norm_g_2': 44.296,
     'sg_norm_g_2': 64.0,
     'norm2_g_2': 21.605,
     'moe_b_router': 4.763,
     'sg_b_2': 8.0}
    for name, (base, spread) in spreads.items():
        noise = np.random.default_rng([zlib.crc32(name.encode()), seed]).standard_normal(out[name].shape)
        drawn = base * np.exp(spread * noise) if base else spread * noise
        out[name] = jnp.asarray(drawn.astype(out[name].dtype))
    for name, factor in factors.items():
        out[name] = (out[name] * factor).astype(out[name].dtype)
    return out
```

```python
import math
from contextlib import ExitStack

import numpy as np
import concourse.bass as bass
from concourse import mybir

F32 = mybir.dt.float32
ALU = mybir.AluOpType
ACT = mybir.ActivationFunctionType
AX = mybir.AxisListType.X

D, S, M, P = 1024, 256, 256, 128
KT = D // P
CH = 256
RW = 512
RT = RW // P
ZT = 15
C = 64
NJ = RT * (S // C)
SP_ = 16
FF, FFE, NE = 2816, 3584, 8
R1, R2 = 6, 5
LEVELS = (2, 4, 8, 16, 32)
LAMBDA_INIT = 0.8 - 0.6 * math.exp(-0.3)
BIG = 1e30



def tiles_of(v):
    v = v.reshape(-1, v.shape[-1] // P, P)
    return v.transpose(2, 0, 1).reshape(P, -1)


def twice(v):
    return np.concatenate([v, v]).reshape(P, 1)


def padded(v, rows):
    out = np.zeros((rows,) + v.shape[1:], v.dtype)
    out[:v.shape[0]] = v
    return out


def states(v):
    return v.reshape(SP_, P).T


def s5_b(b):
    out = np.zeros((4, 2, 16, 4, 2, 64), b.dtype)
    v = b.reshape(4, 4, 2, 64, 16)
    for g in range(2):
        out[:, g, :, :, g, :] = v[:, :, g].transpose(1, 3, 0, 2)
    return out.reshape(P, 4 * P)


def s5_c(c):
    out = np.zeros((2, 64, SP_, 2, 16), c.dtype)
    v = c.reshape(SP_, 2, 16, 64)
    for g in range(2):
        out[g, :, :, g, :] = v[:, g].transpose(2, 0, 1)
    return out.reshape(P, SP_ * 32)


def small_inputs(i):
    a = {
        "g_mix": tiles_of(i["norm_mix"]), "g_xattn": tiles_of(i["norm_xattn"]),
        "g_mem": tiles_of(i["norm_mem"]), "g_ffn": tiles_of(i["norm_ffn"]),
        "g_xq": tiles_of(i["xa_q_gain"]), "g_xk": tiles_of(i["xa_k_gain"]),
        "mu": tiles_of(padded(i["rw_mu"][0], ZT * P)),
        "w0": tiles_of(i["rw_w0"]), "a0": tiles_of(i["rw_a0"]), "k_k": tiles_of(i["rw_k_k"]),
        "k_a": tiles_of(i["rw_k_a"]), "r_k": tiles_of(i["rw_r_k"].reshape(RW)),
        "ln_w": tiles_of(i["rw_ln_w"]), "ln_b": tiles_of(i["rw_ln_b"]),
        "lora": np.concatenate([i["rw_w_up"][0], i["rw_a_up"][0]]),
        "g_up": i["rw_g_up"][0][:P], "g_up2": padded(i["rw_g_up"][0][P:], P),
        "lam_re": states(i["s5_lam_re"][0]), "lam_im": states(i["s5_lam_im"][0]),
        "log_dt": states(np.broadcast_to(i["s5_log_dt"][0][:, None], (32, 64))),
        "b_re": s5_b(i["s5_b_re"][0]), "b_im": s5_b(i["s5_b_im"][0]),
        "c_re": s5_c(i["s5_c_re"][0]), "c_im": s5_c(i["s5_c_im"][0]),
        "s5_d": tiles_of(i["s5_d"]), "b_glu": tiles_of(i["s5_b_glu"]),
        "g_dq": twice(i["da_q_gain"][0]), "g_dk": twice(i["da_k_gain"][0]),
        "g_sub": i["da_sub_gain"][0].reshape(P, 1),
        "lam": padded(np.stack([i["da_lam_q1"][0], i["da_lam_q2"][0],
                                i["da_lam_k1"][0], i["da_lam_k2"][0]], 1), P),
        "b_router": np.broadcast_to(i["moe_b_router"], (P, NE)),
        "w_router": i["moe_w_router"][0].reshape(KT, P, NE).transpose(1, 0, 2).reshape(P, KT * NE),
    }
    for l in range(2):
        a |= {
            f"g1_{l}": tiles_of(i["norm1_g_2"][l]), f"g2_{l}": tiles_of(i["norm2_g_2"][l]),
            f"gq_{l}": twice(i["q_norm_g_2"][l]), f"gk_{l}": twice(i["k_norm_g_2"][l]),
            f"gsg_{l}": tiles_of(i["sg_norm_g_2"][l]),
            f"sgb_{l}": np.broadcast_to(i["sg_b_2"][l].reshape(2, 2, 1, P), (2, 2, 64, P))
            .transpose(1, 2, 0, 3).reshape(P, 2 * P),
            f"sgw_{l}": i["sg_w_2"][l].transpose(2, 0, 1).reshape(P, 4 * P),
            f"cw_{l}": tiles_of(i["conv_w_2"][l]), f"fcw_{l}": tiles_of(i["ffn_conv_w_2"][l]),
        }
    return a


WIDTHS = {
    "g_mix": 16, "g_xattn": 16, "g_mem": 16, "g_ffn": 16, "g_xq": 4, "g_xk": 4, "mu": ZT,
    "w0": 4, "a0": 4, "k_k": 4, "k_a": 4, "r_k": 4, "ln_w": 4, "ln_b": 4,
    "lora": RW, "g_up": RW, "g_up2": RW, "lam_re": SP_, "lam_im": SP_, "log_dt": SP_,
    "b_re": 512, "b_im": 512, "c_re": 512, "c_im": 512, "s5_d": 4, "b_glu": 4,
    "g_dq": 1, "g_dk": 1, "g_sub": 1, "lam": 4, "b_router": NE, "w_router": KT * NE,
}
LAYER_WIDTHS = {"g1": 8, "g2": 8, "gq": 1, "gk": 1, "gsg": 2, "sgb": 256, "sgw": 512, "cw": 6,
                "fcw": 3 * 44}
LAYER_W = sum(LAYER_WIDTHS.values())


def offsets(widths):
    at, out = 0, {}
    for name, w in widths.items():
        out[name] = (at, w)
        at += w
    return out, at


SMALL_AT, LAYERS_AT = offsets(WIDTHS)
LAYER_AT, _ = offsets(LAYER_WIDTHS)
SMALL_W = LAYERS_AT + 2 * LAYER_W


def shape_constants():
    f = np.float32
    p = np.arange(P)
    s, t = (p % C)[:, None], np.arange(C)[None, :]
    pos = np.arange(S)
    inv = (f(1) / f(10000.0) ** (np.arange(16, dtype=f) * f(2) / f(32))).astype(f)
    row = (pos // 64).astype(f)[:, None] * inv
    col = (pos % 64).astype(f)[:, None] * inv
    ang = np.concatenate([row, row, col, col], 1).T.astype(f)
    ang = np.concatenate([ang, ang])
    turn = np.zeros((P, P), f)
    for d in range(P):
        turn[(d + 16, d) if d % 32 < 16 else (d - 16, d)] = -1 if d % 32 < 16 else 1
    dup = [(p[:, None] == 64 * g + p[None, :] % 64).astype(f) for g in range(2)]
    q = np.arange(S).reshape(2, P).T[:, :, None]
    k = np.arange(S)[None, None, :]

    def level(m):
        return (s // (2 * m) == t // (2 * m)) & (s // m % 2 == 0) & (t // m % 2 == 1)

    return {
        "ident": np.eye(P), "ones": np.ones((P, P)), "zeros": np.zeros((P, P)),
        "heads": p[:, None] // 64 == p[None, :] // 64,
        "eye64": s == t, "levels": np.concatenate([level(m) for m in LEVELS], 1),
        "level1": level(1), "level1_low": (s // 2 == t // 2) & (s > t),
        "before": s < t, "upto": s <= t,
        "reset": np.broadcast_to(np.arange(S) % C != 0, (P, S)),
        "cos": np.cos(ang), "sin": np.sin(ang), "turn": turn,
        "dup": np.concatenate(dup, 1), "dupturn": np.concatenate([x @ turn for x in dup], 1),
        "dist": np.abs(q - k).reshape(P, 2 * S),
        "hidden": np.where(k // 64 <= q // 64, 0.0, -BIG).reshape(P, 2 * S),
        "rev": np.broadcast_to(NE - np.arange(NE), (P, NE)),
        "eps": np.full((P, 1), 1e-6), "gn_eps": np.full((P, 1), 1e-5 * 64),
    }


CONST_AT, CONST_W = offsets({n: v.shape[1] for n, v in shape_constants().items()})

FF_STEPS, MOE_STEPS = FF // CH, NE * FFE // CH


class Place:

    def __init__(self):
        self.n = {"meet": 0, "chunk": 0, "evac": 0, "act": 0, "silu": 0, "conv": 0}
        self.loops = []
        self.labels = []

    def enter(self, turn, per):
        self.loops.append((turn, per, dict(self.n)))

    def leave(self, turns):
        _, per, start = self.loops.pop()
        for k, n in self.n.items():
            assert n == start[k] + per.get(k, 0), (k, n - start[k], per)
            self.n[k] = start[k] + turns * per.get(k, 0)

    def value(self, k, offset=0, scale=1):
        v = (self.n[k] + offset) * scale
        for turn, per, _ in self.loops:
            if per.get(k):
                v = turn * (per[k] * scale) + v
        return v

    def add(self, k, by=1):
        self.n[k] += by

    def step(self, what):
        self.labels.append(what)
        self.add("meet")
        return self.value("meet", scale=3)


def build(nc, small, const, x_t, mem_t, w, out_t):
    ctx = ExitStack()
    with ctx:
        def sb(name, shape):
            return ctx.enter_context(nc.sbuf_tensor(name, shape, F32))

        def sem(name):
            return ctx.enter_context(nc.semaphore(name))

        ring = sb("ring", [P, R1, KT * 288])
        small_sb = sb("small_sb", [P, SMALL_W])
        const_sb = sb("const_sb", [P, CONST_W])
        layer_sb = sb("layer_sb", [P, LAYER_W])
        h = sb("h", [P, KT, S])
        hn = sb("hn", [P, KT, S])
        scr = sb("scr", [P, KT, S])
        mix = sb("mix", [P, KT, S])
        rstd = sb("rstd", [P, 2048])
        tiny = sb("tiny", [P, 272])
        arena = sb("arena", [P, 18, 1024])
        ps = ctx.enter_context(nc.psum_tensor("ps", [P, 8, 512], F32))

        def sm(name, a=0, b=None):
            at, width = SMALL_AT[name]
            return small_sb[:, at + a:at + (width if b is None else b)]

        def lay(name, a=0, b=None):
            at, width = LAYER_AT[name]
            return layer_sb[:, at + a:at + (width if b is None else b)]

        def cst(name, a=0, b=None):
            at, width = CONST_AT[name]
            return const_sb[:, at + a:at + (width if b is None else b)]

        def slot(i, n=1):
            return arena[:, i:i + n, :].rearrange("p a b -> p (a b)")

        def tiles(ap, n=S):
            return ap.rearrange("p (t n) -> p t n", n=n)

        def flat(t):
            return t[:, :, :].rearrange("p a b -> p (a b)")

        def banks(b, n=1):
            return ps[:, b:b + n, :].rearrange("p a b -> p (a b)")

        def scalars(ap, shape):
            return ap.unsqueeze(2).to_broadcast(shape)

        def repeated(ap, shape):
            return ap.unsqueeze(1).to_broadcast(shape)

        mem_sb, memn = tiles(slot(0, 2)), tiles(slot(2, 2))
        aq, ak = tiles(slot(4, 2)), tiles(slot(6, 2))
        av = slot(8, 2).rearrange("p (b n) -> p b n", b=2)
        ae = tiles(slot(10, 2))
        apt = slot(12, 2).rearrange("p (k u n) -> p k u n", k=2, n=P)
        apt4 = slot(12).rearrange("p (k u n) -> p k u n", k=2, n=P)
        bias = tiles(slot(14, 2))

        def act_buf(f):
            return tiles(slot(4)[:, (f % 2) * 512:(f % 2) * 512 + 512])

        def silu_buf(f):
            return tiles(slot(5)[:, (f % 2) * 512:(f % 2) * 512 + 512])

        def gate_conv(f):
            return tiles(slot(6)[:, (f % 2) * 512:(f % 2) * 512 + 512])

        def up_conv(f):
            return tiles(slot(7)[:, (f % 2) * 512:(f % 2) * 512 + 512])

        gate_rep = slot(6, 2).rearrange("p (b e n) -> p b e n", b=2, n=P)
        gate_bc = tiles(slot(8, 2))

        def by64(ap):
            return ap.rearrange("p (j n) -> p j n", n=C)

        z12, zg = tiles(slot(0, 3)), tiles(slot(3)[:, 0:3 * S])
        shift_tmp = tiles(slot(4, 3))
        R_, K_, V_, G_, A_, LW_, CL_, KK_ = (slot(i) for i in range(8))
        ar = slot(8, 2).rearrange("p (j n) -> p j n", n=2 * C)
        BE_, KA_, T_, TT_, LT_, MT_, NT_, WT_ = (slot(i) for i in range(10, 18))
        beta, kappa, tri, tri_t = by64(BE_), by64(KA_), by64(T_), by64(TT_)
        neg_lt, m_t, neg_nt, w_t = by64(LT_), by64(MT_), by64(NT_), by64(WT_)
        alpha_tok, beta_tok = by64(flat(hn)[:, 0:1024]), by64(flat(hn)[:, 1024:2048])
        kappa_tok, v_tok = by64(flat(scr)[:, 0:1024]), by64(flat(scr)[:, 1024:2048])
        xbuf, uv, tat, ubuf = by64(A_), by64(LW_), by64(CL_), by64(KK_)
        o_t = mix[:, 0:RT, :]
        work = rstd[:, 0:1024]
        state = by64(rstd[:, 1024:1024 + RT * C])
        chunk_decay = tiny[:, 48:64]

        u_t = mix[:, RT:2 * RT, :]
        e_re, e_im = tiles(slot(0, 4)), tiles(slot(4, 4))
        s5b = [tiles(slot(8 + i)) for i in range(8)]
        c_re, c_im = tiles(slot(16)[:, 0:512], 32), tiles(slot(16)[:, 512:1024], 32)

        def s5t(i):
            return tiny[:, 64 + 16 * i:80 + 16 * i]

        qk = tiles(slot(0, 2))
        q_r = tiles(slot(2, 2))
        v_tok2 = tiles(slot(8)[:, 0:256], P)
        sv_tok = tiles(slot(4)[:, 0:512])
        sv_sq = tiles(slot(4)[:, 512:1024])
        su, cb = tiles(slot(5)[:, 0:512]), tiles(slot(5)[:, 512:1024])
        cc, cx = tiles(slot(6)[:, 0:512]), tiles(slot(6)[:, 512:1024])
        c_out = tiles(slot(7)[:, 0:512])
        rot = tiles(slot(14, 2))

        loaded = sem("loaded")
        mem_loaded = sem("mem_loaded")
        arrived1 = [sem(f"arrived1_{i}") for i in range(R1)]
        arrived2 = [sem(f"arrived2_{i}") for i in range(R2)]
        chunk_used = sem("chunk_used")
        evacuated = sem("evacuated")
        met = sem("met")
        passed = sem("passed")
        silu_done = sem("silu_done")
        conv_done = sem("conv_done")
        act_ready = sem("act_ready")
        result_ready = sem("result_ready")
        stored = sem("stored")


        def pass_loop(eng, at):
            if at.loops:
                eng.sem_inc(passed, 1)

        SECOND = 14 + 16 + 3 * FF_STEPS + 16 + 16 + 3 * MOE_STEPS

        def chunk_place(at):
            n = at.n["chunk"]
            size, sems, m = (R1, arrived1, n) if n < SECOND else (R2, arrived2, n - SECOND)
            value = 16 * (m // size + 1)
            for turn, per, _ in at.loops:
                assert per.get("chunk", 0) % size == 0
                if per.get("chunk"):
                    value = turn * (16 * per["chunk"] // size) + value
            return m % size, sems[m % size], value

        def stream(sp, at, src, width=CH, rows=KT):
            n = at.n["chunk"]
            s_, arr, _ = chunk_place(at)
            if n < SECOND:
                need = n - R1 + 1
            elif n < SECOND + R2:
                need = max(g for g in range(SECOND - R1, SECOND) if g % R1 == n - SECOND) + 1
            else:
                need = n - R2 + 1
            if need > 0:
                sp.wait_ge(chunk_used, at.value("chunk", need - n))
            dst = ring[:, s_, 0:rows * width].rearrange("p (k n) -> p k n", n=width)
            sp.dma_start(dst, src.rearrange("(k p) n -> p k n", p=P)).then_inc(arr, 16)
            at.add("chunk")

        def stream_columns(sp, at, src, first, last):
            for c in range(first, last, CH):
                stream(sp, at, src[:, c:c + CH])

        def stream_memory(sp, at, l):
            stream_columns(sp, at, w["xa_w_q"][l], 0, D)
            stream_columns(sp, at, w["xa_w_kv"][l], 0, 2 * D)
            stream_columns(sp, at, w["xa_w_o"][l], 0, D)

        def stream_ff(sp, at, gate, up, down):
            for f in range(FF_STEPS):
                stream(sp, at, gate[:, f * CH:(f + 1) * CH])
                stream(sp, at, up[:, f * CH:(f + 1) * CH])
                if f:
                    stream(sp, at, down[(f - 1) * CH:f * CH, :], D, 2)
            stream(sp, at, down[(FF_STEPS - 1) * CH:FF_STEPS * CH, :], D, 2)

        EXPERT_PAIRS = FFE // CH // 2

        def expert_loops(eng, at, per_pair, body):
            for e0, e1, j0 in ((0, 1, 1), (1, NE, 0)):
                n = EXPERT_PAIRS - j0
                with eng.Fori(e0, e1) as e:
                    turn = e - e0 if e0 else e
                    at.enter(turn, {k: n * v for k, v in per_pair.items()})
                    with eng.Fori(j0, EXPERT_PAIRS) as j:
                        at.enter(j - j0 if j0 else j, per_pair)
                        body(e, j)
                        at.leave(n)
                    at.leave(e1 - e0)

        def stream_moe(sp, at):
            gate, up = w["moe_w_gate"][0], w["moe_w_up"][0]
            down = w["moe_w_down"][0].rearrange("e f d -> (e f) d")

            def gate_up(e, f):
                for m in (gate, up):
                    src = m[bass.ds(e, 1), :, bass.ds(f * CH, CH)]
                    stream(sp, at, src.rearrange("e k n -> (e k) n"))

            def down_rows(row):
                stream(sp, at, down[bass.ds(row, CH), :], D, 2)

            def pair(e, j):
                gate_up(e, j * 2)
                down_rows(e * FFE + j * (2 * CH) + -CH)
                gate_up(e, j * 2 + 1)
                down_rows(e * FFE + j * (2 * CH))

            gate_up(0, 0)
            gate_up(0, 1)
            down_rows(0)
            expert_loops(sp, at, {"chunk": 6}, pair)
            down_rows(NE * FFE - CH)

        def sync_program(sp):
            at = Place()
            sp.dma_start(const_sb[:, :], const).then_inc(loaded, 16)
            sp.dma_start(small_sb[:, :], small).then_inc(loaded, 16)
            sp.dma_start(h[:, :, :], x_t.rearrange("(k p) n -> p k n", p=P)).then_inc(loaded, 16)
            hy = w["hy_w_in"][0]
            stream_columns(sp, at, hy, 0, 3 * RW)
            stream(sp, at, hy[:, 3 * RW:3 * RW + 288], 288)
            stream_columns(sp, at, hy, 3 * RW + 288, 4 * RW + 288)
            stream(sp, at, w["s5_w_glu"][0], RW, 4)
            stream_columns(sp, at, w["hy_w_out"][0], 0, D)
            stream_memory(sp, at, 0)
            stream_ff(sp, at, w["ff_w_gate"][0], w["ff_w_up"][0], w["ff_w_down"][0])
            stream_columns(sp, at, w["da_w_qkv"][0], 0, 3 * D)
            stream_columns(sp, at, w["da_w_o"][0], 0, D)
            stream_memory(sp, at, 1)
            stream_moe(sp, at)
            assert at.n["chunk"] == SECOND, (at.n["chunk"], SECOND)
            for l in range(2):
                stream_columns(sp, at, w["w_in_2"][l], 0, 2 * D)
                stream_columns(sp, at, w["w_out_2"][l], 0, D)
                up = w["ffn_w_up_2"][l]
                stream_ff(sp, at, up[:, 0:FF], up[:, FF:2 * FF], w["ffn_w_down_2"][l])
            sp.wait_ge(result_ready, 1)
            sp.dma_start(out_t.rearrange("(k p) n -> p k n", p=P), h[:, :, :]).then_inc(stored, 16)
            sp.wait_ge(stored, 16)

        mm = nc.tensor.matmul

        def next_chunk(pe, at, k_tiles=KT, width=CH):
            s_, arr, value = chunk_place(at)
            pe.wait_ge(arr, value)
            return ring[:, s_, 0:k_tiles * width].rearrange("p (k n) -> p k n", n=width)

        def used(last, at):
            last.then_inc(chunk_used, 1)
            at.add("chunk")

        def pe_project(pe, at, src, n, form="feature", width=CH):
            for c in range(n):
                wt = next_chunk(pe, at, width=width)
                if c >= 4:
                    pe.wait_ge(evacuated, at.value("evac", -3))
                parts = []
                feature_tiles = {"token": 0, "both": 1, "feature": -(-width // P)}[form]
                for t in range(feature_tiles):
                    cols = slice(t * P, min(width, t * P + P))
                    parts.append((ps[0:cols.stop - cols.start, c % 4 + t // 2, (t % 2) * S:(t % 2) * S + S],
                                  [(wt[:, k, cols], src[:, k, :]) for k in range(KT)]))
                if form != "feature":
                    first = feature_tiles * P
                    n_ = width - first
                    for b in range(2):
                        at_ = feature_tiles * S + b * n_
                        parts.append((ps[:, c % 4, at_:at_ + n_],
                                      [(src[:, k, b * P:(b + 1) * P], wt[:, k, first:width]) for k in range(KT)]))
                for o, pairs in parts:
                    for k, (lhs, rhs) in enumerate(pairs):
                        last = mm(o, lhs, rhs, start=k == 0, stop=k == KT - 1)
                used(last, at)
                at.add("evac")
            pe.drain().then_inc(met, 1)
            pe.wait_ge(met, at.step("projection copied out"))
            pass_loop(pe, at)

        def pe_norm(pe, at, sq=scr, table="ones", groups=1, per=KT):
            pe.drain().then_inc(met, 1)
            pe.wait_ge(met, at.step("squares"))
            pass_loop(pe, at)
            for g in range(groups):
                for k in range(per):
                    mm(banks(4, 4)[:, g * S:(g + 1) * S], cst(table), sq[:, g * per + k, :],
                       start=k == 0, stop=k == per - 1)
            pe.drain().then_inc(met, 1)
            pe.wait_ge(met, at.step("sums of squares"))
            pass_loop(pe, at)
            pe.drain().then_inc(met, 1)
            pe.wait_ge(met, at.step("roots"))
            pass_loop(pe, at)
            pe.drain().then_inc(met, 1)
            pe.wait_ge(met, at.step("normed"))
            pass_loop(pe, at)

        def counted_loop(eng, at, turns, per, body):
            if turns == 1:
                body()
                return
            with eng.Fori(0, turns) as i:
                at.enter(i, per)
                body()
                at.leave(turns)

        def pe_ff(pe, at, ahead, turns, unroll):
            for b in range(4):
                mm(ps[:, 4 + b, :], cst("zeros"), hn[:, 0:2, :], start=True, stop=False)

            def gate_up(f):
                for half in range(2):
                    wt = next_chunk(pe, at)
                    for t in range(2):
                        for k in range(KT):
                            last = mm(ps[:, 2 * (f % 2) + half, t * S:(t + 1) * S], wt[:, k, t * P:(t + 1) * P],
                                      hn[:, k, :], start=k == 0, stop=k == KT - 1)
                    used(last, at)

            def down(f):
                wt = next_chunk(pe, at, 2, D)
                pe.wait_ge(act_ready, at.value("act", 1))
                at.add("act")
                for k in range(2):
                    for o in range(KT):
                        last = mm(banks(4, 4)[:, o * S:(o + 1) * S], wt[:, k, o * P:(o + 1) * P],
                                  act_buf(f)[:, k, :], start=False, stop=False)
                used(last, at)

            gate_up(0)
            for f in range(1, ahead):
                gate_up(f)
                down(f - 1)

            def body():
                for f in range(ahead, ahead + unroll):
                    gate_up(f)
                    down(f - 1)

            counted_loop(pe, at, turns, {"chunk": 3 * unroll, "act": unroll}, body)
            down(ahead + unroll - 1)
            for b in range(4):
                mm(ps[:, 4 + b, :], cst("zeros"), hn[:, 0:2, :], start=False, stop=True)
            pe.drain().then_inc(met, 1)
            pe.wait_ge(met, at.step("down products"))
            pass_loop(pe, at)
            pe.drain().then_inc(met, 1)
            pe.wait_ge(met, at.step("residual"))
            pass_loop(pe, at)

        def pe_softmax(pe, at, units, unit=lambda u: u):
            pe.drain().then_inc(met, 1)
            pe.wait_ge(met, at.step("scores"))
            pass_loop(pe, at)
            pe.drain().then_inc(met, 1)
            pe.wait_ge(met, at.step("scores less their maxima"))
            pass_loop(pe, at)
            pe.drain().then_inc(met, 1)
            pe.wait_ge(met, at.step("exponentials"))
            pass_loop(pe, at)
            pe.drain().then_inc(met, 1)
            pe.wait_ge(met, at.step("probabilities"))
            pass_loop(pe, at)
            for kb in range(2):
                for u in range(units):
                    i = kb * units + u
                    nc.tensor.transpose(banks(4, 4)[:, i * P:(i + 1) * P], ae[:, unit(u), kb * P:(kb + 1) * P],
                                        cst("ident"))
            pe.drain().then_inc(met, 1)
            pe.wait_ge(met, at.step("transposes"))
            pass_loop(pe, at)
            pe.drain().then_inc(met, 1)
            pe.wait_ge(met, at.step("transposes copied out"))
            pass_loop(pe, at)

        def pe_memory(pe, at):
            pe_norm(pe, at)
            pe_project(pe, at, hn, 4)
            pe_norm(pe, at, groups=4, per=2)
            pe_norm(pe, at)
            pe_project(pe, at, memn, 4)
            pe_project(pe, at, memn, 4, "token")
            pe_norm(pe, at, groups=4, per=2)
            for hd in range(4):
                for qb in range(2):
                    for k in range(2):
                        mm(banks(0, 4)[:, (2 * hd + qb) * M:(2 * hd + qb + 1) * M],
                           aq[:, 2 * hd + k, qb * P:(qb + 1) * P], ak[:, 2 * hd + k, :], start=k == 0, stop=k == 1)
            pe_softmax(pe, at, 8)
            for hd in range(4):
                for j in range(2):
                    for kb in range(2):
                        mm(banks(0, 4)[:, (2 * hd + j) * S:(2 * hd + j + 1) * S],
                           av[:, kb, (2 * hd + j) * P:(2 * hd + j + 1) * P],
                           apt[:, kb, 2 * hd:2 * hd + 2, :].rearrange("p u n -> p (u n)"),
                           start=kb == 0, stop=kb == 1)
            pe.drain().then_inc(met, 1)
            pe.wait_ge(met, at.step("products with v"))
            pe.drain().then_inc(met, 1)
            pe.wait_ge(met, at.step("attention output"))
            pe_project(pe, at, mix, 4)

        HALF = (slice(0, 64), slice(64, 128))

        def problems(n=NJ):
            for j in range(n):
                yield j, HALF[0]
                yield (j + n // 2) % n, HALF[1]

        def pbank(b):
            return by64(banks(b, 2))

        def pe_rwkv(pe, at):
            pe.drain().then_inc(met, 1)
            pe.wait_ge(met, at.step("inputs shifted"))
            pe.drain().then_inc(met, 1)
            pe.wait_ge(met, at.step("lora inputs, squares of kk"))
            for t in range(RT):
                cs, ts = slice(t * P, (t + 1) * P), slice(t * S, (t + 1) * S)
                mm(banks(0, 2)[:, ts], sm("lora")[0:64, cs], zg[0:64, 0, :], start=True, stop=True)
                mm(banks(2, 2)[:, ts], sm("lora")[64:128, cs], zg[64:128, 0, :], start=True, stop=True)
            for t in range(RT):
                cs, ts = slice(t * P, (t + 1) * P), slice(t * S, (t + 1) * S)
                mm(banks(4, 2)[:, ts], sm("g_up")[:, cs], zg[:, 1, :], start=True, stop=False)
                mm(banks(4, 2)[:, ts], sm("g_up2")[0:32, cs], zg[0:32, 2, :], start=False, stop=True)
                mm(banks(6, 2)[:, ts], cst("heads"), work[:, ts], start=True, stop=True)
            pe.drain().then_inc(met, 1)
            pe.wait_ge(met, at.step("lora products, sums for kk"))
            pe.drain().then_inc(met, 1)
            pe.wait_ge(met, at.step("sigmoids"))
            pe.drain().then_inc(met, 1)
            pe.wait_ge(met, at.step("cumulated decays, root for kk"))
            pe.drain().then_inc(met, 1)
            pe.wait_ge(met, at.step("exponentials, kk"))
            pe.drain().then_inc(met, 1)
            pe.wait_ge(met, at.step("alpha, beta, kappa, rho"))
            for j, hs in problems():
                mm(banks(0, 4)[hs, j * P:(j + 1) * P], beta[hs, j, :], ar[hs, j, :], start=True, stop=True)
            for j, hs in problems():
                mm(banks(4, 4)[hs, j * P:(j + 1) * P], kappa[hs, j, :], ar[hs, j, :], start=True, stop=True)
            pe.drain().then_inc(met, 1)
            pe.wait_ge(met, at.step("beta and kappa by alpha and rho"))
            pe.drain().then_inc(met, 1)
            pe.wait_ge(met, at.step("masked"))
            for j, hs in problems():
                mm(pbank(0)[hs, j, :], ar[hs, j, 0:C], beta[hs, j, :], start=True, stop=True)
            for b, src in ((2, ar), (4, beta), (6, kappa)):
                for j, hs in problems():
                    mm(pbank(b)[hs, j, :], src[hs, j, 0:C], cst("eye64")[hs, :], start=True, stop=True)
            pe.drain().then_inc(met, 1)
            pe.wait_ge(met, at.step("alpha by beta, token-major forms"))
            pe.drain().then_inc(met, 1)
            pe.wait_ge(met, at.step("inverse of blocks of two"))
            for j, hs in problems():
                mm(pbank(0)[hs, j, :], by64(V_)[hs, j, :], cst("eye64")[hs, :], start=True, stop=True)
            pe.drain().then_inc(met, 1)
            pe.wait_ge(met, at.step("v token-major"))

            def level():
                pe.drain().then_inc(met, 1)
                pe.wait_ge(met, at.step("blocks below the diagonal"))
                pass_loop(pe, at)
                for j, hs in problems():
                    mm(pbank(2)[hs, j, :], ubuf[hs, j, :], tri[hs, j, :], start=True, stop=True)
                pe.drain().then_inc(met, 1)
                pe.wait_ge(met, at.step("blocks times the inverse"))
                pass_loop(pe, at)
                pe.drain().then_inc(met, 1)
                pe.wait_ge(met, at.step("blocks times the inverse copied out"))
                pass_loop(pe, at)
                for j, hs in problems():
                    mm(pbank(4)[hs, j, :], tri_t[hs, j, :], xbuf[hs, j, :], start=True, stop=True)
                for j, hs in problems():
                    mm(pbank(6)[hs, j, :], xbuf[hs, j, :], tri_t[hs, j, :], start=True, stop=True)
                pe.drain().then_inc(met, 1)
                pe.wait_ge(met, at.step("what the level adds"))
                pass_loop(pe, at)

            counted_loop(pe, at, len(LEVELS), {"meet": 4}, level)
            pe.drain().then_inc(met, 1)
            pe.wait_ge(met, at.step("inverse"))
            for j, hs in problems():
                mm(pbank(0)[hs, j, :], m_t[hs, j, :], v_tok[hs, j, :], start=True, stop=True)
            for j, hs in problems():
                mm(pbank(2)[hs, j, :], alpha_tok[hs, j, :], tri_t[hs, j, :], start=True, stop=True)
            pe.drain().then_inc(met, 1)
            pe.wait_ge(met, at.step("M V and T alpha"))
            pe.drain().then_inc(met, 1)
            pe.wait_ge(met, at.step("M V and T alpha copied out"))
            for j, hs in problems():
                mm(pbank(4)[hs, j, :], tri_t[hs, j, :], xbuf[hs, j, :], start=True, stop=True)
            pe.drain().then_inc(met, 1)
            pe.wait_ge(met, at.step("T M V"))
            pe.drain().then_inc(met, 1)
            pe.wait_ge(met, at.step("T M V copied out"))
            for c in range(S // C):
                for hs in HALF:
                    for t in range(RT):
                        mm(pbank(0)[hs, t, :], tat[hs, 4 * t + c, :], state[hs, t, :], start=True, stop=True)
                pe.drain().then_inc(met, 1)
                pe.wait_ge(met, at.step("T alpha by the state"))
                pe.drain().then_inc(met, 1)
                pe.wait_ge(met, at.step("u"))
                for hs in HALF:
                    for t in range(RT):
                        j = 4 * t + c
                        o = pbank(2)[hs, t, :]
                        mm(o, state[hs, t, :], ar[hs, j, C:2 * C], start=True, stop=False)
                        mm(o, ubuf[hs, t, :], neg_nt[hs, j, :], start=False, stop=False)
                        mm(o, v_tok[hs, j, :], w_t[hs, j, :], start=False, stop=True)
                        o = pbank(4)[hs, t, :]
                        mm(o, beta_tok[hs, j, :], ubuf[hs, t, :], start=True, stop=False)
                        mm(o, kappa_tok[hs, j, :], v_tok[hs, j, :], start=False, stop=True)
                pe.drain().then_inc(met, 1)
                pe.wait_ge(met, at.step("the chunk's output and change of state"))
                pe.drain().then_inc(met, 1)
                pe.wait_ge(met, at.step("the chunk's output and state copied out"))
            for t in range(RT):
                ts = slice(t * S, (t + 1) * S)
                mm(banks(0, 2)[:, ts], cst("heads"), o_t[:, t, :], start=True, stop=True)
                mm(banks(2, 2)[:, ts], cst("heads"), R_[:, ts], start=True, stop=True)
            pe.drain().then_inc(met, 1)
            pe.wait_ge(met, at.step("means, bonus"))
            pe.drain().then_inc(met, 1)
            pe.wait_ge(met, at.step("squares of the centred output"))
            for t in range(RT):
                ts = slice(t * S, (t + 1) * S)
                mm(banks(4, 2)[:, ts], cst("heads"), T_[:, ts], start=True, stop=True)
            pe.drain().then_inc(met, 1)
            pe.wait_ge(met, at.step("variances"))
            pe.drain().then_inc(met, 1)
            pe.wait_ge(met, at.step("root of the variance"))
            pe.drain().then_inc(met, 1)
            pe.wait_ge(met, at.step("rwkv output"))

        def pe_s5(pe, at):
            pe.drain().then_inc(met, 1)
            pe.wait_ge(met, at.step("dt"))
            pe.drain().then_inc(met, 1)
            pe.wait_ge(met, at.step("angles"))
            pe.drain().then_inc(met, 1)
            pe.wait_ge(met, at.step("sines"))
            for grp in range(4):
                cs = slice(grp * P, (grp + 1) * P)
                for t in range(4):
                    rows = slice(32 * t, 32 * t + 32)
                    mm(ps[:, t, 0:S], sm("b_re")[rows, cs], u_t[rows, grp, :], start=True, stop=True)
                    mm(ps[:, t, S:2 * S], sm("b_im")[rows, cs], u_t[rows, grp, :], start=True, stop=True)
                pe.drain().then_inc(met, 1)
                pe.wait_ge(met, at.step("B u"))
                pe.drain().then_inc(met, 1)
                pe.wait_ge(met, at.step("states"))
                for t in range(4):
                    o = ps[32 * t:32 * t + 32, 4 + grp, 0:S]
                    mm(o, c_re[:, 4 * grp + t, :], s5b[0][:, t, :], start=True, stop=False)
                    mm(o, c_im[:, 4 * grp + t, :], s5b[1][:, t, :], start=False, stop=True)
            pe.drain().then_inc(met, 1)
            pe.wait_ge(met, at.step("C x"))
            pe.drain().then_inc(met, 1)
            pe.wait_ge(met, at.step("y"))
            pe.drain().then_inc(met, 1)
            pe.wait_ge(met, at.step("gelu"))
            wt = next_chunk(pe, at, 4, RW)
            for t in range(4):
                for k in range(4):
                    last = mm(banks(0, 2)[:, t * S:(t + 1) * S], wt[:, k, t * P:(t + 1) * P], u_t[:, k, :],
                              start=k == 0, stop=k == 3)
            used(last, at)
            pe.drain().then_inc(met, 1)
            pe.wait_ge(met, at.step("glu product"))
            pe.drain().then_inc(met, 1)
            pe.wait_ge(met, at.step("glu gate"))
            pe.drain().then_inc(met, 1)
            pe.wait_ge(met, at.step("s5 output"))

        def pe_diff(pe, at):
            pe_project(pe, at, hn, 8)
            pe_project(pe, at, hn, 4, "token")
            pe_norm(pe, at, table="heads", groups=8, per=1)
            pe_norm(pe, at, table="heads", groups=8, per=1)
            mm(ps[:, 4, 0:2], cst("ones"), tiny[:, 0:2], start=True, stop=True)
            pe.drain().then_inc(met, 1)
            pe.wait_ge(met, at.step("sums for lambda"))
            pe.drain().then_inc(met, 1)
            pe.wait_ge(met, at.step("exponentials for lambda"))
            for qb in range(2):
                for half in range(2):
                    for hl in range(4):
                        for c in range(2):
                            mm(ps[:, 2 * (hl // 2) + c, (hl % 2) * S:(hl % 2) * S + S],
                               aq[HALF[c], 4 * half + hl, qb * P:(qb + 1) * P], ak[HALF[c], 4 * half + hl, :],
                               start=True, stop=True)
                    pe_softmax(pe, at, 4, lambda u: 4 * (u // 2) + u % 2)
                    for hl in range(4):
                        hd = 4 * half + hl
                        for kb in range(2):
                            mm(ps[:, 0, hl * P:(hl + 1) * P], av[:, kb, hd * P:(hd + 1) * P], apt4[:, kb, hl, :],
                               start=kb == 0, stop=kb == 1)
                    pe.drain().then_inc(met, 1)
                    pe.wait_ge(met, at.step("products with v"))
                    pe.drain().then_inc(met, 1)
                    pe.wait_ge(met, at.step("attention output"))
            pe_norm(pe, at, groups=8, per=1)
            pe_project(pe, at, mix, 4)

        def unit_of(hd):
            return 4 * (hd // 4) + 2 * (hd % 2) + hd // 2 % 2

        def pe_second_mixer(pe, at):
            pe_project(pe, at, hn, 2)
            pe_project(pe, at, hn, 1, "both")
            pe_project(pe, at, hn, 1)
            pe_project(pe, at, hn, 1, "token")
            pe_project(pe, at, hn, 3)
            pe_norm(pe, at, table="heads", groups=5, per=1)
            for t in range(4):
                mm(banks(4, 2)[:, t * S:(t + 1) * S], cst("turn"), qk[:, t, :], start=True, stop=True)
            for g in range(2):
                cs = slice(g * S, (g + 1) * S)
                mm(ps[:, 6, cs], cst("dup", g * P, (g + 1) * P), qk[:, 4, :], start=True, stop=True)
                mm(ps[:, 7, cs], cst("dupturn", g * P, (g + 1) * P), qk[:, 4, :], start=True, stop=True)
            for sh in range(4):
                for b in range(2):
                    mm(ps[HALF[sh % 2], sh // 2, b * P:(b + 1) * P], sv_tok[:, b, 64 * sh:64 * sh + 64],
                       lay("sgw", sh * P, (sh + 1) * P), start=True, stop=True)
            pe.drain().then_inc(met, 1)
            pe.wait_ge(met, at.step("turned features, gating products"))
            pass_loop(pe, at)
            pe.drain().then_inc(met, 1)
            pe.wait_ge(met, at.step("q and k, gating and convolution outputs"))
            pass_loop(pe, at)
            for qb in range(2):
                for hd in range(8):
                    u = unit_of(hd)
                    mm(banks(0, 4)[:, u * S:(u + 1) * S], q_r[HALF[hd % 2], hd // 2, qb * P:(qb + 1) * P],
                       q_r[HALF[hd % 2], 4 + hd // 4, :], start=True, stop=True)
                pe_softmax(pe, at, 8)
                for hd in range(8):
                    g = hd // 4
                    for kb in range(2):
                        mm(ps[HALF[hd % 2], 0, (hd // 2) * P:(hd // 2 + 1) * P],
                           v_tok2[:, kb, 64 * g:64 * g + 64], apt[:, kb, unit_of(hd), :],
                           start=kb == 0, stop=kb == 1)
                pe.drain().then_inc(met, 1)
                pe.wait_ge(met, at.step("products with v"))
                pass_loop(pe, at)
                pe.drain().then_inc(met, 1)
                pe.wait_ge(met, at.step("attention output"))
                pass_loop(pe, at)
            pe_project(pe, at, mix, 4)

        def pe_moe_gates(pe, at):
            for b in range(2):
                for k in range(KT):
                    mm(ps[:, 0, b * NE:(b + 1) * NE], hn[:, k, b * P:(b + 1) * P],
                       sm("w_router", k * NE, (k + 1) * NE), start=k == 0, stop=k == KT - 1)
            pe.drain().then_inc(met, 1)
            pe.wait_ge(met, at.step("logits"))
            pe.drain().then_inc(met, 1)
            pe.wait_ge(met, at.step("the two largest logits"))
            pe.drain().then_inc(met, 1)
            pe.wait_ge(met, at.step("exponential of their difference"))
            pe.drain().then_inc(met, 1)
            pe.wait_ge(met, at.step("gates by token"))
            for e in range(NE):
                for b in range(2):
                    mm(banks(0, 4)[:, e * S + b * P:e * S + (b + 1) * P], gate_rep[:, b, e, :], cst("ident"),
                       start=True, stop=True)
            pe.drain().then_inc(met, 1)
            pe.wait_ge(met, at.step("gates on every partition"))
            pe.drain().then_inc(met, 1)
            pe.wait_ge(met, at.step("gates copied out"))

        def tensor_program(pe, at):
            pe.wait_ge(loaded, 48)
            pe_norm(pe, at)
            pe_project(pe, at, hn, 6)
            pe_project(pe, at, hn, 1, width=288)
            pe_project(pe, at, hn, 2)
            pe_rwkv(pe, at)
            pe_s5(pe, at)
            pe_project(pe, at, mix, 4)
            pe_memory(pe, at)
            pe_norm(pe, at)
            pe_ff(pe, at, 1, 5, 2)
            pe_norm(pe, at)
            pe_diff(pe, at)
            pe_memory(pe, at)
            pe_norm(pe, at)
            pe_moe_gates(pe, at)
            pe_ff(pe, at, 2, (MOE_STEPS - 2) // 2, 2)
            with pe.Fori(0, 2) as layer:
                at.enter(layer, PER_LAYER)
                pe.drain().then_inc(met, 1)
                pe.wait_ge(met, at.step("the layer's small inputs"))
                pass_loop(pe, at)
                pe_norm(pe, at)
                pe_second_mixer(pe, at)
                pe_norm(pe, at)
                pe_ff(pe, at, 1, 1, FF_STEPS - 1)
                at.leave(2)

        PER_LAYER = {"meet": 39, "chunk": 12 + 3 * FF_STEPS, "evac": 12, "act": FF_STEPS}
        PER_LAYER_SILU = {**PER_LAYER, "silu": FF_STEPS, "conv": FF_STEPS}

        def activate(o, i, func, **kw):
            return nc.scalar.activation(o, i, func, **kw)

        def copy(o, i, **kw):
            return nc.scalar.activation(o, i, ACT.Copy, **kw)

        def evac(eng, at, n, copy_out):
            for c in range(n):
                eng.wait_ge(chunk_used, at.value("chunk", 1))
                copy_out(c, banks(c % 4)).then_inc(evacuated, 1)
                at.add("chunk")
                at.add("evac")
            eng.drain().then_inc(met, 1)
            eng.wait_ge(met, at.step("projection copied out"))
            pass_loop(eng, at)

        def leave_evac(eng, at, n):
            at.add("chunk", n)
            at.add("evac", n)
            eng.drain().then_inc(met, 1)
            eng.wait_ge(met, at.step("projection copied out"))
            pass_loop(eng, at)

        def act_root(act, o, i, scale, eps):
            activate(o, i, ACT.Ln, scale=scale, bias=eps)
            act.drain()
            activate(o, o, ACT.Exp, scale=-0.5)

        def act_norm(act, at, dim=D, groups=1, more=None):
            act.drain().then_inc(met, 1)
            act.wait_ge(met, at.step("squares"))
            pass_loop(act, at)
            act.drain().then_inc(met, 1)
            act.wait_ge(met, at.step("sums of squares"))
            pass_loop(act, at)
            act_root(act, rstd[:, 0:groups * S], banks(4, 4)[:, 0:groups * S], 1.0 / dim, cst("eps"))
            if more:
                more()
            act.drain().then_inc(met, 1)
            act.wait_ge(met, at.step("roots"))
            pass_loop(act, at)
            act.drain().then_inc(met, 1)
            act.wait_ge(met, at.step("normed"))
            pass_loop(act, at)

        def act_softmax(act, at, scale, units):
            act.drain().then_inc(met, 1)
            act.wait_ge(met, at.step("scores"))
            pass_loop(act, at)
            act.drain().then_inc(met, 1)
            act.wait_ge(met, at.step("scores less their maxima"))
            pass_loop(act, at)
            activate(ae, ae, ACT.Exp, scale=scale)
            act.drain().then_inc(met, 1)
            act.wait_ge(met, at.step("exponentials"))
            pass_loop(act, at)
            act.drain().then_inc(met, 1)
            act.wait_ge(met, at.step("probabilities"))
            pass_loop(act, at)
            act.drain().then_inc(met, 1)
            act.wait_ge(met, at.step("transposes"))
            pass_loop(act, at)
            n = 2 * units * P
            copy(slot(12, 2)[:, 0:n], banks(4, 4)[:, 0:n])
            act.drain().then_inc(met, 1)
            act.wait_ge(met, at.step("transposes copied out"))
            pass_loop(act, at)

        def act_memory(act, at):
            act.dma_start(mem_sb, mem_t.rearrange("(k p) n -> p k n", p=P)).then_inc(mem_loaded, 16)
            act_norm(act, at)
            evac(act, at, 4, lambda c, b: copy(aq[:, 2 * c:2 * c + 2, :], tiles(b)))
            act_norm(act, at, 256, 4)
            act_norm(act, at)
            evac(act, at, 4, lambda c, b: copy(ak[:, 2 * c:2 * c + 2, :], tiles(b)))
            evac(act, at, 4, lambda c, b: copy(av[:, :, c * CH:(c + 1) * CH], tiles(b)))
            act_norm(act, at, 256, 4)
            act_softmax(act, at, 256 ** -0.5, 8)
            act.drain().then_inc(met, 1)
            act.wait_ge(met, at.step("products with v"))
            copy(flat(mix), banks(0, 4))
            act.drain().then_inc(met, 1)
            act.wait_ge(met, at.step("attention output"))
            leave_evac(act, at, 4)

        def act_ff(act, at, ahead, turns, unroll, convolved=False):
            def step(f):
                if convolved:
                    act.wait_ge(conv_done, at.value("conv", 1))
                    src = gate_conv(f)
                else:
                    act.wait_ge(chunk_used, at.value("chunk", 1))
                    src = tiles(ps[:, 2 * (f % 2), :])
                if f > 1:
                    act.wait_ge(act_ready, at.value("act", -1))
                activate(silu_buf(f), src, ACT.Silu).then_inc(silu_done, 1)
                at.add("chunk", 3 if f else 2)
                for k in ("act", "silu", "conv") if convolved else ("act", "silu"):
                    at.add(k)

            for f in range(ahead):
                step(f)

            def body():
                for f in range(ahead, ahead + unroll):
                    step(f)

            counted_loop(act, at, turns, {"chunk": 3 * unroll, "act": unroll, "silu": unroll}, body)
            at.add("chunk")
            act.drain().then_inc(met, 1)
            act.wait_ge(met, at.step("down products"))
            pass_loop(act, at)
            act.drain().then_inc(met, 1)
            act.wait_ge(met, at.step("residual"))
            pass_loop(act, at)

        def act_rwkv(act, at):
            act.drain().then_inc(met, 1)
            act.wait_ge(met, at.step("inputs shifted"))
            activate(zg[0:64, 0, :], zg[0:64, 0, :], ACT.Tanh)
            activate(zg[:, 1, :], zg[:, 1, :], ACT.Sigmoid)
            activate(zg[0:32, 2, :], zg[0:32, 2, :], ACT.Sigmoid)
            act.drain().then_inc(met, 1)
            act.wait_ge(met, at.step("lora inputs, squares of kk"))
            act.drain().then_inc(met, 1)
            act.wait_ge(met, at.step("lora products, sums for kk"))
            for t in range(RT):
                ts = slice(t * S, (t + 1) * S)
                activate(LW_[:, ts], banks(0, 2)[:, ts], ACT.Sigmoid, bias=sm("w0", t, t + 1))
                activate(A_[:, ts], banks(2, 2)[:, ts], ACT.Sigmoid, bias=sm("a0", t, t + 1))
            copy(G_, banks(4, 2))
            act.drain().then_inc(met, 1)
            act.wait_ge(met, at.step("sigmoids"))
            act_root(act, work, work, 1.0, 0.0)
            act.drain().then_inc(met, 1)
            act.wait_ge(met, at.step("cumulated decays, root for kk"))
            activate(LT_, CL_, ACT.Exp)
            activate(MT_, CL_, ACT.Exp, scale=-1.0)
            activate(NT_, NT_, ACT.Exp)
            act.drain().then_inc(met, 1)
            act.wait_ge(met, at.step("exponentials, kk"))
            act.drain().then_inc(met, 1)
            act.wait_ge(met, at.step("alpha, beta, kappa, rho"))
            act.drain().then_inc(met, 1)
            act.wait_ge(met, at.step("beta and kappa by alpha and rho"))
            act.drain().then_inc(met, 1)
            act.wait_ge(met, at.step("masked"))
            act.drain().then_inc(met, 1)
            act.wait_ge(met, at.step("alpha by beta, token-major forms"))
            copy(alpha_tok, pbank(2))
            copy(beta_tok, pbank(4), scale=-1.0)
            copy(kappa_tok, pbank(6))
            act.drain().then_inc(met, 1)
            act.wait_ge(met, at.step("inverse of blocks of two"))
            act.drain().then_inc(met, 1)
            act.wait_ge(met, at.step("v token-major"))
            copy(v_tok, pbank(0))

            def level():
                act.drain().then_inc(met, 1)
                act.wait_ge(met, at.step("blocks below the diagonal"))
                pass_loop(act, at)
                act.drain().then_inc(met, 1)
                act.wait_ge(met, at.step("blocks times the inverse"))
                pass_loop(act, at)
                copy(xbuf, pbank(2))
                act.drain().then_inc(met, 1)
                act.wait_ge(met, at.step("blocks times the inverse copied out"))
                pass_loop(act, at)
                act.drain().then_inc(met, 1)
                act.wait_ge(met, at.step("what the level adds"))
                pass_loop(act, at)

            counted_loop(act, at, len(LEVELS), {"meet": 4}, level)
            act.drain().then_inc(met, 1)
            act.wait_ge(met, at.step("inverse"))
            act.drain().then_inc(met, 1)
            act.wait_ge(met, at.step("M V and T alpha"))
            copy(xbuf, pbank(0))
            act.drain().then_inc(met, 1)
            act.wait_ge(met, at.step("M V and T alpha copied out"))
            act.drain().then_inc(met, 1)
            act.wait_ge(met, at.step("T M V"))
            copy(uv, pbank(4))
            act.drain().then_inc(met, 1)
            act.wait_ge(met, at.step("T M V copied out"))
            for c in range(S // C):
                act.drain().then_inc(met, 1)
                act.wait_ge(met, at.step("T alpha by the state"))
                act.drain().then_inc(met, 1)
                act.wait_ge(met, at.step("u"))
                act.drain().then_inc(met, 1)
                act.wait_ge(met, at.step("the chunk's output and change of state"))
                copy(o_t[:, :, c * C:(c + 1) * C], pbank(2)[:, 0:RT, :])
                act.drain().then_inc(met, 1)
                act.wait_ge(met, at.step("the chunk's output and state copied out"))
            act.drain().then_inc(met, 1)
            act.wait_ge(met, at.step("means, bonus"))
            act.drain().then_inc(met, 1)
            act.wait_ge(met, at.step("squares of the centred output"))
            act.drain().then_inc(met, 1)
            act.wait_ge(met, at.step("variances"))
            act_root(act, work, banks(4, 2), 1.0 / 64, cst("gn_eps"))
            act.drain().then_inc(met, 1)
            act.wait_ge(met, at.step("root of the variance"))
            act.drain().then_inc(met, 1)
            act.wait_ge(met, at.step("rwkv output"))

        def act_s5(act, at):
            activate(s5t(0), sm("log_dt"), ACT.Exp)
            act.drain().then_inc(met, 1)
            act.wait_ge(met, at.step("dt"))
            act.drain().then_inc(met, 1)
            act.wait_ge(met, at.step("angles"))
            activate(s5t(1), s5t(1), ACT.Exp)
            activate(s5t(2), s5t(2), ACT.Sin)
            activate(s5t(3), s5t(3), ACT.Sin)
            act.drain().then_inc(met, 1)
            act.wait_ge(met, at.step("sines"))
            for grp in range(4):
                act.drain().then_inc(met, 1)
                act.wait_ge(met, at.step("B u"))
                act.drain().then_inc(met, 1)
                act.wait_ge(met, at.step("states"))
            act.drain().then_inc(met, 1)
            act.wait_ge(met, at.step("C x"))
            act.drain().then_inc(met, 1)
            act.wait_ge(met, at.step("y"))
            activate(u_t, u_t, ACT.Gelu_apprx_tanh)
            act.drain().then_inc(met, 1)
            act.wait_ge(met, at.step("gelu"))
            at.add("chunk")
            act.drain().then_inc(met, 1)
            act.wait_ge(met, at.step("glu product"))
            for t in range(4):
                activate(s5b[0][:, t, :], banks(0, 2)[:, t * S:(t + 1) * S], ACT.Sigmoid, bias=sm("b_glu", t, t + 1))
            act.drain().then_inc(met, 1)
            act.wait_ge(met, at.step("glu gate"))
            act.drain().then_inc(met, 1)
            act.wait_ge(met, at.step("s5 output"))

        def act_diff(act, at):
            evac(act, at, 8, lambda c, b: copy((aq if c < 4 else ak)[:, 2 * (c % 4):2 * (c % 4) + 2, :], tiles(b)))
            evac(act, at, 4, lambda c, b: copy(av[:, :, c * CH:(c + 1) * CH], tiles(b)))
            act_norm(act, at, 64, 8)
            act_norm(act, at, 64, 8)
            act.drain().then_inc(met, 1)
            act.wait_ge(met, at.step("sums for lambda"))
            activate(tiny[:, 2:4], ps[:, 4, 0:2], ACT.Exp)
            act.drain().then_inc(met, 1)
            act.wait_ge(met, at.step("exponentials for lambda"))
            for _ in range(4):
                act_softmax(act, at, 1.0, 4)
                act.drain().then_inc(met, 1)
                act.wait_ge(met, at.step("products with v"))
                act.drain().then_inc(met, 1)
                act.wait_ge(met, at.step("attention output"))
            act_norm(act, at, P, 8)
            leave_evac(act, at, 4)

        def act_second_mixer(act, at):
            evac(act, at, 2, lambda c, b: copy(qk[:, 2 * c:2 * c + 2, :], tiles(b)))

            def k_v(c, b):
                copy(qk[:, 4, :], b[:, 0:S])
                act.drain()
                return copy(v_tok2, tiles(b[:, S:2 * S], P))

            evac(act, at, 1, k_v)
            evac(act, at, 1, lambda c, b: copy(su, tiles(b)))
            evac(act, at, 1, lambda c, b: copy(sv_tok, tiles(b)))
            evac(act, at, 3, lambda c, b: copy((cb, cc, cx)[c], tiles(b)))
            act_norm(act, at, 64, 5, lambda: act_root(act, tiny[:, 6:8], tiny[:, 6:8], 1.0 / 256, cst("eps")))
            act.drain().then_inc(met, 1)
            act.wait_ge(met, at.step("turned features, gating products"))
            pass_loop(act, at)
            act.drain().then_inc(met, 1)
            act.wait_ge(met, at.step("q and k, gating and convolution outputs"))
            pass_loop(act, at)
            for _ in range(2):
                act_softmax(act, at, 64 ** -0.5, 8)
                act.drain().then_inc(met, 1)
                act.wait_ge(met, at.step("products with v"))
                pass_loop(act, at)
                act.drain().then_inc(met, 1)
                act.wait_ge(met, at.step("attention output"))
                pass_loop(act, at)
            leave_evac(act, at, 4)

        def act_moe_gates(act, at):
            act.drain().then_inc(met, 1)
            act.wait_ge(met, at.step("logits"))
            act.drain().then_inc(met, 1)
            act.wait_ge(met, at.step("the two largest logits"))
            activate(tiny[:, 100:102], tiny[:, 100:102], ACT.Exp)
            act.drain().then_inc(met, 1)
            act.wait_ge(met, at.step("exponential of their difference"))
            act.drain().then_inc(met, 1)
            act.wait_ge(met, at.step("gates by token"))
            act.drain().then_inc(met, 1)
            act.wait_ge(met, at.step("gates on every partition"))
            copy(slot(8, 2), banks(0, 4))
            act.drain().then_inc(met, 1)
            act.wait_ge(met, at.step("gates copied out"))

        def scalar_program(act, at):
            act.wait_ge(loaded, 48)
            act_norm(act, at)
            evac(act, at, 6, lambda c, b: copy(z12[:, 2 * c:2 * c + 2, :], tiles(b)))

            def lora_in(c, b):
                copy(zg[:, 0:2, :], tiles(b))
                act.drain()
                return copy(zg[0:32, 2, :], ps[0:32, 1, 0:S])

            evac(act, at, 1, lora_in)
            evac(act, at, 2, lambda c, b: copy(u_t[:, 2 * c:2 * c + 2, :], tiles(b)))
            act_rwkv(act, at)
            act_s5(act, at)
            leave_evac(act, at, 4)
            act_memory(act, at)
            act_norm(act, at)
            act_ff(act, at, 3, 4, 2)
            act_norm(act, at)
            act_diff(act, at)
            act_memory(act, at)
            act_norm(act, at)
            act_moe_gates(act, at)
            act_ff(act, at, 2, (MOE_STEPS - 2) // 2, 2)
            with act.Fori(0, 2) as layer:
                at.enter(layer, PER_LAYER_SILU)
                act.drain().then_inc(met, 1)
                act.wait_ge(met, at.step("the layer's small inputs"))
                pass_loop(act, at)
                act_norm(act, at)
                act_second_mixer(act, at)
                act_norm(act, at)
                act_ff(act, at, 1, 1, FF_STEPS - 1, True)
                at.leave(2)

        def tt(dve, o, a, b, op):
            nc.vector.tensor_tensor(o, a, b, op)
            dve.drain()

        def ts(dve, o, a, s1, s2=None, op0=ALU.mult, op1=None):
            nc.vector.tensor_scalar(o, a, s1, s2, op0, *([op1] if op1 is not None else []))
            dve.drain()

        def stt(dve, o, a, s, b, op0, op1):
            nc.vector.scalar_tensor_tensor(o, a, s, b, op0, op1)
            dve.drain()

        MUL, ADD, SUB = ALU.mult, ALU.add, ALU.subtract

        def dve_norm(dve, at, src, dst, gain, groups=1, per=KT, sq=scr, before=None, after=None):
            n = groups * per
            nc.vector.tensor_tensor(sq[:, 0:n, :], src[:, 0:n, :], src[:, 0:n, :], MUL)
            if before:
                before()
            dve.drain().then_inc(met, 1)
            dve.wait_ge(met, at.step("squares"))
            pass_loop(dve, at)
            dve.drain().then_inc(met, 1)
            dve.wait_ge(met, at.step("sums of squares"))
            pass_loop(dve, at)
            dve.drain().then_inc(met, 1)
            dve.wait_ge(met, at.step("roots"))
            pass_loop(dve, at)
            for t in range(n):
                g = t // per
                nc.vector.scalar_tensor_tensor(dst[:, t, :], src[:, t, :], gain(t), rstd[:, g * S:(g + 1) * S],
                                               MUL, MUL)
            if after:
                after()
            dve.drain().then_inc(met, 1)
            dve.wait_ge(met, at.step("normed"))
            pass_loop(dve, at)

        def dve_residual(dve, at, n=4):
            evac(dve, at, n, lambda c, b: nc.vector.tensor_tensor(h[:, 2 * c:2 * c + 2, :], tiles(b),
                                                                  h[:, 2 * c:2 * c + 2, :], ADD))

        def dve_softmax(dve, at, biased=None, lam=None):
            dve.drain().then_inc(met, 1)
            dve.wait_ge(met, at.step("scores"))
            pass_loop(dve, at)
            if biased:
                biased()
            scores = ae if biased else tiles(banks(0, 4))
            top, total = tiny[:, 16:24], tiny[:, 24:32]
            nc.vector.reduce_max(top, scores, AX)
            dve.drain()
            tt(dve, ae, scores, scalars(top, [P, 8, S]), SUB)
            dve.drain().then_inc(met, 1)
            dve.wait_ge(met, at.step("scores less their maxima"))
            pass_loop(dve, at)
            dve.drain().then_inc(met, 1)
            dve.wait_ge(met, at.step("exponentials"))
            pass_loop(dve, at)
            nc.vector.reduce_sum(total, ae, AX)
            dve.drain()
            nc.vector.reciprocal(total, total)
            dve.drain()
            if lam is not None:
                second = total.rearrange("p (a c b) -> p a c b", c=2, b=2)[:, :, 1, :]
                ts(dve, second, second, lam)
            tt(dve, ae, ae, scalars(total, [P, 8, S]), MUL)
            if lam is not None:
                e4 = slot(10, 2).rearrange("p (a c n) -> p a c n", a=2, c=2)
                tt(dve, e4[:, :, 0, :], e4[:, :, 0, :], e4[:, :, 1, :], ADD)
            dve.drain().then_inc(met, 1)
            dve.wait_ge(met, at.step("probabilities"))
            pass_loop(dve, at)
            dve.drain().then_inc(met, 1)
            dve.wait_ge(met, at.step("transposes"))
            pass_loop(dve, at)
            dve.drain().then_inc(met, 1)
            dve.wait_ge(met, at.step("transposes copied out"))
            pass_loop(dve, at)

        def dve_memory(dve, at, l):
            dve_norm(dve, at, h, hn, lambda t: sm("g_xattn", KT * l + t, KT * l + t + 1))
            leave_evac(dve, at, 4)
            dve_norm(dve, at, aq, aq, lambda t: sm("g_xq", 2 * l + t % 2, 2 * l + t % 2 + 1), 4, 2)
            dve.wait_ge(mem_loaded, 16 * (l + 1))
            dve_norm(dve, at, mem_sb, memn, lambda t: sm("g_mem", KT * l + t, KT * l + t + 1))
            leave_evac(dve, at, 4)
            leave_evac(dve, at, 4)
            dve_norm(dve, at, ak, ak, lambda t: sm("g_xk", 2 * l + t % 2, 2 * l + t % 2 + 1), 4, 2)
            dve_softmax(dve, at)
            dve.drain().then_inc(met, 1)
            dve.wait_ge(met, at.step("products with v"))
            dve.drain().then_inc(met, 1)
            dve.wait_ge(met, at.step("attention output"))
            dve_residual(dve, at)

        def dve_conv(dve, o, x, taps):
            for i in range(2):
                ts(dve, o[:, i, :], x[:, i, :], taps(1, i))
                stt(dve, o[:, i, 1:S], x[:, i, 0:S - 1], taps(0, i), o[:, i, 1:S], MUL, ADD)
                stt(dve, o[:, i, 0:S - 1], x[:, i, 1:S], taps(2, i), o[:, i, 0:S - 1], MUL, ADD)

        def dve_step(dve, at, f, gate=None, taps=None):
            up = tiles(ps[:, 2 * (f % 2) + 1, :])
            if taps:
                dve.wait_ge(chunk_used, at.value("chunk", 1))
                dve_conv(dve, gate_conv(f), tiles(ps[:, 2 * (f % 2), :]), lambda tap, i: taps(tap, 2 * f + i))
                dve.drain().then_inc(conv_done, 1)
            dve.wait_ge(chunk_used, at.value("chunk", 2))
            if taps:
                dve_conv(dve, up_conv(f), up, lambda tap, i: taps(tap, 22 + 2 * f + i))
                up = up_conv(f)
            dve.wait_ge(silu_done, at.value("silu", 1))
            ins = nc.vector.tensor_tensor(act_buf(f), silu_buf(f), up, MUL)
            if gate is not None:
                dve.drain()
                ins = nc.vector.tensor_tensor(act_buf(f), act_buf(f), gate, MUL)
            ins.then_inc(act_ready, 1)
            at.add("chunk", 3 if f else 2)
            for k in ("act", "silu", "conv") if taps else ("act", "silu"):
                at.add(k)

        def dve_ff_end(dve, at):
            at.add("chunk")
            dve.drain().then_inc(met, 1)
            dve.wait_ge(met, at.step("down products"))
            pass_loop(dve, at)
            nc.vector.tensor_tensor(flat(h), banks(4, 4), flat(h), ADD)
            dve.drain().then_inc(met, 1)
            dve.wait_ge(met, at.step("residual"))
            pass_loop(dve, at)

        def dve_rwkv(dve, at):
            for z, rows, mu in ((z12, slice(0, P), sm("mu", 0, 12)), (zg[:, 0:2, :], slice(0, P), sm("mu", 12, 14)),
                                (zg[:, 2:3, :], slice(0, 32), sm("mu", 14, 15))):
                n = z.shape[1]
                z, d = z[rows, :, :], shift_tmp[rows, 0:n, :]
                nc.vector.tensor_tensor(d[:, :, 1:S], z[:, :, 0:S - 1], z[:, :, 1:S], SUB)
                ts(dve, d[:, :, 0:1], z[:, :, 0:1], -1.0)
                tt(dve, d, d, scalars(mu[rows, :], [rows.stop, n, S]), MUL)
                tt(dve, z, z, d, ADD)
            dve.drain().then_inc(met, 1)
            dve.wait_ge(met, at.step("inputs shifted"))

            def scale_tiles(o, i, name):
                tt(dve, tiles(o), tiles(i), scalars(sm(name), [P, RT, S]), MUL)

            scale_tiles(KK_, K_, "k_k")
            tt(dve, work, KK_, KK_, MUL)
            dve.drain().then_inc(met, 1)
            dve.wait_ge(met, at.step("lora inputs, squares of kk"))
            dve.drain().then_inc(met, 1)
            dve.wait_ge(met, at.step("lora products, sums for kk"))
            ts(dve, work, banks(6, 2), 1e-24, None, ALU.max)
            dve.drain().then_inc(met, 1)
            dve.wait_ge(met, at.step("sigmoids"))
            ts(dve, LW_, LW_, -math.exp(-0.5))
            for t in range(RT):
                cs = slice(t * S, (t + 1) * S)
                nc.vector.tensor_tensor_scan(CL_[:, cs], cst("reset"), LW_[:, cs], 0.0, MUL, ADD)
            dve.drain()
            tt(dve, NT_, CL_, LW_, SUB)
            ts(dve, tiny[:, 32:36], sm("k_a"), -1.0, 1.0, MUL, ADD)
            scale_tiles(T_, A_, "k_a")
            tt(dve, tiles(T_), tiles(T_), scalars(tiny[:, 32:36], [P, RT, S]), ADD)
            tt(dve, K_, K_, T_, MUL)
            dve.drain().then_inc(met, 1)
            dve.wait_ge(met, at.step("cumulated decays, root for kk"))
            tt(dve, KK_, KK_, work, MUL)
            tt(dve, A_, A_, KK_, MUL)
            dve.drain().then_inc(met, 1)
            dve.wait_ge(met, at.step("exponentials, kk"))
            tt(dve, ar[:, :, 0:C], by64(KK_), by64(NT_), MUL)
            tt(dve, ar[:, :, C:2 * C], by64(R_), by64(LT_), MUL)
            tt(dve, BE_, A_, MT_, MUL)
            tt(dve, KA_, K_, MT_, MUL)
            nc.vector.tensor_copy(chunk_decay, by64(LT_)[:, :, C - 1])
            scale_tiles(R_, R_, "r_k")
            tt(dve, R_, R_, K_, MUL)
            dve.drain().then_inc(met, 1)
            dve.wait_ge(met, at.step("alpha, beta, kappa, rho"))
            dve.drain().then_inc(met, 1)
            dve.wait_ge(met, at.step("beta and kappa by alpha and rho"))
            full = [P, NJ, C]
            by_b, by_k = tiles(banks(0, 4), 2 * C), tiles(banks(4, 4), 2 * C)
            ts(dve, neg_lt, by_b[:, :, 0:C], -1.0)
            stt(dve, neg_nt, by_b[:, :, C:2 * C], -1.0, repeated(cst("upto"), full), MUL, MUL)
            tt(dve, m_t, by_k[:, :, 0:C], repeated(cst("before"), full), MUL)
            tt(dve, w_t, by_k[:, :, C:2 * C], repeated(cst("upto"), full), MUL)
            dve.drain().then_inc(met, 1)
            dve.wait_ge(met, at.step("masked"))
            dve.drain().then_inc(met, 1)
            dve.wait_ge(met, at.step("alpha by beta, token-major forms"))
            stt(dve, tri, pbank(0), -1.0, repeated(cst("level1_low"), full), MUL, MUL)
            tt(dve, tri, tri, repeated(cst("eye64"), full), ADD)
            tt(dve, tri_t, neg_lt, repeated(cst("level1"), full), MUL)
            tt(dve, tri_t, tri_t, repeated(cst("eye64"), full), ADD)
            dve.drain().then_inc(met, 1)
            dve.wait_ge(met, at.step("inverse of blocks of two"))
            dve.drain().then_inc(met, 1)
            dve.wait_ge(met, at.step("v token-major"))
            levels_at = CONST_AT["levels"][0]
            with dve.Fori(0, len(LEVELS)) as i:
                at.enter(i, {"meet": 4})
                mask = const_sb[:, bass.ds(i * C + levels_at, C)]
                tt(dve, ubuf, neg_lt, repeated(mask, full), MUL)
                dve.drain().then_inc(met, 1)
                dve.wait_ge(met, at.step("blocks below the diagonal"))
                pass_loop(dve, at)
                dve.drain().then_inc(met, 1)
                dve.wait_ge(met, at.step("blocks times the inverse"))
                pass_loop(dve, at)
                dve.drain().then_inc(met, 1)
                dve.wait_ge(met, at.step("blocks times the inverse copied out"))
                pass_loop(dve, at)
                dve.drain().then_inc(met, 1)
                dve.wait_ge(met, at.step("what the level adds"))
                pass_loop(dve, at)
                tt(dve, tri, tri, pbank(4), ADD)
                tt(dve, tri_t, tri_t, pbank(6), ADD)
                at.leave(len(LEVELS))
            dve.drain().then_inc(met, 1)
            dve.wait_ge(met, at.step("inverse"))
            dve.drain().then_inc(met, 1)
            dve.wait_ge(met, at.step("M V and T alpha"))
            nc.vector.tensor_copy(tat, pbank(2))
            nc.vector.memset(rstd[:, 1024:1024 + RT * C], 0.0)
            dve.drain().then_inc(met, 1)
            dve.wait_ge(met, at.step("M V and T alpha copied out"))
            dve.drain().then_inc(met, 1)
            dve.wait_ge(met, at.step("T M V"))
            dve.drain().then_inc(met, 1)
            dve.wait_ge(met, at.step("T M V copied out"))
            by_chunk = LW_.rearrange("p (t c n) -> p t c n", t=RT, n=C)
            decay = chunk_decay.rearrange("p (t c) -> p t c", t=RT)
            for c in range(S // C):
                dve.drain().then_inc(met, 1)
                dve.wait_ge(met, at.step("T alpha by the state"))
                tt(dve, ubuf[:, 0:RT, :], pbank(0)[:, 0:RT, :], by_chunk[:, :, c, :], ADD)
                dve.drain().then_inc(met, 1)
                dve.wait_ge(met, at.step("u"))
                dve.drain().then_inc(met, 1)
                dve.wait_ge(met, at.step("the chunk's output and change of state"))
                tt(dve, state, state, pbank(4)[:, 0:RT, :], ADD)
                tt(dve, state, state, scalars(decay[:, :, c], [P, RT, C]), MUL)
                dve.drain().then_inc(met, 1)
                dve.wait_ge(met, at.step("the chunk's output and state copied out"))
            dve.drain().then_inc(met, 1)
            dve.wait_ge(met, at.step("means, bonus"))
            stt(dve, o_t, tiles(banks(0, 2)), -1.0 / 64, o_t, MUL, ADD)
            tt(dve, tiles(T_), o_t, o_t, MUL)
            tt(dve, V_, V_, banks(2, 2), MUL)
            dve.drain().then_inc(met, 1)
            dve.wait_ge(met, at.step("squares of the centred output"))
            dve.drain().then_inc(met, 1)
            dve.wait_ge(met, at.step("variances"))
            dve.drain().then_inc(met, 1)
            dve.wait_ge(met, at.step("root of the variance"))
            for t in range(RT):
                cs = slice(t * S, (t + 1) * S)
                stt(dve, o_t[:, t, :], o_t[:, t, :], sm("ln_w", t, t + 1), work[:, cs], MUL, MUL)
                stt(dve, o_t[:, t, :], o_t[:, t, :], sm("ln_b", t, t + 1), V_[:, cs], ADD, ADD)
            tt(dve, o_t, o_t, tiles(G_), MUL)
            dve.drain().then_inc(met, 1)
            dve.wait_ge(met, at.step("rwkv output"))

        def dve_s5(dve, at):
            lre, lim = sm("lam_re"), sm("lam_im")
            dve.drain().then_inc(met, 1)
            dve.wait_ge(met, at.step("dt"))
            tt(dve, s5t(1), lre, s5t(0), MUL)
            tt(dve, s5t(2), lim, s5t(0), MUL)
            ts(dve, s5t(3), s5t(2), 1.0 / (2 * math.pi), 12582912.0, MUL, ADD)
            ts(dve, s5t(3), s5t(3), -12582912.0, None, ADD)
            stt(dve, s5t(2), s5t(3), -6.28125, s5t(2), MUL, ADD)
            stt(dve, s5t(2), s5t(3), -(2 * math.pi - 6.28125), s5t(2), MUL, ADD)
            ts(dve, s5t(2), s5t(2), 3.1415925, -3.1415925, ALU.min, ALU.max)
            ts(dve, s5t(3), s5t(2), -1.0, None, MUL)
            tt(dve, s5t(3), s5t(3), s5t(2), ALU.max)
            ts(dve, s5t(3), s5t(3), -1.0, math.pi / 2, MUL, ADD)
            dve.drain().then_inc(met, 1)
            dve.wait_ge(met, at.step("angles"))
            dve.drain().then_inc(met, 1)
            dve.wait_ge(met, at.step("sines"))
            mag, sn, cs_ = s5t(1), s5t(2), s5t(3)
            br, bi, den, t1, cr, ci = (s5t(i) for i in range(4, 10))
            tt(dve, br, mag, cs_, MUL)
            tt(dve, bi, mag, sn, MUL)
            ts(dve, br, br, -1.0, None, ADD)
            tt(dve, den, lre, lre, MUL)
            tt(dve, t1, lim, lim, MUL)
            tt(dve, den, den, t1, ADD)
            nc.vector.reciprocal(den, den)
            dve.drain()

            def products(o, a, b, c, d, op, t):
                nc.vector.tensor_tensor(o, a, b, MUL)
                tt(dve, t, c, d, MUL)
                tt(dve, o, o, t, op)

            products(cr, br, lre, bi, lim, ADD, t1)
            products(ci, bi, lre, br, lim, SUB, t1)
            tt(dve, cr, cr, den, MUL)
            tt(dve, ci, ci, den, MUL)
            cshape = [P, SP_, 32]
            w1 = tiles(slot(17)[:, 0:512], 32)
            products(c_re, tiles(sm("c_re"), 32), scalars(cr, cshape), tiles(sm("c_im"), 32), scalars(ci, cshape), SUB, w1)
            products(c_im, tiles(sm("c_re"), 32), scalars(ci, cshape), tiles(sm("c_im"), 32), scalars(cr, cshape), ADD, w1)
            ts(dve, c_im, c_im, -1.0)
            nc.vector.memset(e_re[:, :, 0:1], 1.0)
            nc.vector.memset(e_im[:, :, 0:1], 0.0)
            pr, pi, p2 = s5t(10), s5t(11), s5t(12)
            nc.vector.tensor_copy(pr, cs_)
            nc.vector.tensor_copy(pi, sn)
            dve.drain()
            m = 1
            while m < S:
                shape = [P, SP_, m]
                lo, hi = slice(0, m), slice(m, 2 * m)
                t = slot(8, 2).rearrange("p (j n) -> p j n", n=128)[:, :, 0:m]
                products(e_re[:, :, hi], e_re[:, :, lo], scalars(pr, shape), e_im[:, :, lo], scalars(pi, shape), SUB, t)
                products(e_im[:, :, hi], e_re[:, :, lo], scalars(pi, shape), e_im[:, :, lo], scalars(pr, shape), ADD, t)
                products(p2, pr, pr, pi, pi, SUB, t1)
                stt(dve, pi, pi, 2.0, pr, MUL, MUL)
                nc.vector.tensor_copy(pr, p2)
                dve.drain()
                m *= 2
            for grp in range(4):
                er, ei = e_re[:, 4 * grp:4 * grp + 4, :], e_im[:, 4 * grp:4 * grp + 4, :]
                vr, vi = ps[:, 0:4, 0:S], ps[:, 0:4, S:2 * S]
                xr, xi, zr, zi, yr, yi, t = s5b[:7]
                dve.drain().then_inc(met, 1)
                dve.wait_ge(met, at.step("B u"))
                products(zr, er, vr, ei, vi, ADD, t)
                products(zi, er, vi, ei, vr, SUB, t)
                for q in range(4):
                    a = mag[:, 4 * grp + q:4 * grp + q + 1].to_broadcast([P, S])
                    nc.vector.tensor_tensor_scan(yr[:, q, :], a, zr[:, q, :], 0.0, MUL, ADD)
                    nc.vector.tensor_tensor_scan(yi[:, q, :], a, zi[:, q, :], 0.0, MUL, ADD)
                dve.drain()
                products(xr, er, yr, ei, yi, SUB, t)
                products(xi, er, yi, ei, yr, ADD, t)
                dve.drain().then_inc(met, 1)
                dve.wait_ge(met, at.step("states"))
            dve.drain().then_inc(met, 1)
            dve.wait_ge(met, at.step("C x"))
            for t in range(4):
                stt(dve, u_t[:, t, :], u_t[:, t, :], sm("s5_d", t, t + 1), ps[:, 4 + t, 0:S], MUL, ADD)
            dve.drain().then_inc(met, 1)
            dve.wait_ge(met, at.step("y"))
            dve.drain().then_inc(met, 1)
            dve.wait_ge(met, at.step("gelu"))
            at.add("chunk")
            dve.drain().then_inc(met, 1)
            dve.wait_ge(met, at.step("glu product"))
            dve.drain().then_inc(met, 1)
            dve.wait_ge(met, at.step("glu gate"))
            tt(dve, u_t, u_t, s5b[0], MUL)
            dve.drain().then_inc(met, 1)
            dve.wait_ge(met, at.step("s5 output"))

        def dve_diff(dve, at):
            leave_evac(dve, at, 8)
            leave_evac(dve, at, 4)
            dve_norm(dve, at, aq, aq, lambda t: sm("g_dq"), 8, 1)
            dve_norm(dve, at, ak, ak, lambda t: sm("g_dk"), 8, 1,
                     after=lambda: nc.vector.tensor_tensor(tiny[:, 0:2], sm("lam", 0, 2), sm("lam", 2, 4), MUL))
            dve.drain().then_inc(met, 1)
            dve.wait_ge(met, at.step("sums for lambda"))
            dve.drain().then_inc(met, 1)
            dve.wait_ge(met, at.step("exponentials for lambda"))
            neg_lam = tiny[:, 4:5]
            tt(dve, neg_lam, tiny[:, 3:4], tiny[:, 2:3], SUB)
            ts(dve, neg_lam, neg_lam, -LAMBDA_INIT, None, ADD)
            ts(dve, tiny[:, 5:6], sm("g_sub"), 1.0 - LAMBDA_INIT)
            for qb in range(2):
                for hd in range(8):
                    nc.vector.scalar_tensor_tensor(bias[:, hd, :], cst("dist", qb * S, (qb + 1) * S), -2.0 ** -(hd + 1),
                                                   cst("hidden", qb * S, (qb + 1) * S), MUL, ADD)
                dve.drain()
                for half in range(2):
                    def biased():
                        for hl in range(4):
                            for c in range(2):
                                u = 4 * (hl // 2) + 2 * c + hl % 2
                                nc.vector.scalar_tensor_tensor(ae[:, u, :], tiles(banks(0, 4))[:, u, :], 64 ** -0.5,
                                                               bias[:, 4 * half + hl, :], MUL, ADD)
                        dve.drain()

                    dve_softmax(dve, at, biased, neg_lam)
                    dve.drain().then_inc(met, 1)
                    dve.wait_ge(met, at.step("products with v"))
                    nc.vector.tensor_copy(mix[:, 4 * half:4 * half + 4, qb * P:(qb + 1) * P], tiles(banks(0), P))
                    dve.drain().then_inc(met, 1)
                    dve.wait_ge(met, at.step("attention output"))
            dve_norm(dve, at, mix, mix, lambda t: tiny[:, 5:6], 8, 1)
            dve_residual(dve, at)

        def dve_second_mixer(dve, at):
            for n in (2, 1, 1, 1, 3):
                leave_evac(dve, at, n)

            def gating_squares():
                tt(dve, sv_sq, sv_tok, sv_tok, MUL)
                nc.vector.reduce_sum(tiny[:, 6:8], sv_sq, AX)

            def gating_normed():
                tt(dve, sv_tok, sv_tok, scalars(tiny[:, 6:8], [P, 2, 256]), MUL)

            dve_norm(dve, at, qk, qk, lambda t: lay("gq") if t < 4 else lay("gk"), 5, 1,
                     before=gating_squares, after=gating_normed)
            dve.drain().then_inc(met, 1)
            dve.wait_ge(met, at.step("turned features, gating products"))
            pass_loop(dve, at)
            four = [P, 4, S]
            two = [P, 2, S]
            tt(dve, rot[:, 0:4, :], tiles(banks(4, 2)), repeated(cst("sin"), four), MUL)
            tt(dve, rot[:, 4:6, :], tiles(banks(7)), repeated(cst("sin"), two), MUL)
            tt(dve, q_r[:, 0:4, :], qk[:, 0:4, :], repeated(cst("cos"), four), MUL)
            tt(dve, q_r[:, 4:6, :], tiles(banks(6)), repeated(cst("cos"), two), MUL)
            tt(dve, q_r[:, 0:6, :], q_r[:, 0:6, :], rot[:, 0:6, :], ADD)
            for t in range(2):
                o = mix[:, 4 + t, :]
                stt(dve, tiles(o, P), tiles(ps[:, t, 0:S], P), lay("gsg", t, t + 1),
                    repeated(lay("sgb", t * P, (t + 1) * P), [P, 2, P]), MUL, ADD)
            tt(dve, mix[:, 4:6, :], mix[:, 4:6, :], su, MUL)
            tt(dve, cc, cc, cx, MUL)
            dve_conv(dve, c_out, cc, lambda tap, i: lay("cw", 2 * tap + i, 2 * tap + i + 1))
            tt(dve, mix[:, 6:8, :], c_out, cb, MUL)
            dve.drain().then_inc(met, 1)
            dve.wait_ge(met, at.step("q and k, gating and convolution outputs"))
            pass_loop(dve, at)
            for qb in range(2):
                dve_softmax(dve, at)
                dve.drain().then_inc(met, 1)
                dve.wait_ge(met, at.step("products with v"))
                pass_loop(dve, at)
                nc.vector.tensor_copy(mix[:, 0:4, qb * P:(qb + 1) * P], tiles(banks(0), P))
                dve.drain().then_inc(met, 1)
                dve.wait_ge(met, at.step("attention output"))
                pass_loop(dve, at)
            dve_residual(dve, at)

        def dve_moe_gates(dve, at):
            shape = [P, 2, NE]

            def area(i):
                return tiles(tiny[:, 128 + 16 * i:144 + 16 * i], NE)

            logit, chosen, first, second = area(0), area(1), area(2), area(3)
            top, mark = tiny[:, 96:98], tiny[:, 98:100]
            diff, p1, p2 = tiny[:, 100:102], tiny[:, 102:104], tiny[:, 104:106]

            def take_largest(o, largest):
                nc.vector.reduce_max(largest, logit, AX)
                dve.drain()
                tt(dve, chosen, logit, scalars(largest, shape), ALU.is_ge)
                tt(dve, chosen, chosen, repeated(cst("rev"), shape), MUL)
                nc.vector.reduce_max(mark, chosen, AX)
                dve.drain()
                tt(dve, o, chosen, scalars(mark, shape), ALU.is_ge)

            dve.drain().then_inc(met, 1)
            dve.wait_ge(met, at.step("logits"))
            tt(dve, logit, tiles(ps[:, 0, 0:2 * NE], NE), repeated(sm("b_router"), shape), ADD)
            take_largest(first, top)
            stt(dve, logit, first, -BIG, logit, MUL, ADD)
            take_largest(second, diff)
            tt(dve, diff, diff, top, SUB)
            dve.drain().then_inc(met, 1)
            dve.wait_ge(met, at.step("the two largest logits"))
            dve.drain().then_inc(met, 1)
            dve.wait_ge(met, at.step("exponential of their difference"))
            ts(dve, p1, diff, 1.0, None, ADD)
            nc.vector.reciprocal(p1, p1)
            dve.drain()
            tt(dve, p2, p1, diff, MUL)
            tt(dve, first, first, scalars(p1, shape), MUL)
            tt(dve, second, second, scalars(p2, shape), MUL)
            tt(dve, first, first, second, ADD)
            flat16 = tiny[:, 160:176]
            nc.vector.tensor_copy(slot(6, 2).rearrange("p (b n) -> p b n", n=P), scalars(flat16, [P, 16, P]))
            dve.drain().then_inc(met, 1)
            dve.wait_ge(met, at.step("gates by token"))
            dve.drain().then_inc(met, 1)
            dve.wait_ge(met, at.step("gates on every partition"))
            dve.drain().then_inc(met, 1)
            dve.wait_ge(met, at.step("gates copied out"))

        def vector_program(dve, at):
            dve.wait_ge(loaded, 48)
            dve_norm(dve, at, h, hn, lambda t: sm("g_mix", t, t + 1))
            leave_evac(dve, at, 6)
            leave_evac(dve, at, 1)
            leave_evac(dve, at, 2)
            dve_rwkv(dve, at)
            dve_s5(dve, at)
            dve_residual(dve, at)
            dve_memory(dve, at, 0)
            dve_norm(dve, at, h, hn, lambda t: sm("g_ffn", t, t + 1))
            dve_step(dve, at, 0)
            with dve.Fori(0, (FF_STEPS - 1) // 2) as i:
                at.enter(i, {"chunk": 6, "act": 2, "silu": 2})
                dve_step(dve, at, 1)
                dve_step(dve, at, 2)
                at.leave((FF_STEPS - 1) // 2)
            dve_ff_end(dve, at)
            dve_norm(dve, at, h, hn, lambda t: sm("g_mix", KT + t, KT + t + 1))
            dve_diff(dve, at)
            dve_memory(dve, at, 1)
            dve_norm(dve, at, h, hn, lambda t: sm("g_ffn", KT + t, KT + t + 1))
            dve_moe_gates(dve, at)

            def gates(e):
                return gate_bc[:, bass.ds(e, 1), :].to_broadcast([P, 2, S])

            def expert_pair(e, j):
                dve_step(dve, at, 2, gates(e))
                dve_step(dve, at, 3, gates(e))

            dve_step(dve, at, 0, gates(0))
            dve_step(dve, at, 1, gates(0))
            expert_loops(dve, at, {"chunk": 6, "act": 2, "silu": 2}, expert_pair)
            dve_ff_end(dve, at)
            with dve.Fori(0, 2) as layer:
                at.enter(layer, PER_LAYER_SILU)
                nc.vector.tensor_copy(layer_sb[:, :], small_sb[:, bass.ds(layer * LAYER_W + LAYERS_AT, LAYER_W)])
                dve.drain().then_inc(met, 1)
                dve.wait_ge(met, at.step("the layer's small inputs"))
                pass_loop(dve, at)
                dve_norm(dve, at, h, hn, lambda t: lay("g1", t, t + 1))
                dve_second_mixer(dve, at)
                dve_norm(dve, at, h, hn, lambda t: lay("g2", t, t + 1))
                for f in range(FF_STEPS):
                    dve_step(dve, at, f, taps=lambda tap, i: lay("fcw", 44 * tap + i, 44 * tap + i + 1))
                dve_ff_end(dve, at)
                at.leave(2)
            dve.drain().then_inc(result_ready, 1)

        block = ctx.enter_context(nc.Block())
        places = [Place(), Place(), Place()]

        @block.sync
        def _(sp):
            sync_program(sp)

        @block.tensor
        def _(pe):
            tensor_program(pe, places[0])

        @block.scalar
        def _(act):
            scalar_program(act, places[1])

        @block.vector
        def _(dve):
            vector_program(dve, places[2])

        for other in places[1:]:
            for n, (a, b) in enumerate(zip(places[0].labels, other.labels)):
                assert a == b, (n, a, b)
            assert len(places[0].labels) == len(other.labels)


WEIGHTS = ["hy_w_in", "s5_w_glu", "hy_w_out", "xa_w_q", "xa_w_kv", "xa_w_o", "ff_w_gate", "ff_w_up",
           "ff_w_down", "da_w_qkv", "da_w_o", "moe_w_gate", "moe_w_up", "moe_w_down", "w_in_2",
           "w_out_2", "ffn_w_up_2", "ffn_w_down_2"]


def launch_arrays(inputs):
    i = {k: np.asarray(v) for k, v in inputs.items()}
    packed = small_inputs(i)
    names = list(WIDTHS) + [f"{n}_{l}" for l in range(2) for n in LAYER_WIDTHS]
    widths = {**WIDTHS, **{f"{n}_{l}": w for l in range(2) for n, w in LAYER_WIDTHS.items()}}
    for n in names:
        assert packed[n].shape == (P, widths[n]), (n, packed[n].shape)
    arrays = {
        "small": np.ascontiguousarray(np.concatenate([packed[n] for n in names], 1)),
        "const": np.concatenate([np.asarray(v, np.float32) for v in shape_constants().values()], 1),
        "x_t": np.ascontiguousarray(i["x"][0].T),
        "mem_t": np.ascontiguousarray(i["mem"][0].T),
    }
    for n in WEIGHTS:
        arrays[n] = np.ascontiguousarray(i[n])
    return arrays


def kernel(**inputs):
    import concourse.bacc as bacc
    from concourse.bass_utils import run_bass_kernel_spmd

    arrays = launch_arrays(inputs)
    nc = bacc.Bacc("TRN2", target_bir_lowering=False, num_devices=1)
    aps = {n: nc.dram_tensor(n, a.shape, F32, kind="ExternalInput").ap() for n, a in arrays.items()}
    out_t = nc.dram_tensor("out_t", (D, S), F32, kind="ExternalOutput").ap()
    build(nc, aps["small"], aps["const"], aps["x_t"], aps["mem_t"], {n: aps[n] for n in WEIGHTS}, out_t)
    result = run_bass_kernel_spmd(nc, [arrays], core_ids=[0])
    return np.ascontiguousarray(result.results[0]["out_t"].T)[None]
```

```python
import math
from contextlib import ExitStack

import numpy as np
import concourse.bass as bass
from concourse import mybir

F32 = mybir.dt.float32
F32R = mybir.dt.float32r
ALU = mybir.AluOpType
ACT = mybir.ActivationFunctionType
AX = mybir.AxisListType.X

D, S, M, P = 1024, 256, 256, 128
KT = D // P
CH = 256
RW = 512
RT = RW // P
ZT = 15
C = 64
NJ = RT * (S // C)
SP_ = 16
FF, FFE, NE = 2816, 3584, 8
RING, HALVES = 3, 4
LEVELS = (2, 4, 8, 16, 32)
LAMBDA_INIT = 0.8 - 0.6 * math.exp(-0.3)
BIG = 1e30



def tiles_of(v):
    v = v.reshape(-1, v.shape[-1] // P, P)
    return v.transpose(2, 0, 1).reshape(P, -1)


def twice(v):
    return np.concatenate([v, v]).reshape(P, 1)


def padded(v, rows):
    out = np.zeros((rows,) + v.shape[1:], v.dtype)
    out[:v.shape[0]] = v
    return out


def states(v):
    return v.reshape(SP_, P).T


def s5_b(b):
    out = np.zeros((4, 2, 16, 4, 2, 64), b.dtype)
    v = b.reshape(4, 4, 2, 64, 16)
    for g in range(2):
        out[:, g, :, :, g, :] = v[:, :, g].transpose(1, 3, 0, 2)
    return out.reshape(P, 4 * P)


def s5_c(c):
    out = np.zeros((2, 64, SP_, 2, 16), c.dtype)
    v = c.reshape(SP_, 2, 16, 64)
    for g in range(2):
        out[g, :, :, g, :] = v[:, g].transpose(2, 0, 1)
    return out.reshape(P, SP_ * 32)


def small_inputs(i):
    a = {
        "g_mix": tiles_of(i["norm_mix"]), "g_xattn": tiles_of(i["norm_xattn"]),
        "g_mem": tiles_of(i["norm_mem"]), "g_ffn": tiles_of(i["norm_ffn"]),
        "g_xq": tiles_of(i["xa_q_gain"]), "g_xk": tiles_of(i["xa_k_gain"]),
        "mu": tiles_of(padded(i["rw_mu"][0], ZT * P)),
        "w0": tiles_of(i["rw_w0"]), "a0": tiles_of(i["rw_a0"]), "k_k": tiles_of(i["rw_k_k"]),
        "k_a": tiles_of(i["rw_k_a"]), "r_k": tiles_of(i["rw_r_k"].reshape(RW)),
        "ln_w": tiles_of(i["rw_ln_w"]), "ln_b": tiles_of(i["rw_ln_b"]),
        "lora": np.concatenate([i["rw_w_up"][0], i["rw_a_up"][0]]),
        "g_up": i["rw_g_up"][0][:P], "g_up2": padded(i["rw_g_up"][0][P:], P),
        "lam_re": states(i["s5_lam_re"][0]), "lam_im": states(i["s5_lam_im"][0]),
        "log_dt": states(np.broadcast_to(i["s5_log_dt"][0][:, None], (32, 64))),
        "b_re": s5_b(i["s5_b_re"][0]), "b_im": s5_b(i["s5_b_im"][0]),
        "c_re": s5_c(i["s5_c_re"][0]), "c_im": s5_c(i["s5_c_im"][0]),
        "s5_d": tiles_of(i["s5_d"]), "b_glu": tiles_of(i["s5_b_glu"]),
        "g_dq": twice(i["da_q_gain"][0]), "g_dk": twice(i["da_k_gain"][0]),
        "g_sub": i["da_sub_gain"][0].reshape(P, 1),
        "lam": padded(np.stack([i["da_lam_q1"][0], i["da_lam_q2"][0],
                                i["da_lam_k1"][0], i["da_lam_k2"][0]], 1), P),
        "b_router": np.broadcast_to(i["moe_b_router"], (P, NE)),
        "w_router": i["moe_w_router"][0].reshape(KT, P, NE).transpose(1, 0, 2).reshape(P, KT * NE),
    }
    for l in range(2):
        a |= {
            f"g1_{l}": tiles_of(i["norm1_g_2"][l]), f"g2_{l}": tiles_of(i["norm2_g_2"][l]),
            f"gq_{l}": twice(i["q_norm_g_2"][l]), f"gk_{l}": twice(i["k_norm_g_2"][l]),
            f"gsg_{l}": tiles_of(i["sg_norm_g_2"][l]),
            f"sgb_{l}": np.broadcast_to(i["sg_b_2"][l].reshape(2, 2, 1, P), (2, 2, 64, P))
            .transpose(1, 2, 0, 3).reshape(P, 2 * P),
            f"sgw_{l}": i["sg_w_2"][l].transpose(2, 0, 1).reshape(P, 4 * P),
            f"cw_{l}": tiles_of(i["conv_w_2"][l]), f"fcw_{l}": tiles_of(i["ffn_conv_w_2"][l]),
        }
    return a


WIDTHS = {
    "g_mix": 16, "g_xattn": 16, "g_mem": 16, "g_ffn": 16, "g_xq": 4, "g_xk": 4, "mu": ZT,
    "w0": 4, "a0": 4, "k_k": 4, "k_a": 4, "r_k": 4, "ln_w": 4, "ln_b": 4,
    "lora": RW, "g_up": RW, "g_up2": RW, "lam_re": SP_, "lam_im": SP_, "log_dt": SP_,
    "b_re": 512, "b_im": 512, "c_re": 512, "c_im": 512, "s5_d": 4, "b_glu": 4,
    "g_dq": 1, "g_dk": 1, "g_sub": 1, "lam": 4, "b_router": NE, "w_router": KT * NE,
}
LAYER_WIDTHS = {"g1": 8, "g2": 8, "gq": 1, "gk": 1, "gsg": 2, "sgb": 256, "sgw": 512, "cw": 6,
                "fcw": 3 * 44}
LAYER_W = sum(LAYER_WIDTHS.values())


def offsets(widths):
    at, out = 0, {}
    for name, w in widths.items():
        out[name] = (at, w)
        at += w
    return out, at


SMALL_AT, LAYERS_AT = offsets(WIDTHS)
LAYER_AT, _ = offsets(LAYER_WIDTHS)
SMALL_W = LAYERS_AT + 2 * LAYER_W


def shape_constants():
    f = np.float32
    p = np.arange(P)
    s, t = (p % C)[:, None], np.arange(C)[None, :]
    pos = np.arange(S)
    inv = (f(1) / f(10000.0) ** (np.arange(16, dtype=f) * f(2) / f(32))).astype(f)
    row = (pos // 64).astype(f)[:, None] * inv
    col = (pos % 64).astype(f)[:, None] * inv
    ang = np.concatenate([row, row, col, col], 1).T.astype(f)
    ang = np.concatenate([ang, ang])
    turn = np.zeros((P, P), f)
    for d in range(P):
        turn[(d + 16, d) if d % 32 < 16 else (d - 16, d)] = -1 if d % 32 < 16 else 1
    dup = [(p[:, None] == 64 * g + p[None, :] % 64).astype(f) for g in range(2)]
    q = np.arange(S).reshape(2, P).T[:, :, None]
    k = np.arange(S)[None, None, :]

    def level(m):
        return (s // (2 * m) == t // (2 * m)) & (s // m % 2 == 0) & (t // m % 2 == 1)

    return {
        "ident": np.eye(P), "ones": np.ones((P, P)), "zeros": np.zeros((P, P)),
        "heads": p[:, None] // 64 == p[None, :] // 64,
        "eye64": s == t, "levels": np.concatenate([level(m) for m in LEVELS], 1),
        "level1": level(1), "level1_low": (s // 2 == t // 2) & (s > t),
        "before": s < t, "upto": s <= t,
        "reset": np.broadcast_to(np.arange(S) % C != 0, (P, S)),
        "cos": np.cos(ang), "sin": np.sin(ang), "turn": turn,
        "dup": np.concatenate(dup, 1), "dupturn": np.concatenate([x @ turn for x in dup], 1),
        "dist": np.abs(q - k).reshape(P, 2 * S),
        "hidden": np.where(k // 64 <= q // 64, 0.0, -BIG).reshape(P, 2 * S),
        "rev": np.broadcast_to(NE - np.arange(NE), (P, NE)),
        "eps": np.full((P, 1), 1e-6), "gn_eps": np.full((P, 1), 1e-5 * 64),
    }


CONST_AT, CONST_W = offsets({n: v.shape[1] for n, v in shape_constants().items()})

FF_STEPS, MOE_STEPS = FF // CH, NE * FFE // CH


class Place:

    def __init__(self):
        self.n = {"meet": 0, "chunk": 0, "evac": 0, "act": 0, "silu": 0, "conv": 0,
                  "fetch": 0, "half": 0}
        self.loops = []
        self.labels = []

    def enter(self, turn, per):
        self.loops.append((turn, per, dict(self.n)))

    def leave(self, turns):
        _, per, start = self.loops.pop()
        for k, n in self.n.items():
            assert n == start[k] + per.get(k, 0), (k, n - start[k], per)
            self.n[k] = start[k] + turns * per.get(k, 0)

    def value(self, k, offset=0, scale=1):
        v = (self.n[k] + offset) * scale
        for turn, per, _ in self.loops:
            if per.get(k):
                v = turn * (per[k] * scale) + v
        return v

    def add(self, k, by=1):
        self.n[k] += by

    def step(self, what):
        self.labels.append(what)
        self.add("meet")
        return self.value("meet", scale=3)


def build(nc, small, const, x_t, mem_t, w, out_t):
    ctx = ExitStack()
    with ctx:
        def sb(name, shape, dtype=F32):
            return ctx.enter_context(nc.sbuf_tensor(name, shape, dtype))

        def sem(name):
            return ctx.enter_context(nc.semaphore(name))

        ring = sb("ring", [P, RING, KT * 288])
        w_hi = sb("w_hi", [P, HALVES, 1024], F32R)
        w_lo = sb("w_lo", [P, HALVES, 1024], F32R)
        x_hi = sb("x_hi", [P, KT, S], F32R)
        x_lo = sb("x_lo", [P, KT, S], F32R)
        act_hi = sb("act_hi", [P, 2, 2, S], F32R)
        act_lo = sb("act_lo", [P, 2, 2, S], F32R)
        small_sb = sb("small_sb", [P, SMALL_W])
        const_sb = sb("const_sb", [P, CONST_W])
        layer_sb = sb("layer_sb", [P, LAYER_W])
        h = sb("h", [P, KT, S])
        mix = sb("mix", [P, KT, S])
        rstd = sb("rstd", [P, 2048])
        tiny = sb("tiny", [P, 272])
        arena = sb("arena", [P, 18, 1024])
        ps = ctx.enter_context(nc.psum_tensor("ps", [P, 8, 512], F32))

        def sm(name, a=0, b=None):
            at, width = SMALL_AT[name]
            return small_sb[:, at + a:at + (width if b is None else b)]

        def lay(name, a=0, b=None):
            at, width = LAYER_AT[name]
            return layer_sb[:, at + a:at + (width if b is None else b)]

        def cst(name, a=0, b=None):
            at, width = CONST_AT[name]
            return const_sb[:, at + a:at + (width if b is None else b)]

        def slot(i, n=1):
            return arena[:, i:i + n, :].rearrange("p a b -> p (a b)")

        def tiles(ap, n=S):
            return ap.rearrange("p (t n) -> p t n", n=n)

        def flat(t):
            return t[:, :, :].rearrange("p a b -> p (a b)")

        def banks(b, n=1):
            return ps[:, b:b + n, :].rearrange("p a b -> p (a b)")

        def scalars(ap, shape):
            return ap.unsqueeze(2).to_broadcast(shape)

        def repeated(ap, shape):
            return ap.unsqueeze(1).to_broadcast(shape)

        mem_sb = tiles(slot(0, 2))
        aq, ak = tiles(slot(4, 2)), tiles(slot(6, 2))
        av = slot(8, 2).rearrange("p (b n) -> p b n", b=2)
        ae = tiles(slot(10, 2))
        apt = slot(12, 2).rearrange("p (k u n) -> p k u n", k=2, n=P)
        apt4 = slot(12).rearrange("p (k u n) -> p k u n", k=2, n=P)
        bias = tiles(slot(14, 2))

        def act_buf(f):
            return tiles(slot(4)[:, (f % 2) * 512:(f % 2) * 512 + 512])

        def silu_buf(f):
            return tiles(slot(5)[:, (f % 2) * 512:(f % 2) * 512 + 512])

        def gate_conv(f):
            return tiles(slot(6)[:, (f % 2) * 512:(f % 2) * 512 + 512])

        def up_conv(f):
            return tiles(slot(7)[:, (f % 2) * 512:(f % 2) * 512 + 512])

        gate_rep = slot(6, 2).rearrange("p (b e n) -> p b e n", b=2, n=P)
        gate_bc = tiles(slot(8, 2))

        def by64(ap):
            return ap.rearrange("p (j n) -> p j n", n=C)

        z12, zg = tiles(slot(0, 3)), tiles(slot(3)[:, 0:3 * S])
        shift_tmp = tiles(slot(4, 3))
        R_, K_, V_, G_, A_, LW_, CL_, KK_ = (slot(i) for i in range(8))
        ar = slot(8, 2).rearrange("p (j n) -> p j n", n=2 * C)
        BE_, KA_, T_, TT_, LT_, MT_, NT_, WT_ = (slot(i) for i in range(10, 18))
        beta, kappa, tri, tri_t = by64(BE_), by64(KA_), by64(T_), by64(TT_)
        neg_lt, m_t, neg_nt, w_t = by64(LT_), by64(MT_), by64(NT_), by64(WT_)
        alpha_tok, beta_tok, kappa_tok, v_tok = by64(K_), by64(BE_), by64(KA_), by64(rstd[:, 0:1024])
        xbuf, uv, tat, ubuf = by64(A_), by64(LW_), by64(CL_), by64(KK_)
        o_t = mix[:, 0:RT, :]
        work = rstd[:, 0:1024]
        state = by64(rstd[:, 1024:1024 + RT * C])
        chunk_decay = tiny[:, 48:64]

        u_t = mix[:, RT:2 * RT, :]
        e_re, e_im = tiles(slot(0, 4)), tiles(slot(4, 4))
        s5b = [tiles(slot(8 + i)) for i in range(8)]
        c_re, c_im = tiles(slot(16)[:, 0:512], 32), tiles(slot(16)[:, 512:1024], 32)

        def s5t(i):
            return tiny[:, 64 + 16 * i:80 + 16 * i]

        qk = tiles(slot(0, 2))
        q_r = tiles(slot(2, 2))
        v_tok2 = tiles(slot(8)[:, 0:256], P)
        sv_tok = tiles(slot(4)[:, 0:512])
        sv_sq = tiles(slot(4)[:, 512:1024])
        su, cb = tiles(slot(5)[:, 0:512]), tiles(slot(5)[:, 512:1024])
        cc, cx = tiles(slot(6)[:, 0:512]), tiles(slot(6)[:, 512:1024])
        c_out = tiles(slot(7)[:, 0:512])
        rot = tiles(slot(14, 2))

        loaded = sem("loaded")
        mem_loaded = sem("mem_loaded")
        arrived = [sem(f"arrived{i}") for i in range(RING)]
        hi_ready = sem("hi_ready")
        lo_ready = sem("lo_ready")
        half_used = sem("half_used")
        chunk_used = sem("chunk_used")
        evacuated = sem("evacuated")
        met = sem("met")
        passed = sem("passed")
        silu_done = sem("silu_done")
        conv_done = sem("conv_done")
        act_ready = sem("act_ready")
        result_ready = sem("result_ready")
        stored = sem("stored")


        def pass_loop(eng, at):
            if at.loops:
                eng.sem_inc(passed, 1)

        SECOND = 14 + 16 + 3 * FF_STEPS + 16 + 16 + 3 * MOE_STEPS

        def chunk_place(at, key="chunk"):
            n = at.n[key]
            value = 16 * (n // RING + 1)
            for turn, per, _ in at.loops:
                assert per.get(key, 0) % RING == 0
                if per.get(key):
                    value = turn * (16 * per[key] // RING) + value
            return n % RING, arrived[n % RING], value

        def half_slot(at, half):
            for _, per, _ in at.loops:
                assert per.get("half", 0) % 2 == 0
            return (2 * at.n["half"] + half) % HALVES

        def stream(sp, at, src, width=CH, rows=KT):
            n = at.n["chunk"]
            s_, arr, _ = chunk_place(at)
            if n >= RING:
                sp.wait_ge(chunk_used, at.value("chunk", 1 - RING))
            dst = ring[:, s_, 0:rows * width].rearrange("p (k n) -> p k n", n=width)
            sp.dma_start(dst, src.rearrange("(k p) n -> p k n", p=P)).then_inc(arr, 16)
            at.add("chunk")

        def stream_columns(sp, at, src, first, last):
            for c in range(first, last, CH):
                stream(sp, at, src[:, c:c + CH])

        def stream_memory(sp, at, l):
            stream_columns(sp, at, w["xa_w_q"][l], 0, D)
            stream_columns(sp, at, w["xa_w_kv"][l], 0, 2 * D)
            stream_columns(sp, at, w["xa_w_o"][l], 0, D)

        def stream_ff(sp, at, gate, up, down):
            for f in range(FF_STEPS):
                stream(sp, at, gate[:, f * CH:(f + 1) * CH])
                stream(sp, at, up[:, f * CH:(f + 1) * CH])
                if f:
                    stream(sp, at, down[(f - 1) * CH:f * CH, :], D, 2)
            stream(sp, at, down[(FF_STEPS - 1) * CH:FF_STEPS * CH, :], D, 2)

        EXPERT_PAIRS = FFE // CH // 2

        def expert_loops(eng, at, per_pair, body, last=EXPERT_PAIRS):
            parts = ((0, 1, 1, EXPERT_PAIRS), (1, NE - 1, 0, EXPERT_PAIRS), (NE - 1, NE, 0, last))
            for e0, e1, j0, j1 in parts:
                n = j1 - j0
                with eng.Fori(e0, e1) as e:
                    turn = e - e0 if e0 else e
                    at.enter(turn, {k: n * v for k, v in per_pair.items()})
                    with eng.Fori(j0, j1) as j:
                        at.enter(j - j0 if j0 else j, per_pair)
                        body(e, j)
                        at.leave(n)
                    at.leave(e1 - e0)

        def stream_moe(sp, at):
            gate, up = w["moe_w_gate"][0], w["moe_w_up"][0]
            down = w["moe_w_down"][0].rearrange("e f d -> (e f) d")

            def gate_up(e, f):
                for m in (gate, up):
                    src = m[bass.ds(e, 1), :, bass.ds(f * CH, CH)]
                    stream(sp, at, src.rearrange("e k n -> (e k) n"))

            def down_rows(row):
                stream(sp, at, down[bass.ds(row, CH), :], D, 2)

            def pair(e, j):
                gate_up(e, j * 2)
                down_rows(e * FFE + j * (2 * CH) + -CH)
                gate_up(e, j * 2 + 1)
                down_rows(e * FFE + j * (2 * CH))

            gate_up(0, 0)
            gate_up(0, 1)
            down_rows(0)
            expert_loops(sp, at, {"chunk": 6}, pair)
            down_rows(NE * FFE - CH)

        def sync_program(sp):
            at = Place()
            sp.dma_start(const_sb[:, :], const).then_inc(loaded, 16)
            sp.dma_start(small_sb[:, :], small).then_inc(loaded, 16)
            sp.dma_start(h[:, :, :], x_t.rearrange("(k p) n -> p k n", p=P)).then_inc(loaded, 16)
            hy = w["hy_w_in"][0]
            stream_columns(sp, at, hy, 0, 3 * RW)
            stream(sp, at, hy[:, 3 * RW:3 * RW + 288], 288)
            stream_columns(sp, at, hy, 3 * RW + 288, 4 * RW + 288)
            stream(sp, at, w["s5_w_glu"][0], RW, 4)
            stream_columns(sp, at, w["hy_w_out"][0], 0, D)
            stream_memory(sp, at, 0)
            stream_ff(sp, at, w["ff_w_gate"][0], w["ff_w_up"][0], w["ff_w_down"][0])
            stream_columns(sp, at, w["da_w_qkv"][0], 0, 3 * D)
            stream_columns(sp, at, w["da_w_o"][0], 0, D)
            stream_memory(sp, at, 1)
            stream_moe(sp, at)
            assert at.n["chunk"] == SECOND, (at.n["chunk"], SECOND)
            for l in range(2):
                stream_columns(sp, at, w["w_in_2"][l], 0, 2 * D)
                stream_columns(sp, at, w["w_out_2"][l], 0, D)
                up = w["ffn_w_up_2"][l]
                stream_ff(sp, at, up[:, 0:FF], up[:, FF:2 * FF], w["ffn_w_down_2"][l])
            sp.wait_ge(result_ready, 1)
            sp.dma_start(out_t.rearrange("(k p) n -> p k n", p=P), h[:, :, :]).then_inc(stored, 16)
            sp.wait_ge(stored, 16)

        mm = nc.tensor.matmul

        def next_chunk(pe, at, k_tiles=KT, width=CH):
            s_, arr, value = chunk_place(at)
            pe.wait_ge(arr, value)
            return ring[:, s_, 0:k_tiles * width].rearrange("p (k n) -> p k n", n=width)

        def used(last, at):
            last.then_inc(chunk_used, 1)
            at.add("chunk")

        def next_half(pe, at, half, width=CH):
            pe.wait_ge(lo_ready, at.value("half", scale=2) + (half + 1))
            i = half_slot(at, half)
            return [w_[:, i, :].rearrange("p (k n) -> p k n", n=width) for w_ in (w_hi, w_lo)]

        def half_done(last, at, half):
            if half == 0:
                last.then_inc(half_used, 1)
            else:
                used(last, at)
                at.add("half")

        def three(o, lhs, rhs, start=False, stop=False):
            mm(o, lhs[0], rhs[0], start=start, stop=False)
            mm(o, lhs[0], rhs[1], start=False, stop=False)
            return mm(o, lhs[1], rhs[0], start=False, stop=stop)

        def pe_project(pe, at, n, token=False):
            for c in range(n):
                if c >= 4:
                    pe.wait_ge(evacuated, at.value("evac", -3))
                for half in range(2):
                    ws = next_half(pe, at, half)
                    for i in range(2):
                        o = ps[:, c % 4, i * S:(i + 1) * S]
                        cs = slice(i * P, (i + 1) * P)
                        for k in range(4):
                            xk = 4 * half + k
                            first, last_ = half == 0 and i == 0 and k == 0, half == 1 and i == 1 and k == 3
                            if token:
                                last = three(o, (x_hi[:, xk, cs], x_lo[:, xk, cs]), (ws[0][:, k, :], ws[1][:, k, :]),
                                             first, last_)
                            else:
                                last = three(o, (ws[0][:, k, cs], ws[1][:, k, cs]), (x_hi[:, xk, :], x_lo[:, xk, :]),
                                             first, last_)
                    half_done(last, at, half)
                at.add("evac")
            pe.drain().then_inc(met, 1)
            pe.wait_ge(met, at.step("projection copied out"))
            pass_loop(pe, at)

        def pe_project_raw(pe, at, width, token_from):
            wt = next_chunk(pe, at, width=width)
            parts = []
            for t in range(-(-token_from // P)):
                cols = slice(t * P, min(token_from, t * P + P))
                parts.append((ps[0:cols.stop - cols.start, t // 2, (t % 2) * S:(t % 2) * S + S],
                              [(wt[:, k, cols], mix[:, k, :]) for k in range(KT)]))
            if token_from < width:
                for b in range(2):
                    parts.append((ps[:, 0, S + b * P:S + (b + 1) * P],
                                  [(mix[:, k, b * P:(b + 1) * P], wt[:, k, token_from:width]) for k in range(KT)]))
            for o, pairs in parts:
                for k, (lhs, rhs) in enumerate(pairs):
                    last = mm(o, lhs, rhs, start=k == 0, stop=k == KT - 1)
            used(last, at)
            at.add("evac")
            pe.drain().then_inc(met, 1)
            pe.wait_ge(met, at.step("projection copied out"))
            pass_loop(pe, at)

        def pe_norm(pe, at, sq=mix, table="ones", groups=1, per=KT):
            pe.drain().then_inc(met, 1)
            pe.wait_ge(met, at.step("squares"))
            pass_loop(pe, at)
            for g in range(groups):
                for k in range(per):
                    mm(banks(4, 4)[:, g * S:(g + 1) * S], cst(table), sq[:, g * per + k, :],
                       start=k == 0, stop=k == per - 1)
            pe.drain().then_inc(met, 1)
            pe.wait_ge(met, at.step("sums of squares"))
            pass_loop(pe, at)
            pe.drain().then_inc(met, 1)
            pe.wait_ge(met, at.step("roots"))
            pass_loop(pe, at)
            pe.drain().then_inc(met, 1)
            pe.wait_ge(met, at.step("normed"))
            pass_loop(pe, at)

        def counted_loop(eng, at, turns, per, body):
            if turns == 1:
                body()
                return
            with eng.Fori(0, turns) as i:
                at.enter(i, per)
                body()
                at.leave(turns)

        def ff_steps(eng, at, steps, per_pair, step, looped=True):
            if not looped:
                for f in range(1, steps):
                    step(f)
                return steps - 1
            step(1)
            step(2)
            turns = (steps - 3) // 2
            with eng.Fori(0, turns) as i:
                at.enter(i, per_pair)
                step(3)
                step(4)
                at.leave(turns)
            if steps % 2 == 0:
                step(5)
            return 4 + (steps % 2 == 0)

        def pe_ff(pe, at, steps, looped=True):
            for b in range(4):
                mm(ps[:, 4 + b, :], cst("zeros"), mix[:, 0:2, :], start=True, stop=False)

            def gate_up(f):
                for part in range(2):
                    for half in range(2):
                        ws = next_half(pe, at, half)
                        for i in range(2):
                            cs = slice(i * P, (i + 1) * P)
                            for k in range(4):
                                last = three(ps[:, 2 * (f % 2) + part, i * S:(i + 1) * S],
                                             (ws[0][:, k, cs], ws[1][:, k, cs]),
                                             (x_hi[:, 4 * half + k, :], x_lo[:, 4 * half + k, :]),
                                             half == 0 and i == 0 and k == 0, half == 1 and i == 1 and k == 3)
                        half_done(last, at, half)

            def down(f):
                pe.wait_ge(act_ready, at.value("act", 1))
                for half in range(2):
                    ws = next_half(pe, at, half, D)
                    for o in range(KT):
                        cs = slice(o * P, (o + 1) * P)
                        last = three(banks(4, 4)[:, o * S:(o + 1) * S], (ws[0][:, 0, cs], ws[1][:, 0, cs]),
                                     (act_hi[:, f % 2, half, :], act_lo[:, f % 2, half, :]))
                    half_done(last, at, half)
                at.add("act")

            def step(f):
                gate_up(f)
                down(f - 1)

            gate_up(0)
            f = ff_steps(pe, at, steps, {"chunk": 6, "half": 6, "act": 2}, step, looped)
            down(f)
            for b in range(4):
                mm(ps[:, 4 + b, :], cst("zeros"), mix[:, 0:2, :], start=False, stop=True)
            pe.drain().then_inc(met, 1)
            pe.wait_ge(met, at.step("down products"))
            pass_loop(pe, at)
            pe.drain().then_inc(met, 1)
            pe.wait_ge(met, at.step("residual"))
            pass_loop(pe, at)

        def pe_softmax(pe, at, units, unit=lambda u: u):
            pe.drain().then_inc(met, 1)
            pe.wait_ge(met, at.step("scores"))
            pass_loop(pe, at)
            pe.drain().then_inc(met, 1)
            pe.wait_ge(met, at.step("scores less their maxima"))
            pass_loop(pe, at)
            pe.drain().then_inc(met, 1)
            pe.wait_ge(met, at.step("exponentials"))
            pass_loop(pe, at)
            pe.drain().then_inc(met, 1)
            pe.wait_ge(met, at.step("probabilities"))
            pass_loop(pe, at)
            for kb in range(2):
                for u in range(units):
                    i = kb * units + u
                    nc.tensor.transpose(banks(4, 4)[:, i * P:(i + 1) * P], ae[:, unit(u), kb * P:(kb + 1) * P],
                                        cst("ident"))
            pe.drain().then_inc(met, 1)
            pe.wait_ge(met, at.step("transposes"))
            pass_loop(pe, at)
            pe.drain().then_inc(met, 1)
            pe.wait_ge(met, at.step("transposes copied out"))
            pass_loop(pe, at)

        def pe_memory(pe, at):
            pe_norm(pe, at)
            pe_project(pe, at, 4)
            pe_norm(pe, at, groups=4, per=2)
            pe_norm(pe, at)
            pe_project(pe, at, 4)
            pe_project(pe, at, 4, True)
            pe_norm(pe, at, groups=4, per=2)
            for hd in range(4):
                for qb in range(2):
                    for k in range(2):
                        mm(banks(0, 4)[:, (2 * hd + qb) * M:(2 * hd + qb + 1) * M],
                           aq[:, 2 * hd + k, qb * P:(qb + 1) * P], ak[:, 2 * hd + k, :], start=k == 0, stop=k == 1)
            pe_softmax(pe, at, 8)
            for hd in range(4):
                for j in range(2):
                    for kb in range(2):
                        mm(banks(0, 4)[:, (2 * hd + j) * S:(2 * hd + j + 1) * S],
                           av[:, kb, (2 * hd + j) * P:(2 * hd + j + 1) * P],
                           apt[:, kb, 2 * hd:2 * hd + 2, :].rearrange("p u n -> p (u n)"),
                           start=kb == 0, stop=kb == 1)
            pe.drain().then_inc(met, 1)
            pe.wait_ge(met, at.step("products with v"))
            pe.drain().then_inc(met, 1)
            pe.wait_ge(met, at.step("attention output's high part"))
            pe.drain().then_inc(met, 1)
            pe.wait_ge(met, at.step("attention output"))
            pe_project(pe, at, 4)

        HALF = (slice(0, 64), slice(64, 128))

        def problems(n=NJ):
            for j in range(n):
                yield j, HALF[0]
                yield (j + n // 2) % n, HALF[1]

        def pbank(b):
            return by64(banks(b, 2))

        def pe_rwkv(pe, at):
            pe.drain().then_inc(met, 1)
            pe.wait_ge(met, at.step("inputs shifted"))
            pe.drain().then_inc(met, 1)
            pe.wait_ge(met, at.step("lora inputs, squares of kk"))
            for t in range(RT):
                cs, ts = slice(t * P, (t + 1) * P), slice(t * S, (t + 1) * S)
                mm(banks(0, 2)[:, ts], sm("lora")[0:64, cs], zg[0:64, 0, :], start=True, stop=True)
                mm(banks(2, 2)[:, ts], sm("lora")[64:128, cs], zg[64:128, 0, :], start=True, stop=True)
            for t in range(RT):
                cs, ts = slice(t * P, (t + 1) * P), slice(t * S, (t + 1) * S)
                mm(banks(4, 2)[:, ts], sm("g_up")[:, cs], zg[:, 1, :], start=True, stop=False)
                mm(banks(4, 2)[:, ts], sm("g_up2")[0:32, cs], zg[0:32, 2, :], start=False, stop=True)
                mm(banks(6, 2)[:, ts], cst("heads"), work[:, ts], start=True, stop=True)
            pe.drain().then_inc(met, 1)
            pe.wait_ge(met, at.step("lora products, sums for kk"))
            pe.drain().then_inc(met, 1)
            pe.wait_ge(met, at.step("sigmoids"))
            pe.drain().then_inc(met, 1)
            pe.wait_ge(met, at.step("cumulated decays, root for kk"))
            pe.drain().then_inc(met, 1)
            pe.wait_ge(met, at.step("exponentials, kk"))
            pe.drain().then_inc(met, 1)
            pe.wait_ge(met, at.step("alpha, beta, kappa, rho"))
            for j, hs in problems():
                mm(banks(0, 4)[hs, j * P:(j + 1) * P], beta[hs, j, :], ar[hs, j, :], start=True, stop=True)
            for j, hs in problems():
                mm(banks(4, 4)[hs, j * P:(j + 1) * P], kappa[hs, j, :], ar[hs, j, :], start=True, stop=True)
            pe.drain().then_inc(met, 1)
            pe.wait_ge(met, at.step("beta and kappa by alpha and rho"))
            pe.drain().then_inc(met, 1)
            pe.wait_ge(met, at.step("masked"))
            for j, hs in problems():
                mm(pbank(0)[hs, j, :], ar[hs, j, 0:C], beta[hs, j, :], start=True, stop=True)
            for b, src in ((2, ar), (4, beta), (6, kappa)):
                for j, hs in problems():
                    mm(pbank(b)[hs, j, :], src[hs, j, 0:C], cst("eye64")[hs, :], start=True, stop=True)
            pe.drain().then_inc(met, 1)
            pe.wait_ge(met, at.step("alpha by beta, token-major forms"))
            pe.drain().then_inc(met, 1)
            pe.wait_ge(met, at.step("inverse of blocks of two"))
            for j, hs in problems():
                mm(pbank(0)[hs, j, :], by64(V_)[hs, j, :], cst("eye64")[hs, :], start=True, stop=True)
            pe.drain().then_inc(met, 1)
            pe.wait_ge(met, at.step("v token-major"))

            def level():
                pe.drain().then_inc(met, 1)
                pe.wait_ge(met, at.step("blocks below the diagonal"))
                pass_loop(pe, at)
                for j, hs in problems():
                    mm(pbank(2)[hs, j, :], ubuf[hs, j, :], tri[hs, j, :], start=True, stop=True)
                pe.drain().then_inc(met, 1)
                pe.wait_ge(met, at.step("blocks times the inverse"))
                pass_loop(pe, at)
                pe.drain().then_inc(met, 1)
                pe.wait_ge(met, at.step("blocks times the inverse copied out"))
                pass_loop(pe, at)
                for j, hs in problems():
                    mm(pbank(4)[hs, j, :], tri_t[hs, j, :], xbuf[hs, j, :], start=True, stop=True)
                for j, hs in problems():
                    mm(pbank(6)[hs, j, :], xbuf[hs, j, :], tri_t[hs, j, :], start=True, stop=True)
                pe.drain().then_inc(met, 1)
                pe.wait_ge(met, at.step("what the level adds"))
                pass_loop(pe, at)

            counted_loop(pe, at, len(LEVELS), {"meet": 4}, level)
            pe.drain().then_inc(met, 1)
            pe.wait_ge(met, at.step("inverse"))
            for j, hs in problems():
                mm(pbank(0)[hs, j, :], m_t[hs, j, :], v_tok[hs, j, :], start=True, stop=True)
            for j, hs in problems():
                mm(pbank(2)[hs, j, :], alpha_tok[hs, j, :], tri_t[hs, j, :], start=True, stop=True)
            pe.drain().then_inc(met, 1)
            pe.wait_ge(met, at.step("M V and T alpha"))
            pe.drain().then_inc(met, 1)
            pe.wait_ge(met, at.step("M V and T alpha copied out"))
            for j, hs in problems():
                mm(pbank(4)[hs, j, :], tri_t[hs, j, :], xbuf[hs, j, :], start=True, stop=True)
            pe.drain().then_inc(met, 1)
            pe.wait_ge(met, at.step("T M V"))
            pe.drain().then_inc(met, 1)
            pe.wait_ge(met, at.step("T M V copied out"))
            for c in range(S // C):
                for hs in HALF:
                    for t in range(RT):
                        mm(pbank(0)[hs, t, :], tat[hs, 4 * t + c, :], state[hs, t, :], start=True, stop=True)
                pe.drain().then_inc(met, 1)
                pe.wait_ge(met, at.step("T alpha by the state"))
                pe.drain().then_inc(met, 1)
                pe.wait_ge(met, at.step("u"))
                for hs in HALF:
                    for t in range(RT):
                        j = 4 * t + c
                        o = pbank(2)[hs, t, :]
                        mm(o, state[hs, t, :], ar[hs, j, C:2 * C], start=True, stop=False)
                        mm(o, ubuf[hs, t, :], neg_nt[hs, j, :], start=False, stop=False)
                        mm(o, v_tok[hs, j, :], w_t[hs, j, :], start=False, stop=True)
                        o = pbank(4)[hs, t, :]
                        mm(o, beta_tok[hs, j, :], ubuf[hs, t, :], start=True, stop=False)
                        mm(o, kappa_tok[hs, j, :], v_tok[hs, j, :], start=False, stop=True)
                pe.drain().then_inc(met, 1)
                pe.wait_ge(met, at.step("the chunk's output and change of state"))
                pe.drain().then_inc(met, 1)
                pe.wait_ge(met, at.step("the chunk's output and state copied out"))
            for t in range(RT):
                ts = slice(t * S, (t + 1) * S)
                mm(banks(0, 2)[:, ts], cst("heads"), o_t[:, t, :], start=True, stop=True)
                mm(banks(2, 2)[:, ts], cst("heads"), R_[:, ts], start=True, stop=True)
            pe.drain().then_inc(met, 1)
            pe.wait_ge(met, at.step("means, bonus"))
            pe.drain().then_inc(met, 1)
            pe.wait_ge(met, at.step("squares of the centred output"))
            for t in range(RT):
                ts = slice(t * S, (t + 1) * S)
                mm(banks(4, 2)[:, ts], cst("heads"), T_[:, ts], start=True, stop=True)
            pe.drain().then_inc(met, 1)
            pe.wait_ge(met, at.step("variances"))
            pe.drain().then_inc(met, 1)
            pe.wait_ge(met, at.step("root of the variance"))
            pe.drain().then_inc(met, 1)
            pe.wait_ge(met, at.step("rwkv output"))

        def pe_s5(pe, at):
            pe.drain().then_inc(met, 1)
            pe.wait_ge(met, at.step("dt"))
            pe.drain().then_inc(met, 1)
            pe.wait_ge(met, at.step("angles"))
            pe.drain().then_inc(met, 1)
            pe.wait_ge(met, at.step("sines"))
            for grp in range(4):
                cs = slice(grp * P, (grp + 1) * P)
                for t in range(4):
                    rows = slice(32 * t, 32 * t + 32)
                    mm(ps[:, t, 0:S], sm("b_re")[rows, cs], u_t[rows, grp, :], start=True, stop=True)
                    mm(ps[:, t, S:2 * S], sm("b_im")[rows, cs], u_t[rows, grp, :], start=True, stop=True)
                pe.drain().then_inc(met, 1)
                pe.wait_ge(met, at.step("B u"))
                pe.drain().then_inc(met, 1)
                pe.wait_ge(met, at.step("states"))
                for t in range(4):
                    o = ps[32 * t:32 * t + 32, 4 + grp, 0:S]
                    mm(o, c_re[:, 4 * grp + t, :], s5b[0][:, t, :], start=True, stop=False)
                    mm(o, c_im[:, 4 * grp + t, :], s5b[1][:, t, :], start=False, stop=True)
            pe.drain().then_inc(met, 1)
            pe.wait_ge(met, at.step("C x"))
            pe.drain().then_inc(met, 1)
            pe.wait_ge(met, at.step("y"))
            pe.drain().then_inc(met, 1)
            pe.wait_ge(met, at.step("gelu"))
            wt = next_chunk(pe, at, 4, RW)
            for t in range(4):
                for k in range(4):
                    last = mm(banks(0, 2)[:, t * S:(t + 1) * S], wt[:, k, t * P:(t + 1) * P], u_t[:, k, :],
                              start=k == 0, stop=k == 3)
            used(last, at)
            pe.drain().then_inc(met, 1)
            pe.wait_ge(met, at.step("glu product"))
            pe.drain().then_inc(met, 1)
            pe.wait_ge(met, at.step("glu gate"))
            pe.drain().then_inc(met, 1)
            pe.wait_ge(met, at.step("s5 output"))

        def pe_diff(pe, at):
            pe_project(pe, at, 8)
            pe_project(pe, at, 4, True)
            pe_norm(pe, at, table="heads", groups=8, per=1)
            pe_norm(pe, at, table="heads", groups=8, per=1)
            mm(ps[:, 4, 0:2], cst("ones"), tiny[:, 0:2], start=True, stop=True)
            pe.drain().then_inc(met, 1)
            pe.wait_ge(met, at.step("sums for lambda"))
            pe.drain().then_inc(met, 1)
            pe.wait_ge(met, at.step("exponentials for lambda"))
            for qb in range(2):
                for half in range(2):
                    for hl in range(4):
                        for c in range(2):
                            mm(ps[:, 2 * (hl // 2) + c, (hl % 2) * S:(hl % 2) * S + S],
                               aq[HALF[c], 4 * half + hl, qb * P:(qb + 1) * P], ak[HALF[c], 4 * half + hl, :],
                               start=True, stop=True)
                    pe_softmax(pe, at, 4, lambda u: 4 * (u // 2) + u % 2)
                    for hl in range(4):
                        hd = 4 * half + hl
                        for kb in range(2):
                            mm(ps[:, 0, hl * P:(hl + 1) * P], av[:, kb, hd * P:(hd + 1) * P], apt4[:, kb, hl, :],
                               start=kb == 0, stop=kb == 1)
                    pe.drain().then_inc(met, 1)
                    pe.wait_ge(met, at.step("products with v"))
                    pe.drain().then_inc(met, 1)
                    pe.wait_ge(met, at.step("attention output"))
            pe_norm(pe, at, ae, groups=8, per=1)
            pe_project(pe, at, 4)

        def unit_of(hd):
            return 4 * (hd // 4) + 2 * (hd % 2) + hd // 2 % 2

        def pe_second_mixer(pe, at):
            pe_project(pe, at, 2)
            pe_project_raw(pe, at, CH, P)
            pe_project(pe, at, 1)
            pe_project(pe, at, 1, True)
            pe_project(pe, at, 3)
            pe_norm(pe, at, table="heads", groups=5, per=1)
            for t in range(4):
                mm(banks(4, 2)[:, t * S:(t + 1) * S], cst("turn"), qk[:, t, :], start=True, stop=True)
            for g in range(2):
                cs = slice(g * S, (g + 1) * S)
                mm(ps[:, 6, cs], cst("dup", g * P, (g + 1) * P), qk[:, 4, :], start=True, stop=True)
                mm(ps[:, 7, cs], cst("dupturn", g * P, (g + 1) * P), qk[:, 4, :], start=True, stop=True)
            for sh in range(4):
                for b in range(2):
                    mm(ps[HALF[sh % 2], sh // 2, b * P:(b + 1) * P], sv_tok[:, b, 64 * sh:64 * sh + 64],
                       lay("sgw", sh * P, (sh + 1) * P), start=True, stop=True)
            pe.drain().then_inc(met, 1)
            pe.wait_ge(met, at.step("turned features, gating products"))
            pass_loop(pe, at)
            pe.drain().then_inc(met, 1)
            pe.wait_ge(met, at.step("q and k, gating and convolution outputs"))
            pass_loop(pe, at)
            for qb in range(2):
                for hd in range(8):
                    u = unit_of(hd)
                    mm(banks(0, 4)[:, u * S:(u + 1) * S], q_r[HALF[hd % 2], hd // 2, qb * P:(qb + 1) * P],
                       q_r[HALF[hd % 2], 4 + hd // 4, :], start=True, stop=True)
                pe_softmax(pe, at, 8)
                for hd in range(8):
                    g = hd // 4
                    for kb in range(2):
                        mm(ps[HALF[hd % 2], 0, (hd // 2) * P:(hd // 2 + 1) * P],
                           v_tok2[:, kb, 64 * g:64 * g + 64], apt[:, kb, unit_of(hd), :],
                           start=kb == 0, stop=kb == 1)
                pe.drain().then_inc(met, 1)
                pe.wait_ge(met, at.step("products with v"))
                pass_loop(pe, at)
                pe.drain().then_inc(met, 1)
                pe.wait_ge(met, at.step("attention output"))
                pass_loop(pe, at)
            pe_project(pe, at, 4)

        def pe_moe_gates(pe, at):
            for b in range(2):
                for k in range(KT):
                    mm(ps[:, 0, b * NE:(b + 1) * NE], mix[:, k, b * P:(b + 1) * P],
                       sm("w_router", k * NE, (k + 1) * NE), start=k == 0, stop=k == KT - 1)
            pe.drain().then_inc(met, 1)
            pe.wait_ge(met, at.step("logits"))
            pe.drain().then_inc(met, 1)
            pe.wait_ge(met, at.step("the two largest logits"))
            pe.drain().then_inc(met, 1)
            pe.wait_ge(met, at.step("exponential of their difference"))
            pe.drain().then_inc(met, 1)
            pe.wait_ge(met, at.step("gates by token"))
            for e in range(NE):
                for b in range(2):
                    mm(banks(0, 4)[:, e * S + b * P:e * S + (b + 1) * P], gate_rep[:, b, e, :], cst("ident"),
                       start=True, stop=True)
            pe.drain().then_inc(met, 1)
            pe.wait_ge(met, at.step("gates on every partition"))
            pe.drain().then_inc(met, 1)
            pe.wait_ge(met, at.step("gates copied out"))

        def tensor_program(pe, at):
            pe.wait_ge(loaded, 48)
            pe_norm(pe, at)
            pe_project(pe, at, 6)
            pe_project_raw(pe, at, 288, 288)
            pe_project(pe, at, 2)
            pe_rwkv(pe, at)
            pe_s5(pe, at)
            pe_project(pe, at, 4)
            pe_memory(pe, at)
            pe_norm(pe, at)
            pe_ff(pe, at, FF_STEPS)
            pe_norm(pe, at)
            pe_diff(pe, at)
            pe_memory(pe, at)
            pe_norm(pe, at)
            pe_moe_gates(pe, at)
            pe_ff(pe, at, MOE_STEPS)
            with pe.Fori(0, 2) as layer:
                at.enter(layer, PER_LAYER)
                pe.drain().then_inc(met, 1)
                pe.wait_ge(met, at.step("the layer's small inputs"))
                pass_loop(pe, at)
                pe_norm(pe, at)
                pe_second_mixer(pe, at)
                pe_norm(pe, at)
                pe_ff(pe, at, FF_STEPS, False)
                at.leave(2)

        PER_LAYER = {"meet": 39, "chunk": 12 + 3 * FF_STEPS, "half": 11 + 3 * FF_STEPS, "evac": 12,
                     "act": FF_STEPS}
        PER_LAYER_SILU = {**PER_LAYER, "fetch": PER_LAYER["chunk"], "silu": FF_STEPS, "conv": FF_STEPS}

        def activate(o, i, func, **kw):
            return nc.scalar.activation(o, i, func, **kw)

        def copy(o, i, **kw):
            return nc.scalar.activation(o, i, ACT.Copy, **kw)

        def evac_one(eng, at, c, copy_out):
            eng.wait_ge(chunk_used, at.value("chunk", 1))
            copy_out(c, banks(c % 4)).then_inc(evacuated, 1)
            at.add("chunk")
            at.add("evac")

        def evac_raw(act, at, copy_out):
            at.add("fetch")
            evac_one(act, at, 0, copy_out)
            act.drain().then_inc(met, 1)
            act.wait_ge(met, at.step("projection copied out"))
            pass_loop(act, at)

        def leave_raw(dve, at):
            for k in ("fetch", "chunk", "evac"):
                at.add(k)
            dve.drain().then_inc(met, 1)
            dve.wait_ge(met, at.step("projection copied out"))
            pass_loop(dve, at)

        def split_hi(act, at, free=False):
            s_, arr, value = chunk_place(at, "fetch")
            act.wait_ge(arr, value)
            for half in range(2):
                if at.n["half"] >= 2 - half and not free:
                    act.wait_ge(half_used, at.value("half", half - 1))
                nc.scalar.activation(w_hi[:, half_slot(at, half), :], ring[:, s_, half * 1024:half * 1024 + 1024],
                                     ACT.Copy).then_inc(hi_ready, 1)
            at.add("fetch")
            at.add("half")

        def split_lo(dve, at):
            s_ = at.n["fetch"] % RING
            for half in range(2):
                i = half_slot(at, half)
                dve.wait_ge(hi_ready, at.value("half", scale=2) + (half + 1))
                nc.vector.tensor_tensor(w_lo[:, i, :], ring[:, s_, half * 1024:half * 1024 + 1024], w_hi[:, i, :],
                                        ALU.subtract).then_inc(lo_ready, 1)
            at.add("fetch")
            at.add("half")

        def act_project(act, at, n, copy_out=None, ahead=0):
            for c in range(n):
                if c >= ahead:
                    split_hi(act, at)
                if copy_out and c:
                    evac_one(act, at, c - 1, copy_out)
            if copy_out:
                evac_one(act, at, n - 1, copy_out)
            else:
                at.add("chunk", n)
                at.add("evac", n)
            act.drain().then_inc(met, 1)
            act.wait_ge(met, at.step("projection copied out"))
            pass_loop(act, at)

        def dve_project(dve, at, n, copy_out=None, ahead=0):
            for c in range(n):
                if c >= ahead:
                    split_lo(dve, at)
                if copy_out and c:
                    evac_one(dve, at, c - 1, copy_out)
            if copy_out:
                evac_one(dve, at, n - 1, copy_out)
            else:
                at.add("chunk", n)
                at.add("evac", n)
            dve.drain().then_inc(met, 1)
            dve.wait_ge(met, at.step("projection copied out"))
            pass_loop(dve, at)

        def act_root(act, o, i, scale, eps):
            activate(o, i, ACT.Ln, scale=scale, bias=eps)
            act.drain()
            activate(o, o, ACT.Exp, scale=-0.5)

        def act_norm(act, at, dim=D, groups=1, more=None, into_x=None):
            if dim == D if into_x is None else into_x:
                split_hi(act, at, True)
                split_hi(act, at, True)
            act.drain().then_inc(met, 1)
            act.wait_ge(met, at.step("squares"))
            pass_loop(act, at)
            act.drain().then_inc(met, 1)
            act.wait_ge(met, at.step("sums of squares"))
            pass_loop(act, at)
            act_root(act, rstd[:, 0:groups * S], banks(4, 4)[:, 0:groups * S], 1.0 / dim, cst("eps"))
            if more:
                more()
            act.drain().then_inc(met, 1)
            act.wait_ge(met, at.step("roots"))
            pass_loop(act, at)
            act.drain().then_inc(met, 1)
            act.wait_ge(met, at.step("normed"))
            pass_loop(act, at)

        def act_softmax(act, at, scale, units):
            act.drain().then_inc(met, 1)
            act.wait_ge(met, at.step("scores"))
            pass_loop(act, at)
            act.drain().then_inc(met, 1)
            act.wait_ge(met, at.step("scores less their maxima"))
            pass_loop(act, at)
            activate(ae, ae, ACT.Exp, scale=scale)
            act.drain().then_inc(met, 1)
            act.wait_ge(met, at.step("exponentials"))
            pass_loop(act, at)
            act.drain().then_inc(met, 1)
            act.wait_ge(met, at.step("probabilities"))
            pass_loop(act, at)
            act.drain().then_inc(met, 1)
            act.wait_ge(met, at.step("transposes"))
            pass_loop(act, at)
            n = 2 * units * P
            copy(slot(12, 2)[:, 0:n], banks(4, 4)[:, 0:n])
            act.drain().then_inc(met, 1)
            act.wait_ge(met, at.step("transposes copied out"))
            pass_loop(act, at)

        def act_memory(act, at):
            act.dma_start(mem_sb, mem_t.rearrange("(k p) n -> p k n", p=P)).then_inc(mem_loaded, 16)
            act_norm(act, at)
            act_project(act, at, 4, lambda c, b: copy(aq[:, 2 * c:2 * c + 2, :], tiles(b)), 2)
            act_norm(act, at, 256, 4)
            act_norm(act, at)
            act_project(act, at, 4, lambda c, b: copy(ak[:, 2 * c:2 * c + 2, :], tiles(b)), 2)
            act_project(act, at, 4, lambda c, b: copy(av[:, :, c * CH:(c + 1) * CH], tiles(b)))
            act_norm(act, at, 256, 4)
            act_softmax(act, at, 256 ** -0.5, 8)
            act.drain().then_inc(met, 1)
            act.wait_ge(met, at.step("products with v"))
            copy(flat(x_hi), banks(0, 4))
            act.drain().then_inc(met, 1)
            act.wait_ge(met, at.step("attention output's high part"))
            act.drain().then_inc(met, 1)
            act.wait_ge(met, at.step("attention output"))
            act_project(act, at, 4)

        def act_ff(act, at, steps, convolved=False):
            def silu(f):
                if convolved:
                    act.wait_ge(conv_done, at.value("conv", 1))
                    src = gate_conv(f)
                else:
                    act.wait_ge(chunk_used, at.value("chunk", 1))
                    src = tiles(ps[:, 2 * (f % 2), :])
                if f > 1:
                    act.wait_ge(act_ready, at.value("act", -1))
                activate(silu_buf(f), src, ACT.Silu).then_inc(silu_done, 1)
                at.add("chunk", 3 if f else 2)
                for k in ("act", "silu", "conv") if convolved else ("act", "silu"):
                    at.add(k)

            def step(f):
                split_hi(act, at)
                if not convolved:
                    silu(f - 1)
                split_hi(act, at)
                if convolved:
                    silu(f - 1)
                split_hi(act, at)

            f = ff_steps(act, at, steps, {"chunk": 6, "fetch": 6, "half": 6, "act": 2, "silu": 2}, step, not convolved)
            silu(f)
            split_hi(act, at)
            at.add("chunk")
            act.drain().then_inc(met, 1)
            act.wait_ge(met, at.step("down products"))
            pass_loop(act, at)
            act.drain().then_inc(met, 1)
            act.wait_ge(met, at.step("residual"))
            pass_loop(act, at)

        def act_rwkv(act, at):
            act.drain().then_inc(met, 1)
            act.wait_ge(met, at.step("inputs shifted"))
            activate(zg[0:64, 0, :], zg[0:64, 0, :], ACT.Tanh)
            activate(zg[:, 1, :], zg[:, 1, :], ACT.Sigmoid)
            activate(zg[0:32, 2, :], zg[0:32, 2, :], ACT.Sigmoid)
            act.drain().then_inc(met, 1)
            act.wait_ge(met, at.step("lora inputs, squares of kk"))
            act.drain().then_inc(met, 1)
            act.wait_ge(met, at.step("lora products, sums for kk"))
            for t in range(RT):
                ts = slice(t * S, (t + 1) * S)
                activate(LW_[:, ts], banks(0, 2)[:, ts], ACT.Sigmoid, bias=sm("w0", t, t + 1))
                activate(A_[:, ts], banks(2, 2)[:, ts], ACT.Sigmoid, bias=sm("a0", t, t + 1))
            copy(G_, banks(4, 2))
            act.drain().then_inc(met, 1)
            act.wait_ge(met, at.step("sigmoids"))
            act_root(act, work, work, 1.0, 0.0)
            act.drain().then_inc(met, 1)
            act.wait_ge(met, at.step("cumulated decays, root for kk"))
            activate(LT_, CL_, ACT.Exp)
            activate(MT_, CL_, ACT.Exp, scale=-1.0)
            activate(NT_, NT_, ACT.Exp)
            act.drain().then_inc(met, 1)
            act.wait_ge(met, at.step("exponentials, kk"))
            act.drain().then_inc(met, 1)
            act.wait_ge(met, at.step("alpha, beta, kappa, rho"))
            act.drain().then_inc(met, 1)
            act.wait_ge(met, at.step("beta and kappa by alpha and rho"))
            act.drain().then_inc(met, 1)
            act.wait_ge(met, at.step("masked"))
            act.drain().then_inc(met, 1)
            act.wait_ge(met, at.step("alpha by beta, token-major forms"))
            copy(alpha_tok, pbank(2))
            copy(beta_tok, pbank(4), scale=-1.0)
            copy(kappa_tok, pbank(6))
            act.drain().then_inc(met, 1)
            act.wait_ge(met, at.step("inverse of blocks of two"))
            act.drain().then_inc(met, 1)
            act.wait_ge(met, at.step("v token-major"))
            copy(v_tok, pbank(0))

            def level():
                act.drain().then_inc(met, 1)
                act.wait_ge(met, at.step("blocks below the diagonal"))
                pass_loop(act, at)
                act.drain().then_inc(met, 1)
                act.wait_ge(met, at.step("blocks times the inverse"))
                pass_loop(act, at)
                copy(xbuf, pbank(2))
                act.drain().then_inc(met, 1)
                act.wait_ge(met, at.step("blocks times the inverse copied out"))
                pass_loop(act, at)
                act.drain().then_inc(met, 1)
                act.wait_ge(met, at.step("what the level adds"))
                pass_loop(act, at)

            counted_loop(act, at, len(LEVELS), {"meet": 4}, level)
            act.drain().then_inc(met, 1)
            act.wait_ge(met, at.step("inverse"))
            act.drain().then_inc(met, 1)
            act.wait_ge(met, at.step("M V and T alpha"))
            copy(xbuf, pbank(0))
            act.drain().then_inc(met, 1)
            act.wait_ge(met, at.step("M V and T alpha copied out"))
            act.drain().then_inc(met, 1)
            act.wait_ge(met, at.step("T M V"))
            copy(uv, pbank(4))
            act.drain().then_inc(met, 1)
            act.wait_ge(met, at.step("T M V copied out"))
            for c in range(S // C):
                act.drain().then_inc(met, 1)
                act.wait_ge(met, at.step("T alpha by the state"))
                act.drain().then_inc(met, 1)
                act.wait_ge(met, at.step("u"))
                act.drain().then_inc(met, 1)
                act.wait_ge(met, at.step("the chunk's output and change of state"))
                copy(o_t[:, :, c * C:(c + 1) * C], pbank(2)[:, 0:RT, :])
                act.drain().then_inc(met, 1)
                act.wait_ge(met, at.step("the chunk's output and state copied out"))
            act.drain().then_inc(met, 1)
            act.wait_ge(met, at.step("means, bonus"))
            act.drain().then_inc(met, 1)
            act.wait_ge(met, at.step("squares of the centred output"))
            act.drain().then_inc(met, 1)
            act.wait_ge(met, at.step("variances"))
            act_root(act, work, banks(4, 2), 1.0 / 64, cst("gn_eps"))
            act.drain().then_inc(met, 1)
            act.wait_ge(met, at.step("root of the variance"))
            act.drain().then_inc(met, 1)
            act.wait_ge(met, at.step("rwkv output"))

        def act_s5(act, at):
            activate(s5t(0), sm("log_dt"), ACT.Exp)
            act.drain().then_inc(met, 1)
            act.wait_ge(met, at.step("dt"))
            act.drain().then_inc(met, 1)
            act.wait_ge(met, at.step("angles"))
            activate(s5t(1), s5t(1), ACT.Exp)
            activate(s5t(2), s5t(2), ACT.Sin)
            activate(s5t(3), s5t(3), ACT.Sin)
            act.drain().then_inc(met, 1)
            act.wait_ge(met, at.step("sines"))
            for grp in range(4):
                act.drain().then_inc(met, 1)
                act.wait_ge(met, at.step("B u"))
                act.drain().then_inc(met, 1)
                act.wait_ge(met, at.step("states"))
            act.drain().then_inc(met, 1)
            act.wait_ge(met, at.step("C x"))
            act.drain().then_inc(met, 1)
            act.wait_ge(met, at.step("y"))
            activate(u_t, u_t, ACT.Gelu_apprx_tanh)
            act.drain().then_inc(met, 1)
            act.wait_ge(met, at.step("gelu"))
            at.add("chunk")
            at.add("fetch")
            act.drain().then_inc(met, 1)
            act.wait_ge(met, at.step("glu product"))
            for t in range(4):
                activate(s5b[0][:, t, :], banks(0, 2)[:, t * S:(t + 1) * S], ACT.Sigmoid, bias=sm("b_glu", t, t + 1))
            act.drain().then_inc(met, 1)
            act.wait_ge(met, at.step("glu gate"))
            act.drain().then_inc(met, 1)
            act.wait_ge(met, at.step("s5 output"))

        def act_diff(act, at):
            act_project(act, at, 8, lambda c, b: copy((aq if c < 4 else ak)[:, 2 * (c % 4):2 * (c % 4) + 2, :], tiles(b)),
                        2)
            act_project(act, at, 4, lambda c, b: copy(av[:, :, c * CH:(c + 1) * CH], tiles(b)))
            act_norm(act, at, 64, 8)
            act_norm(act, at, 64, 8)
            act.drain().then_inc(met, 1)
            act.wait_ge(met, at.step("sums for lambda"))
            activate(tiny[:, 2:4], ps[:, 4, 0:2], ACT.Exp)
            act.drain().then_inc(met, 1)
            act.wait_ge(met, at.step("exponentials for lambda"))
            for _ in range(4):
                act_softmax(act, at, 1.0, 4)
                act.drain().then_inc(met, 1)
                act.wait_ge(met, at.step("products with v"))
                act.drain().then_inc(met, 1)
                act.wait_ge(met, at.step("attention output"))
            act_norm(act, at, P, 8, into_x=True)
            act_project(act, at, 4, ahead=2)

        def act_second_mixer(act, at):
            act_project(act, at, 2, lambda c, b: copy(qk[:, 2 * c:2 * c + 2, :], tiles(b)), 2)

            def k_v(c, b):
                copy(qk[:, 4, :], b[:, 0:S])
                act.drain()
                return copy(v_tok2, tiles(b[:, S:2 * S], P))

            evac_raw(act, at, k_v)
            act_project(act, at, 1, lambda c, b: copy(su, tiles(b)))
            act_project(act, at, 1, lambda c, b: copy(sv_tok, tiles(b)))
            act_project(act, at, 3, lambda c, b: copy((cb, cc, cx)[c], tiles(b)))
            act_norm(act, at, 64, 5, lambda: act_root(act, tiny[:, 6:8], tiny[:, 6:8], 1.0 / 256, cst("eps")))
            act.drain().then_inc(met, 1)
            act.wait_ge(met, at.step("turned features, gating products"))
            pass_loop(act, at)
            act.drain().then_inc(met, 1)
            act.wait_ge(met, at.step("q and k, gating and convolution outputs"))
            pass_loop(act, at)
            for _ in range(2):
                act_softmax(act, at, 64 ** -0.5, 8)
                act.drain().then_inc(met, 1)
                act.wait_ge(met, at.step("products with v"))
                pass_loop(act, at)
                act.drain().then_inc(met, 1)
                act.wait_ge(met, at.step("attention output"))
                pass_loop(act, at)
            act_project(act, at, 4)

        def act_moe_gates(act, at):
            act.drain().then_inc(met, 1)
            act.wait_ge(met, at.step("logits"))
            act.drain().then_inc(met, 1)
            act.wait_ge(met, at.step("the two largest logits"))
            activate(tiny[:, 100:102], tiny[:, 100:102], ACT.Exp)
            act.drain().then_inc(met, 1)
            act.wait_ge(met, at.step("exponential of their difference"))
            act.drain().then_inc(met, 1)
            act.wait_ge(met, at.step("gates by token"))
            act.drain().then_inc(met, 1)
            act.wait_ge(met, at.step("gates on every partition"))
            copy(slot(8, 2), banks(0, 4))
            act.drain().then_inc(met, 1)
            act.wait_ge(met, at.step("gates copied out"))

        def scalar_program(act, at):
            act.wait_ge(loaded, 48)
            act_norm(act, at)
            act_project(act, at, 6, lambda c, b: copy(z12[:, 2 * c:2 * c + 2, :], tiles(b)), 2)

            def lora_in(c, b):
                copy(zg[:, 0:2, :], tiles(b))
                act.drain()
                return copy(zg[0:32, 2, :], ps[0:32, 1, 0:S])

            evac_raw(act, at, lora_in)
            act_project(act, at, 2, lambda c, b: copy(u_t[:, 2 * c:2 * c + 2, :], tiles(b)))
            act_rwkv(act, at)
            act_s5(act, at)
            act_project(act, at, 4)
            act_memory(act, at)
            act_norm(act, at)
            act_ff(act, at, FF_STEPS)
            act_norm(act, at)
            act_diff(act, at)
            act_memory(act, at)
            act_norm(act, at)
            act_moe_gates(act, at)
            act_ff(act, at, MOE_STEPS)
            with act.Fori(0, 2) as layer:
                at.enter(layer, PER_LAYER_SILU)
                act.drain().then_inc(met, 1)
                act.wait_ge(met, at.step("the layer's small inputs"))
                pass_loop(act, at)
                act_norm(act, at)
                act_second_mixer(act, at)
                act_norm(act, at)
                act_ff(act, at, FF_STEPS, True)
                at.leave(2)

        def tt(dve, o, a, b, op):
            nc.vector.tensor_tensor(o, a, b, op)
            dve.drain()

        def ts(dve, o, a, s1, s2=None, op0=ALU.mult, op1=None):
            nc.vector.tensor_scalar(o, a, s1, s2, op0, *([op1] if op1 is not None else []))
            dve.drain()

        def stt(dve, o, a, s, b, op0, op1):
            nc.vector.scalar_tensor_tensor(o, a, s, b, op0, op1)
            dve.drain()

        MUL, ADD, SUB = ALU.mult, ALU.add, ALU.subtract

        def split_x(dve):
            nc.vector.tensor_copy(x_hi[:, :, :], mix[:, :, :])
            dve.drain()
            nc.vector.tensor_tensor(x_lo[:, :, :], mix[:, :, :], x_hi[:, :, :], SUB)

        def dve_norm(dve, at, src, dst, gain, groups=1, per=KT, sq=mix, before=None, after=None):
            x = dst is None
            dst = mix if x else dst
            n = groups * per
            nc.vector.tensor_tensor(sq[:, 0:n, :], src[:, 0:n, :], src[:, 0:n, :], MUL)
            if before:
                before()
            dve.drain().then_inc(met, 1)
            dve.wait_ge(met, at.step("squares"))
            pass_loop(dve, at)
            if x:
                split_lo(dve, at)
            dve.drain().then_inc(met, 1)
            dve.wait_ge(met, at.step("sums of squares"))
            pass_loop(dve, at)
            if x:
                split_lo(dve, at)
            dve.drain().then_inc(met, 1)
            dve.wait_ge(met, at.step("roots"))
            pass_loop(dve, at)
            for t in range(n):
                g = t // per
                nc.vector.scalar_tensor_tensor(dst[:, t, :], src[:, t, :], gain(t), rstd[:, g * S:(g + 1) * S],
                                               MUL, MUL)
            if x:
                dve.drain()
                split_x(dve)
            if after:
                after()
            dve.drain().then_inc(met, 1)
            dve.wait_ge(met, at.step("normed"))
            pass_loop(dve, at)

        def dve_residual(dve, at, n=4, ahead=0):
            dve_project(dve, at, n, ahead=ahead, copy_out=lambda c, b: nc.vector.tensor_tensor(h[:, 2 * c:2 * c + 2, :], tiles(b),
                                                                  h[:, 2 * c:2 * c + 2, :], ADD))

        def dve_softmax(dve, at, biased=None, lam=None):
            dve.drain().then_inc(met, 1)
            dve.wait_ge(met, at.step("scores"))
            pass_loop(dve, at)
            if biased:
                biased()
            scores = ae if biased else tiles(banks(0, 4))
            top, total = tiny[:, 16:24], tiny[:, 24:32]
            nc.vector.reduce_max(top, scores, AX)
            dve.drain()
            tt(dve, ae, scores, scalars(top, [P, 8, S]), SUB)
            dve.drain().then_inc(met, 1)
            dve.wait_ge(met, at.step("scores less their maxima"))
            pass_loop(dve, at)
            dve.drain().then_inc(met, 1)
            dve.wait_ge(met, at.step("exponentials"))
            pass_loop(dve, at)
            nc.vector.reduce_sum(total, ae, AX)
            dve.drain()
            nc.vector.reciprocal(total, total)
            dve.drain()
            if lam is not None:
                second = total.rearrange("p (a c b) -> p a c b", c=2, b=2)[:, :, 1, :]
                ts(dve, second, second, lam)
            tt(dve, ae, ae, scalars(total, [P, 8, S]), MUL)
            if lam is not None:
                e4 = slot(10, 2).rearrange("p (a c n) -> p a c n", a=2, c=2)
                tt(dve, e4[:, :, 0, :], e4[:, :, 0, :], e4[:, :, 1, :], ADD)
            dve.drain().then_inc(met, 1)
            dve.wait_ge(met, at.step("probabilities"))
            pass_loop(dve, at)
            dve.drain().then_inc(met, 1)
            dve.wait_ge(met, at.step("transposes"))
            pass_loop(dve, at)
            dve.drain().then_inc(met, 1)
            dve.wait_ge(met, at.step("transposes copied out"))
            pass_loop(dve, at)

        def dve_memory(dve, at, l):
            dve_norm(dve, at, h, None, lambda t: sm("g_xattn", KT * l + t, KT * l + t + 1))
            dve_project(dve, at, 4, ahead=2)
            dve_norm(dve, at, aq, aq, lambda t: sm("g_xq", 2 * l + t % 2, 2 * l + t % 2 + 1), 4, 2)
            dve.wait_ge(mem_loaded, 16 * (l + 1))
            dve_norm(dve, at, mem_sb, None, lambda t: sm("g_mem", KT * l + t, KT * l + t + 1))
            dve_project(dve, at, 4, ahead=2)
            dve_project(dve, at, 4)
            dve_norm(dve, at, ak, ak, lambda t: sm("g_xk", 2 * l + t % 2, 2 * l + t % 2 + 1), 4, 2)
            dve_softmax(dve, at)
            dve.drain().then_inc(met, 1)
            dve.wait_ge(met, at.step("products with v"))
            dve.drain().then_inc(met, 1)
            dve.wait_ge(met, at.step("attention output's high part"))
            nc.vector.tensor_tensor(flat(x_lo), banks(0, 4), flat(x_hi), SUB)
            dve.drain().then_inc(met, 1)
            dve.wait_ge(met, at.step("attention output"))
            dve_residual(dve, at)

        def dve_conv(dve, o, x, taps):
            for i in range(2):
                nc.vector.tensor_scalar(o[:, i, :], x[:, i, :], taps(1, i), None, MUL)
            dve.drain()
            for i in range(2):
                nc.vector.scalar_tensor_tensor(o[:, i, 1:S], x[:, i, 0:S - 1], taps(0, i), o[:, i, 1:S], MUL, ADD)
            dve.drain()
            for i in range(2):
                nc.vector.scalar_tensor_tensor(o[:, i, 0:S - 1], x[:, i, 1:S], taps(2, i), o[:, i, 0:S - 1], MUL, ADD)
            dve.drain()

        def dve_step(dve, at, f, gate=None, taps=None):
            split_lo(dve, at)
            if taps:
                dve_act(dve, at, f - 1, gate, taps, lambda: split_lo(dve, at))
            else:
                dve_act(dve, at, f - 1, gate)
                split_lo(dve, at)
            split_lo(dve, at)

        def dve_act(dve, at, f, gate=None, taps=None, between=None):
            up = tiles(ps[:, 2 * (f % 2) + 1, :])
            if taps:
                dve.wait_ge(chunk_used, at.value("chunk", 1))
                dve_conv(dve, gate_conv(f), tiles(ps[:, 2 * (f % 2), :]), lambda tap, i: taps(tap, 2 * f + i))
                dve.drain().then_inc(conv_done, 1)
                if between:
                    between()
            dve.wait_ge(chunk_used, at.value("chunk", 2))
            if taps:
                dve_conv(dve, up_conv(f), up, lambda tap, i: taps(tap, 22 + 2 * f + i))
                up = up_conv(f)
            dve.wait_ge(silu_done, at.value("silu", 1))
            tt(dve, act_buf(f), silu_buf(f), up, MUL)
            if gate is not None:
                tt(dve, act_buf(f), act_buf(f), gate, MUL)
            nc.vector.tensor_copy(act_hi[:, f % 2, :, :], act_buf(f))
            dve.drain()
            nc.vector.tensor_tensor(act_lo[:, f % 2, :, :], act_buf(f), act_hi[:, f % 2, :, :],
                                    SUB).then_inc(act_ready, 1)
            at.add("chunk", 3 if f else 2)
            for k in ("act", "silu", "conv") if taps else ("act", "silu"):
                at.add(k)

        def dve_ff_end(dve, at, f, gate=None, taps=None):
            dve_act(dve, at, f, gate, taps)
            split_lo(dve, at)
            at.add("chunk")
            dve.drain().then_inc(met, 1)
            dve.wait_ge(met, at.step("down products"))
            pass_loop(dve, at)
            nc.vector.tensor_tensor(flat(h), banks(4, 4), flat(h), ADD)
            dve.drain().then_inc(met, 1)
            dve.wait_ge(met, at.step("residual"))
            pass_loop(dve, at)

        def dve_rwkv(dve, at):
            for z, rows, mu in ((z12, slice(0, P), sm("mu", 0, 12)), (zg[:, 0:2, :], slice(0, P), sm("mu", 12, 14)),
                                (zg[:, 2:3, :], slice(0, 32), sm("mu", 14, 15))):
                n = z.shape[1]
                z, d = z[rows, :, :], shift_tmp[rows, 0:n, :]
                nc.vector.tensor_tensor(d[:, :, 1:S], z[:, :, 0:S - 1], z[:, :, 1:S], SUB)
                ts(dve, d[:, :, 0:1], z[:, :, 0:1], -1.0)
                tt(dve, d, d, scalars(mu[rows, :], [rows.stop, n, S]), MUL)
                tt(dve, z, z, d, ADD)
            dve.drain().then_inc(met, 1)
            dve.wait_ge(met, at.step("inputs shifted"))

            def scale_tiles(o, i, name):
                tt(dve, tiles(o), tiles(i), scalars(sm(name), [P, RT, S]), MUL)

            scale_tiles(KK_, K_, "k_k")
            tt(dve, work, KK_, KK_, MUL)
            dve.drain().then_inc(met, 1)
            dve.wait_ge(met, at.step("lora inputs, squares of kk"))
            dve.drain().then_inc(met, 1)
            dve.wait_ge(met, at.step("lora products, sums for kk"))
            ts(dve, work, banks(6, 2), 1e-24, None, ALU.max)
            dve.drain().then_inc(met, 1)
            dve.wait_ge(met, at.step("sigmoids"))
            ts(dve, LW_, LW_, -math.exp(-0.5))
            for t in range(RT):
                cs = slice(t * S, (t + 1) * S)
                nc.vector.tensor_tensor_scan(CL_[:, cs], cst("reset"), LW_[:, cs], 0.0, MUL, ADD)
            dve.drain()
            tt(dve, NT_, CL_, LW_, SUB)
            ts(dve, tiny[:, 32:36], sm("k_a"), -1.0, 1.0, MUL, ADD)
            scale_tiles(T_, A_, "k_a")
            tt(dve, tiles(T_), tiles(T_), scalars(tiny[:, 32:36], [P, RT, S]), ADD)
            tt(dve, K_, K_, T_, MUL)
            dve.drain().then_inc(met, 1)
            dve.wait_ge(met, at.step("cumulated decays, root for kk"))
            tt(dve, KK_, KK_, work, MUL)
            tt(dve, A_, A_, KK_, MUL)
            dve.drain().then_inc(met, 1)
            dve.wait_ge(met, at.step("exponentials, kk"))
            tt(dve, ar[:, :, 0:C], by64(KK_), by64(NT_), MUL)
            tt(dve, ar[:, :, C:2 * C], by64(R_), by64(LT_), MUL)
            tt(dve, BE_, A_, MT_, MUL)
            tt(dve, KA_, K_, MT_, MUL)
            nc.vector.tensor_copy(chunk_decay, by64(LT_)[:, :, C - 1])
            scale_tiles(R_, R_, "r_k")
            tt(dve, R_, R_, K_, MUL)
            dve.drain().then_inc(met, 1)
            dve.wait_ge(met, at.step("alpha, beta, kappa, rho"))
            dve.drain().then_inc(met, 1)
            dve.wait_ge(met, at.step("beta and kappa by alpha and rho"))
            full = [P, NJ, C]
            by_b, by_k = tiles(banks(0, 4), 2 * C), tiles(banks(4, 4), 2 * C)
            ts(dve, neg_lt, by_b[:, :, 0:C], -1.0)
            stt(dve, neg_nt, by_b[:, :, C:2 * C], -1.0, repeated(cst("upto"), full), MUL, MUL)
            tt(dve, m_t, by_k[:, :, 0:C], repeated(cst("before"), full), MUL)
            tt(dve, w_t, by_k[:, :, C:2 * C], repeated(cst("upto"), full), MUL)
            dve.drain().then_inc(met, 1)
            dve.wait_ge(met, at.step("masked"))
            dve.drain().then_inc(met, 1)
            dve.wait_ge(met, at.step("alpha by beta, token-major forms"))
            stt(dve, tri, pbank(0), -1.0, repeated(cst("level1_low"), full), MUL, MUL)
            tt(dve, tri, tri, repeated(cst("eye64"), full), ADD)
            tt(dve, tri_t, neg_lt, repeated(cst("level1"), full), MUL)
            tt(dve, tri_t, tri_t, repeated(cst("eye64"), full), ADD)
            dve.drain().then_inc(met, 1)
            dve.wait_ge(met, at.step("inverse of blocks of two"))
            dve.drain().then_inc(met, 1)
            dve.wait_ge(met, at.step("v token-major"))
            levels_at = CONST_AT["levels"][0]
            with dve.Fori(0, len(LEVELS)) as i:
                at.enter(i, {"meet": 4})
                mask = const_sb[:, bass.ds(i * C + levels_at, C)]
                tt(dve, ubuf, neg_lt, repeated(mask, full), MUL)
                dve.drain().then_inc(met, 1)
                dve.wait_ge(met, at.step("blocks below the diagonal"))
                pass_loop(dve, at)
                dve.drain().then_inc(met, 1)
                dve.wait_ge(met, at.step("blocks times the inverse"))
                pass_loop(dve, at)
                dve.drain().then_inc(met, 1)
                dve.wait_ge(met, at.step("blocks times the inverse copied out"))
                pass_loop(dve, at)
                dve.drain().then_inc(met, 1)
                dve.wait_ge(met, at.step("what the level adds"))
                pass_loop(dve, at)
                tt(dve, tri, tri, pbank(4), ADD)
                tt(dve, tri_t, tri_t, pbank(6), ADD)
                at.leave(len(LEVELS))
            dve.drain().then_inc(met, 1)
            dve.wait_ge(met, at.step("inverse"))
            dve.drain().then_inc(met, 1)
            dve.wait_ge(met, at.step("M V and T alpha"))
            nc.vector.tensor_copy(tat, pbank(2))
            nc.vector.memset(rstd[:, 1024:1024 + RT * C], 0.0)
            dve.drain().then_inc(met, 1)
            dve.wait_ge(met, at.step("M V and T alpha copied out"))
            dve.drain().then_inc(met, 1)
            dve.wait_ge(met, at.step("T M V"))
            dve.drain().then_inc(met, 1)
            dve.wait_ge(met, at.step("T M V copied out"))
            by_chunk = LW_.rearrange("p (t c n) -> p t c n", t=RT, n=C)
            decay = chunk_decay.rearrange("p (t c) -> p t c", t=RT)
            for c in range(S // C):
                dve.drain().then_inc(met, 1)
                dve.wait_ge(met, at.step("T alpha by the state"))
                tt(dve, ubuf[:, 0:RT, :], pbank(0)[:, 0:RT, :], by_chunk[:, :, c, :], ADD)
                dve.drain().then_inc(met, 1)
                dve.wait_ge(met, at.step("u"))
                dve.drain().then_inc(met, 1)
                dve.wait_ge(met, at.step("the chunk's output and change of state"))
                tt(dve, state, state, pbank(4)[:, 0:RT, :], ADD)
                tt(dve, state, state, scalars(decay[:, :, c], [P, RT, C]), MUL)
                dve.drain().then_inc(met, 1)
                dve.wait_ge(met, at.step("the chunk's output and state copied out"))
            dve.drain().then_inc(met, 1)
            dve.wait_ge(met, at.step("means, bonus"))
            stt(dve, o_t, tiles(banks(0, 2)), -1.0 / 64, o_t, MUL, ADD)
            tt(dve, tiles(T_), o_t, o_t, MUL)
            tt(dve, V_, V_, banks(2, 2), MUL)
            dve.drain().then_inc(met, 1)
            dve.wait_ge(met, at.step("squares of the centred output"))
            dve.drain().then_inc(met, 1)
            dve.wait_ge(met, at.step("variances"))
            dve.drain().then_inc(met, 1)
            dve.wait_ge(met, at.step("root of the variance"))
            for t in range(RT):
                cs = slice(t * S, (t + 1) * S)
                stt(dve, o_t[:, t, :], o_t[:, t, :], sm("ln_w", t, t + 1), work[:, cs], MUL, MUL)
                stt(dve, o_t[:, t, :], o_t[:, t, :], sm("ln_b", t, t + 1), V_[:, cs], ADD, ADD)
            tt(dve, o_t, o_t, tiles(G_), MUL)
            dve.drain().then_inc(met, 1)
            dve.wait_ge(met, at.step("rwkv output"))

        def dve_s5(dve, at):
            lre, lim = sm("lam_re"), sm("lam_im")
            dve.drain().then_inc(met, 1)
            dve.wait_ge(met, at.step("dt"))
            tt(dve, s5t(1), lre, s5t(0), MUL)
            tt(dve, s5t(2), lim, s5t(0), MUL)
            ts(dve, s5t(3), s5t(2), 1.0 / (2 * math.pi), 12582912.0, MUL, ADD)
            ts(dve, s5t(3), s5t(3), -12582912.0, None, ADD)
            stt(dve, s5t(2), s5t(3), -6.28125, s5t(2), MUL, ADD)
            stt(dve, s5t(2), s5t(3), -(2 * math.pi - 6.28125), s5t(2), MUL, ADD)
            ts(dve, s5t(2), s5t(2), 3.1415925, -3.1415925, ALU.min, ALU.max)
            ts(dve, s5t(3), s5t(2), -1.0, None, MUL)
            tt(dve, s5t(3), s5t(3), s5t(2), ALU.max)
            ts(dve, s5t(3), s5t(3), -1.0, math.pi / 2, MUL, ADD)
            dve.drain().then_inc(met, 1)
            dve.wait_ge(met, at.step("angles"))
            dve.drain().then_inc(met, 1)
            dve.wait_ge(met, at.step("sines"))
            mag, sn, cs_ = s5t(1), s5t(2), s5t(3)
            br, bi, den, t1, cr, ci = (s5t(i) for i in range(4, 10))
            tt(dve, br, mag, cs_, MUL)
            tt(dve, bi, mag, sn, MUL)
            ts(dve, br, br, -1.0, None, ADD)
            tt(dve, den, lre, lre, MUL)
            tt(dve, t1, lim, lim, MUL)
            tt(dve, den, den, t1, ADD)
            nc.vector.reciprocal(den, den)
            dve.drain()

            def products(o, a, b, c, d, op, t):
                nc.vector.tensor_tensor(o, a, b, MUL)
                tt(dve, t, c, d, MUL)
                tt(dve, o, o, t, op)

            products(cr, br, lre, bi, lim, ADD, t1)
            products(ci, bi, lre, br, lim, SUB, t1)
            tt(dve, cr, cr, den, MUL)
            tt(dve, ci, ci, den, MUL)
            cshape = [P, SP_, 32]
            w1 = tiles(slot(17)[:, 0:512], 32)
            products(c_re, tiles(sm("c_re"), 32), scalars(cr, cshape), tiles(sm("c_im"), 32), scalars(ci, cshape), SUB, w1)
            products(c_im, tiles(sm("c_re"), 32), scalars(ci, cshape), tiles(sm("c_im"), 32), scalars(cr, cshape), ADD, w1)
            ts(dve, c_im, c_im, -1.0)
            nc.vector.memset(e_re[:, :, 0:1], 1.0)
            nc.vector.memset(e_im[:, :, 0:1], 0.0)
            pr, pi, p2 = s5t(10), s5t(11), s5t(12)
            nc.vector.tensor_copy(pr, cs_)
            nc.vector.tensor_copy(pi, sn)
            dve.drain()
            m = 1
            while m < S:
                shape = [P, SP_, m]
                lo, hi = slice(0, m), slice(m, 2 * m)
                t = slot(8, 2).rearrange("p (j n) -> p j n", n=128)[:, :, 0:m]
                products(e_re[:, :, hi], e_re[:, :, lo], scalars(pr, shape), e_im[:, :, lo], scalars(pi, shape), SUB, t)
                products(e_im[:, :, hi], e_re[:, :, lo], scalars(pi, shape), e_im[:, :, lo], scalars(pr, shape), ADD, t)
                products(p2, pr, pr, pi, pi, SUB, t1)
                stt(dve, pi, pi, 2.0, pr, MUL, MUL)
                nc.vector.tensor_copy(pr, p2)
                dve.drain()
                m *= 2
            for grp in range(4):
                er, ei = e_re[:, 4 * grp:4 * grp + 4, :], e_im[:, 4 * grp:4 * grp + 4, :]
                vr, vi = ps[:, 0:4, 0:S], ps[:, 0:4, S:2 * S]
                xr, xi, zr, zi, yr, yi, t = s5b[:7]
                dve.drain().then_inc(met, 1)
                dve.wait_ge(met, at.step("B u"))
                products(zr, er, vr, ei, vi, ADD, t)
                products(zi, er, vi, ei, vr, SUB, t)
                for q in range(4):
                    a = mag[:, 4 * grp + q:4 * grp + q + 1].to_broadcast([P, S])
                    nc.vector.tensor_tensor_scan(yr[:, q, :], a, zr[:, q, :], 0.0, MUL, ADD)
                    nc.vector.tensor_tensor_scan(yi[:, q, :], a, zi[:, q, :], 0.0, MUL, ADD)
                dve.drain()
                products(xr, er, yr, ei, yi, SUB, t)
                products(xi, er, yi, ei, yr, ADD, t)
                dve.drain().then_inc(met, 1)
                dve.wait_ge(met, at.step("states"))
            dve.drain().then_inc(met, 1)
            dve.wait_ge(met, at.step("C x"))
            for t in range(4):
                stt(dve, u_t[:, t, :], u_t[:, t, :], sm("s5_d", t, t + 1), ps[:, 4 + t, 0:S], MUL, ADD)
            dve.drain().then_inc(met, 1)
            dve.wait_ge(met, at.step("y"))
            dve.drain().then_inc(met, 1)
            dve.wait_ge(met, at.step("gelu"))
            at.add("chunk")
            at.add("fetch")
            dve.drain().then_inc(met, 1)
            dve.wait_ge(met, at.step("glu product"))
            dve.drain().then_inc(met, 1)
            dve.wait_ge(met, at.step("glu gate"))
            tt(dve, u_t, u_t, s5b[0], MUL)
            split_x(dve)
            dve.drain().then_inc(met, 1)
            dve.wait_ge(met, at.step("s5 output"))

        def dve_diff(dve, at):
            dve_project(dve, at, 8, ahead=2)
            dve_project(dve, at, 4)
            dve_norm(dve, at, aq, aq, lambda t: sm("g_dq"), 8, 1)
            dve_norm(dve, at, ak, ak, lambda t: sm("g_dk"), 8, 1,
                     after=lambda: nc.vector.tensor_tensor(tiny[:, 0:2], sm("lam", 0, 2), sm("lam", 2, 4), MUL))
            dve.drain().then_inc(met, 1)
            dve.wait_ge(met, at.step("sums for lambda"))
            dve.drain().then_inc(met, 1)
            dve.wait_ge(met, at.step("exponentials for lambda"))
            neg_lam = tiny[:, 4:5]
            tt(dve, neg_lam, tiny[:, 3:4], tiny[:, 2:3], SUB)
            ts(dve, neg_lam, neg_lam, -LAMBDA_INIT, None, ADD)
            ts(dve, tiny[:, 5:6], sm("g_sub"), 1.0 - LAMBDA_INIT)
            for qb in range(2):
                for hd in range(8):
                    nc.vector.scalar_tensor_tensor(bias[:, hd, :], cst("dist", qb * S, (qb + 1) * S), -2.0 ** -(hd + 1),
                                                   cst("hidden", qb * S, (qb + 1) * S), MUL, ADD)
                dve.drain()
                for half in range(2):
                    def biased():
                        for hl in range(4):
                            for c in range(2):
                                u = 4 * (hl // 2) + 2 * c + hl % 2
                                nc.vector.scalar_tensor_tensor(ae[:, u, :], tiles(banks(0, 4))[:, u, :], 64 ** -0.5,
                                                               bias[:, 4 * half + hl, :], MUL, ADD)
                        dve.drain()

                    dve_softmax(dve, at, biased, neg_lam)
                    dve.drain().then_inc(met, 1)
                    dve.wait_ge(met, at.step("products with v"))
                    nc.vector.tensor_copy(mix[:, 4 * half:4 * half + 4, qb * P:(qb + 1) * P], tiles(banks(0), P))
                    dve.drain().then_inc(met, 1)
                    dve.wait_ge(met, at.step("attention output"))
            dve_norm(dve, at, mix, None, lambda t: tiny[:, 5:6], 8, 1, sq=ae)
            dve_residual(dve, at, ahead=2)

        def dve_second_mixer(dve, at):
            dve_project(dve, at, 2, ahead=2)
            leave_raw(dve, at)
            for n in (1, 1, 3):
                dve_project(dve, at, n)

            def gating_squares():
                tt(dve, sv_sq, sv_tok, sv_tok, MUL)
                nc.vector.reduce_sum(tiny[:, 6:8], sv_sq, AX)

            def gating_normed():
                tt(dve, sv_tok, sv_tok, scalars(tiny[:, 6:8], [P, 2, 256]), MUL)

            dve_norm(dve, at, qk, qk, lambda t: lay("gq") if t < 4 else lay("gk"), 5, 1,
                     before=gating_squares, after=gating_normed)
            dve.drain().then_inc(met, 1)
            dve.wait_ge(met, at.step("turned features, gating products"))
            pass_loop(dve, at)
            four = [P, 4, S]
            two = [P, 2, S]
            tt(dve, rot[:, 0:4, :], tiles(banks(4, 2)), repeated(cst("sin"), four), MUL)
            tt(dve, rot[:, 4:6, :], tiles(banks(7)), repeated(cst("sin"), two), MUL)
            tt(dve, q_r[:, 0:4, :], qk[:, 0:4, :], repeated(cst("cos"), four), MUL)
            tt(dve, q_r[:, 4:6, :], tiles(banks(6)), repeated(cst("cos"), two), MUL)
            tt(dve, q_r[:, 0:6, :], q_r[:, 0:6, :], rot[:, 0:6, :], ADD)
            for t in range(2):
                o = mix[:, 4 + t, :]
                stt(dve, tiles(o, P), tiles(ps[:, t, 0:S], P), lay("gsg", t, t + 1),
                    repeated(lay("sgb", t * P, (t + 1) * P), [P, 2, P]), MUL, ADD)
            tt(dve, mix[:, 4:6, :], mix[:, 4:6, :], su, MUL)
            tt(dve, cc, cc, cx, MUL)
            dve_conv(dve, c_out, cc, lambda tap, i: lay("cw", 2 * tap + i, 2 * tap + i + 1))
            tt(dve, mix[:, 6:8, :], c_out, cb, MUL)
            dve.drain().then_inc(met, 1)
            dve.wait_ge(met, at.step("q and k, gating and convolution outputs"))
            pass_loop(dve, at)
            for qb in range(2):
                dve_softmax(dve, at)
                dve.drain().then_inc(met, 1)
                dve.wait_ge(met, at.step("products with v"))
                pass_loop(dve, at)
                nc.vector.tensor_copy(mix[:, 0:4, qb * P:(qb + 1) * P], tiles(banks(0), P))
                if qb:
                    dve.drain()
                    split_x(dve)
                dve.drain().then_inc(met, 1)
                dve.wait_ge(met, at.step("attention output"))
                pass_loop(dve, at)
            dve_residual(dve, at)

        def dve_moe_gates(dve, at):
            shape = [P, 2, NE]

            def area(i):
                return tiles(tiny[:, 128 + 16 * i:144 + 16 * i], NE)

            logit, chosen, first, second = area(0), area(1), area(2), area(3)
            top, mark = tiny[:, 96:98], tiny[:, 98:100]
            diff, p1, p2 = tiny[:, 100:102], tiny[:, 102:104], tiny[:, 104:106]

            def take_largest(o, largest):
                nc.vector.reduce_max(largest, logit, AX)
                dve.drain()
                tt(dve, chosen, logit, scalars(largest, shape), ALU.is_ge)
                tt(dve, chosen, chosen, repeated(cst("rev"), shape), MUL)
                nc.vector.reduce_max(mark, chosen, AX)
                dve.drain()
                tt(dve, o, chosen, scalars(mark, shape), ALU.is_ge)

            dve.drain().then_inc(met, 1)
            dve.wait_ge(met, at.step("logits"))
            tt(dve, logit, tiles(ps[:, 0, 0:2 * NE], NE), repeated(sm("b_router"), shape), ADD)
            take_largest(first, top)
            stt(dve, logit, first, -BIG, logit, MUL, ADD)
            take_largest(second, diff)
            tt(dve, diff, diff, top, SUB)
            dve.drain().then_inc(met, 1)
            dve.wait_ge(met, at.step("the two largest logits"))
            dve.drain().then_inc(met, 1)
            dve.wait_ge(met, at.step("exponential of their difference"))
            ts(dve, p1, diff, 1.0, None, ADD)
            nc.vector.reciprocal(p1, p1)
            dve.drain()
            tt(dve, p2, p1, diff, MUL)
            tt(dve, first, first, scalars(p1, shape), MUL)
            tt(dve, second, second, scalars(p2, shape), MUL)
            tt(dve, first, first, second, ADD)
            flat16 = tiny[:, 160:176]
            nc.vector.tensor_copy(slot(6, 2).rearrange("p (b n) -> p b n", n=P), scalars(flat16, [P, 16, P]))
            dve.drain().then_inc(met, 1)
            dve.wait_ge(met, at.step("gates by token"))
            dve.drain().then_inc(met, 1)
            dve.wait_ge(met, at.step("gates on every partition"))
            dve.drain().then_inc(met, 1)
            dve.wait_ge(met, at.step("gates copied out"))

        def vector_program(dve, at):
            dve.wait_ge(loaded, 48)
            dve_norm(dve, at, h, None, lambda t: sm("g_mix", t, t + 1))
            dve_project(dve, at, 6, ahead=2)
            leave_raw(dve, at)
            dve_project(dve, at, 2)
            dve_rwkv(dve, at)
            dve_s5(dve, at)
            dve_residual(dve, at)
            dve_memory(dve, at, 0)
            dve_norm(dve, at, h, None, lambda t: sm("g_ffn", t, t + 1))
            f = ff_steps(dve, at, FF_STEPS, {"chunk": 6, "fetch": 6, "half": 6, "act": 2, "silu": 2},
                         lambda f: dve_step(dve, at, f))
            dve_ff_end(dve, at, f)
            dve_norm(dve, at, h, None, lambda t: sm("g_mix", KT + t, KT + t + 1))
            dve_diff(dve, at)
            dve_memory(dve, at, 1)
            dve_norm(dve, at, h, None, lambda t: sm("g_ffn", KT + t, KT + t + 1))
            dve_moe_gates(dve, at)

            def gates(e):
                return gate_bc[:, bass.ds(e, 1), :].to_broadcast([P, 2, S])

            def expert_pair(e, j):
                dve_step(dve, at, 3, gates(e))
                dve_step(dve, at, 4, gates(e))

            dve_step(dve, at, 1, gates(0))
            dve_step(dve, at, 2, gates(0))
            expert_loops(dve, at, {"chunk": 6, "fetch": 6, "half": 6, "act": 2, "silu": 2}, expert_pair,
                         EXPERT_PAIRS - 1)
            dve_step(dve, at, 5, gates(NE - 1))
            dve_ff_end(dve, at, 5, gates(NE - 1))
            with dve.Fori(0, 2) as layer:
                at.enter(layer, PER_LAYER_SILU)
                nc.vector.tensor_copy(layer_sb[:, :], small_sb[:, bass.ds(layer * LAYER_W + LAYERS_AT, LAYER_W)])
                dve.drain().then_inc(met, 1)
                dve.wait_ge(met, at.step("the layer's small inputs"))
                pass_loop(dve, at)
                dve_norm(dve, at, h, None, lambda t: lay("g1", t, t + 1))
                dve_second_mixer(dve, at)
                dve_norm(dve, at, h, None, lambda t: lay("g2", t, t + 1))
                def taps(tap, i):
                    return lay("fcw", 44 * tap + i, 44 * tap + i + 1)

                for f in range(1, FF_STEPS):
                    dve_step(dve, at, f, taps=taps)
                dve_ff_end(dve, at, FF_STEPS - 1, taps=taps)
                at.leave(2)
            dve.drain().then_inc(result_ready, 1)

        block = ctx.enter_context(nc.Block())
        places = [Place(), Place(), Place()]

        @block.sync
        def _(sp):
            sync_program(sp)

        @block.tensor
        def _(pe):
            tensor_program(pe, places[0])

        @block.scalar
        def _(act):
            scalar_program(act, places[1])

        @block.vector
        def _(dve):
            vector_program(dve, places[2])

        for other in places[1:]:
            for n, (a, b) in enumerate(zip(places[0].labels, other.labels)):
                assert a == b, (n, a, b)
            assert len(places[0].labels) == len(other.labels)


WEIGHTS = ["hy_w_in", "s5_w_glu", "hy_w_out", "xa_w_q", "xa_w_kv", "xa_w_o", "ff_w_gate", "ff_w_up",
           "ff_w_down", "da_w_qkv", "da_w_o", "moe_w_gate", "moe_w_up", "moe_w_down", "w_in_2",
           "w_out_2", "ffn_w_up_2", "ffn_w_down_2"]


def launch_arrays(inputs):
    i = {k: np.asarray(v) for k, v in inputs.items()}
    packed = small_inputs(i)
    names = list(WIDTHS) + [f"{n}_{l}" for l in range(2) for n in LAYER_WIDTHS]
    widths = {**WIDTHS, **{f"{n}_{l}": w for l in range(2) for n, w in LAYER_WIDTHS.items()}}
    for n in names:
        assert packed[n].shape == (P, widths[n]), (n, packed[n].shape)
    arrays = {
        "small": np.ascontiguousarray(np.concatenate([packed[n] for n in names], 1)),
        "const": np.concatenate([np.asarray(v, np.float32) for v in shape_constants().values()], 1),
        "x_t": np.ascontiguousarray(i["x"][0].T),
        "mem_t": np.ascontiguousarray(i["mem"][0].T),
    }
    for n in WEIGHTS:
        arrays[n] = np.ascontiguousarray(i[n])
    return arrays


def kernel(**inputs):
    import concourse.bacc as bacc
    from concourse.bass_utils import run_bass_kernel_spmd

    arrays = launch_arrays(inputs)
    nc = bacc.Bacc("TRN2", target_bir_lowering=False, num_devices=1, dynamic_dma_scratch_size=1024)
    aps = {n: nc.dram_tensor(n, a.shape, F32, kind="ExternalInput").ap() for n, a in arrays.items()}
    out_t = nc.dram_tensor("out_t", (D, S), F32, kind="ExternalOutput").ap()
    build(nc, aps["small"], aps["const"], aps["x_t"], aps["mem_t"], {n: aps[n] for n in WEIGHTS}, out_t)
    result = run_bass_kernel_spmd(nc, [arrays], core_ids=[0])
    return np.ascontiguousarray(result.results[0]["out_t"].T)[None]
```
